# Optimizing a Trainium2 kernel written in Bass

```python
import math
import jax, jax.numpy as jnp
from jax import lax
import numpy as np
import jax
import jax.numpy as jnp

D_MODEL = 1024
BATCH = 1
SEQ = 256
DEPTH = 2

HEAD_DIM = 64
GROUP_W = D_MODEL // 4
MIX_W = 4 * GROUP_W
DIFF_HEADS = GROUP_W // HEAD_DIM
DIFF_QK_DIM = HEAD_DIM // 2
CONV_W = GROUP_W
CONV_KERNEL = 31
GMLP_HEADS = GROUP_W // HEAD_DIM
GMLP_W = GROUP_W
CHUNK = 128
FOX_HEADS = GROUP_W // HEAD_DIM
FOX_W = GROUP_W
D_FF = ((8 * D_MODEL // 3 + 127) // 128) * 128
Q_BLOCK = 128
N_MOD = 9
EPS = 1e-6
NEG_INF = -1e30

DIFF_Q0 = 0
DIFF_K0 = DIFF_Q0 + DIFF_HEADS * 2 * DIFF_QK_DIM
DIFF_V0 = DIFF_K0 + DIFF_HEADS * 2 * DIFF_QK_DIM
CONV0 = DIFF_V0 + DIFF_HEADS * HEAD_DIM
GMLP0 = CONV0 + 2 * CONV_W
FOX_Q0 = GMLP0 + 2 * GMLP_W
FOX_K0 = FOX_Q0 + FOX_W
FOX_V0 = FOX_K0 + FOX_W
FOX_F0 = FOX_V0 + FOX_W
IN_COLS = FOX_F0 + FOX_HEADS


def _rms_norm(x, g):
    xf = x.astype(jnp.float32)
    y = xf * lax.rsqrt(jnp.mean(xf * xf, axis=-1, keepdims=True) + EPS)
    return (y * g.astype(jnp.float32)).astype(x.dtype)

def _layer_norm(x, g, b):
    xf = x.astype(jnp.float32)
    mu = jnp.mean(xf, axis=-1, keepdims=True)
    var = jnp.mean(jnp.square(xf - mu), axis=-1, keepdims=True)
    y = (xf - mu) * lax.rsqrt(var + EPS)
    return (y * g.astype(jnp.float32) + b.astype(jnp.float32)).astype(x.dtype)

def _modulate(xn, shift, scale):
    return xn * (1 + scale[:, None, :]) + shift[:, None, :]

def _swiglu(x, w_in, w_out):
    gate, up = jnp.split(x @ w_in, 2, axis=-1)
    return (jax.nn.silu(gate) * up) @ w_out

def _differential_attention(q, k, v, lam, lam_init, out_g):
    B, S, H, _, dq = q.shape
    dv = v.shape[-1]
    nb = S // Q_BLOCK
    q_blocks = jnp.moveaxis(q.reshape(B, nb, Q_BLOCK, H, 2, dq), 1, 0)
    k_pos = jnp.arange(S)
    scale = dq ** -0.5

    def one_block(args):
        qi, i = args
        s = jnp.einsum('bqhcd,bkhcd->bhcqk', qi, k).astype(jnp.float32) * scale
        q_pos = i * Q_BLOCK + jnp.arange(Q_BLOCK)
        causal = k_pos[None, :] <= q_pos[:, None]
        p = jax.nn.softmax(jnp.where(causal, s, NEG_INF), axis=-1)
        a = p[:, :, 0] - lam * p[:, :, 1]
        return jnp.einsum('bhqk,bkhe->bqhe', a.astype(v.dtype), v)

    o = lax.map(one_block, (q_blocks, jnp.arange(nb)))
    o = jnp.moveaxis(o, 0, 1).reshape(B, S, H, dv)
    o = _rms_norm(o, out_g) * (1.0 - lam_init)
    return o.reshape(B, S, H * dv)

def _conformer_conv(z, w, b, ng, nb_):
    a, g = jnp.split(z, 2, axis=-1)
    y = a * jax.nn.sigmoid(g)
    y = lax.conv_general_dilated(
        y, w[:, None, :].astype(y.dtype), window_strides=(1,),
        padding=[(CONV_KERNEL - 1, 0)],
        dimension_numbers=('NWC', 'WIO', 'NWC'),
        feature_group_count=CONV_W) + b
    return jax.nn.silu(_layer_norm(y, ng, nb_))

def _chunked_spatial_gating(z, ng, nb_, ws, bs):
    u, v = jnp.split(jax.nn.gelu(z), 2, axis=-1)
    v = _layer_norm(v, ng, nb_)
    B, S, _ = v.shape
    nc = S // CHUNK
    vh = v.reshape(B, nc, CHUNK, GMLP_HEADS, HEAD_DIM)
    w = ws * jnp.tril(jnp.ones((CHUNK, CHUNK), ws.dtype))[None]
    s = jnp.einsum('hts,bnshd->bnthd', w, vh) + jnp.transpose(bs)[None, None, :, :, None]
    return u * s.reshape(B, S, GMLP_W)

def _forgetting_attention(q, k, v, log_f):
    B, S, H, d = q.shape
    nb = S // Q_BLOCK
    cum = jnp.cumsum(log_f.astype(jnp.float32), axis=1)
    q_blocks = jnp.moveaxis(q.reshape(B, nb, Q_BLOCK, H, d), 1, 0)
    c_blocks = jnp.moveaxis(cum.reshape(B, nb, Q_BLOCK, H), 1, 0)
    cum_k = jnp.transpose(cum, (0, 2, 1))
    k_pos = jnp.arange(S)
    scale = d ** -0.5

    def one_block(args):
        qi, ci, i = args
        s = jnp.einsum('bqhd,bkhd->bhqk', qi, k).astype(jnp.float32) * scale
        s = s + jnp.transpose(ci, (0, 2, 1))[..., None] - cum_k[:, :, None, :]
        q_pos = i * Q_BLOCK + jnp.arange(Q_BLOCK)
        causal = k_pos[None, :] <= q_pos[:, None]
        p = jax.nn.softmax(jnp.where(causal, s, NEG_INF), axis=-1)
        return jnp.einsum('bhqk,bkhd->bqhd', p.astype(v.dtype), v)

    o = lax.map(one_block, (q_blocks, c_blocks, jnp.arange(nb)))
    return jnp.moveaxis(o, 0, 1).reshape(B, S, H * d)

def first_inputs(seed: int = 0) -> dict:
    key = jax.random.key(seed)
    ks = jax.random.split(key, 24)
    f32 = jnp.float32

    def nrm(k, shape, s):
        return jax.random.normal(k, shape, f32) * s

    L = DEPTH
    return {
        'x': nrm(ks[0], (BATCH, SEQ, D_MODEL), 1.0),
        'c': nrm(ks[1], (BATCH, D_MODEL), 1.0),
        'ada_w': nrm(ks[2], (L, D_MODEL, N_MOD * D_MODEL), 0.5 * D_MODEL ** -0.5),
        'ada_b': nrm(ks[3], (L, N_MOD * D_MODEL), 0.02),
        'norm_g': 1.0 + nrm(ks[4], (L, 3, D_MODEL), 0.05),
        'ffn1_w_in': nrm(ks[5], (L, D_MODEL, 2 * D_FF), D_MODEL ** -0.5),
        'ffn1_w_out': nrm(ks[6], (L, D_FF, D_MODEL), D_FF ** -0.5),
        'ffn2_w_in': nrm(ks[7], (L, D_MODEL, 2 * D_FF), D_MODEL ** -0.5),
        'ffn2_w_out': nrm(ks[8], (L, D_FF, D_MODEL), D_FF ** -0.5),
        'w_in': nrm(ks[9], (L, D_MODEL, IN_COLS), D_MODEL ** -0.5),
        'w_out': nrm(ks[10], (L, MIX_W, D_MODEL), MIX_W ** -0.5),
        'diff_qk_g': 1.0 + nrm(ks[11], (L, 2, DIFF_QK_DIM), 0.05),
        'diff_lambda': nrm(ks[12], (L, 4, DIFF_QK_DIM), 0.1),
        'diff_out_g': 1.0 + nrm(ks[13], (L, HEAD_DIM), 0.05),
        'conv_w': nrm(ks[14], (L, CONV_KERNEL, CONV_W), CONV_KERNEL ** -0.5),
        'conv_b': nrm(ks[15], (L, CONV_W), 0.02),
        'conv_norm_g': 1.0 + nrm(ks[16], (L, CONV_W), 0.05),
        'conv_norm_b': nrm(ks[17], (L, CONV_W), 0.02),
        'gmlp_norm_g': 1.0 + nrm(ks[18], (L, GMLP_W), 0.05),
        'gmlp_norm_b': nrm(ks[19], (L, GMLP_W), 0.02),
        'gmlp_ws': nrm(ks[20], (L, GMLP_HEADS, CHUNK, CHUNK), CHUNK ** -0.5),
        'gmlp_bs': 1.0 + nrm(ks[21], (L, GMLP_HEADS, CHUNK), 0.1),
        'fox_qk_g': 1.0 + nrm(ks[22], (L, 2, HEAD_DIM), 0.05),
        'fox_fb': 2.0 + nrm(ks[23], (L, FOX_HEADS), 0.5),
    }

def first_block(x, c, ada_w, ada_b, norm_g, ffn1_w_in, ffn1_w_out, ffn2_w_in, ffn2_w_out,
              w_in, w_out, diff_qk_g, diff_lambda, diff_out_g, conv_w, conv_b,
              conv_norm_g, conv_norm_b, gmlp_norm_g, gmlp_norm_b, gmlp_ws, gmlp_bs,
              fox_qk_g, fox_fb):
    B, S, _ = x.shape
    h = x
    cond = jax.nn.silu(c)
    for l in range(DEPTH):
        mod = cond @ ada_w[l] + ada_b[l]
        sh1, sc1, g1, sh2, sc2, g2, sh3, sc3, g3 = jnp.split(mod, N_MOD, axis=-1)

        hn = _modulate(_rms_norm(h, norm_g[l, 0]), sh1, sc1)
        h = h + 0.5 * g1[:, None, :] * _swiglu(hn, ffn1_w_in[l], ffn1_w_out[l])

        hn = _modulate(_rms_norm(h, norm_g[l, 1]), sh2, sc2)
        z = hn @ w_in[l]

        qa = _rms_norm(z[..., DIFF_Q0:DIFF_K0].reshape(B, S, DIFF_HEADS, 2, DIFF_QK_DIM), diff_qk_g[l, 0])
        ka = _rms_norm(z[..., DIFF_K0:DIFF_V0].reshape(B, S, DIFF_HEADS, 2, DIFF_QK_DIM), diff_qk_g[l, 1])
        va = z[..., DIFF_V0:CONV0].reshape(B, S, DIFF_HEADS, HEAD_DIM)
        lam_init = 0.8 - 0.6 * math.exp(-0.3 * l)
        lv = diff_lambda[l].astype(jnp.float32)
        lam = jnp.exp(jnp.sum(lv[0] * lv[1])) - jnp.exp(jnp.sum(lv[2] * lv[3])) + lam_init
        o_a = _differential_attention(qa, ka, va, lam, lam_init, diff_out_g[l])

        o_b = _conformer_conv(z[..., CONV0:GMLP0], conv_w[l], conv_b[l], conv_norm_g[l], conv_norm_b[l])

        o_c = _chunked_spatial_gating(z[..., GMLP0:FOX_Q0], gmlp_norm_g[l], gmlp_norm_b[l], gmlp_ws[l], gmlp_bs[l])

        qd = _rms_norm(z[..., FOX_Q0:FOX_K0].reshape(B, S, FOX_HEADS, HEAD_DIM), fox_qk_g[l, 0])
        kd = _rms_norm(z[..., FOX_K0:FOX_V0].reshape(B, S, FOX_HEADS, HEAD_DIM), fox_qk_g[l, 1])
        vd = z[..., FOX_V0:FOX_F0].reshape(B, S, FOX_HEADS, HEAD_DIM)
        log_f = jax.nn.log_sigmoid((z[..., FOX_F0:IN_COLS] + fox_fb[l]).astype(jnp.float32))
        o_d = _forgetting_attention(qd, kd, vd, log_f)

        mixed = jnp.concatenate([o_a, o_b, o_c, o_d], axis=-1)
        h = h + g2[:, None, :] * (mixed @ w_out[l])

        hn = _modulate(_rms_norm(h, norm_g[l, 2]), sh3, sc3)
        h = h + 0.5 * g3[:, None, :] * _swiglu(hn, ffn2_w_in[l], ffn2_w_out[l])
    return h


DIL_GROUPS = ((128, 1), (512, 4), (2048, 16))
HEADS_PER_DIL_GROUP = 4
N_HEADS_A = HEADS_PER_DIL_GROUP * len(DIL_GROUPS)
N_HEADS_B = 6
N_HEADS_C = 6
N_HEADS = N_HEADS_A + N_HEADS_B + N_HEADS_C
MIX_WIDTH = N_HEADS * HEAD_DIM
WIDTH_A = HEADS_PER_DIL_GROUP * HEAD_DIM
WIDTH_B = N_HEADS_B * HEAD_DIM
WIDTH_C = N_HEADS_C * HEAD_DIM
ROPE_DIM = HEAD_DIM // 4
ROPE_THETA = 500000.0
MOBA_BLOCK = 256
MOBA_TOPK = 3
MOBA_QCHUNK = 32
SB_QBLOCK = 128
D_FF_2 = 4 * D_MODEL
N_BRANCHES = 3
NORM_EPS = 1e-6
IN_COLS_2 = 3 * MIX_WIDTH + N_BRANCHES * D_MODEL


def rmsnorm(x, g):
    xf = x.astype(jnp.float32)
    y = xf * lax.rsqrt(jnp.mean(xf * xf, axis=-1, keepdims=True) + NORM_EPS)
    return (y * g.astype(jnp.float32)).astype(x.dtype)

def partial_rope(t, pos):
    inv_freq = jnp.exp(-math.log(ROPE_THETA) * jnp.arange(0, ROPE_DIM, 2, dtype=jnp.float32) / ROPE_DIM)
    ang = pos[:, None] * inv_freq[None, :]
    cos, sin = jnp.cos(ang), jnp.sin(ang)
    half = ROPE_DIM // 2
    x1, x2, rest = t[..., :half], t[..., half:ROPE_DIM], t[..., ROPE_DIM:]
    return jnp.concatenate([x1 * cos - x2 * sin, x2 * cos + x1 * sin, rest], axis=-1)

def dilated_window_attention(q, k, v, window, dilation):
    B, H, S, Dh = q.shape
    span = window // dilation
    blk = span
    unit = dilation * blk
    L = -(-S // unit) * unit
    nb = L // unit
    pad = ((0, 0), (0, 0), (0, L - S), (0, 0))

    def split(t):
        t = jnp.pad(t, pad).reshape(B, H, L // dilation, dilation, Dh)
        return jnp.swapaxes(t, 2, 3).reshape(B, H, dilation, nb, blk, Dh)

    def with_prev(t):
        prev = jnp.concatenate([jnp.zeros_like(t[:, :, :, :1]), t[:, :, :, :-1]], axis=3)
        return jnp.concatenate([prev, t], axis=4)

    qb = split(q)
    kc, vc = with_prev(split(k)), with_prev(split(v))
    s = jnp.einsum('bhrnqd,bhrnkd->bhrnqk', qb, kc) * (Dh ** -0.5)
    qi = jnp.arange(blk)[:, None]
    kj = jnp.arange(2 * blk)[None, :]
    dist = qi + blk - kj
    band = (dist >= 0) & (dist <= span)
    first = (jnp.arange(nb) == 0)[:, None, None]
    mask = band[None] & ~(first & (kj < blk)[None])
    s = jnp.where(mask, s, -jnp.inf)
    m = jnp.max(s, axis=-1, keepdims=True)
    p = jnp.exp(s - m)
    l = jnp.sum(p, axis=-1, keepdims=True)
    o = jnp.einsum('bhrnqk,bhrnkd->bhrnqd', p, vc) / l
    lse = (m + jnp.log(l))[..., 0]

    def merge(t):
        tail = t.shape[5:]
        t = t.reshape((B, H, dilation, L // dilation) + tail)
        return jnp.swapaxes(t, 2, 3).reshape((B, H, L) + tail)[:, :, :S]

    return merge(o), merge(lse)

def dilated_mixture(q, k, v):
    outs, lses = [], []
    for g, (w, d) in enumerate(DIL_GROUPS):
        sl = slice(g * HEADS_PER_DIL_GROUP, (g + 1) * HEADS_PER_DIL_GROUP)
        o, lse = dilated_window_attention(q[:, sl], k[:, sl], v[:, sl], w, d)
        outs.append(o)
        lses.append(lse)
    o = jnp.stack(outs, axis=0)
    wgt = jax.nn.softmax(jnp.stack(lses, axis=0), axis=0)
    return jnp.sum(wgt[..., None] * o, axis=0)

def moba_attention(q, k, v):
    B, H, S, Dh = q.shape
    L = -(-S // MOBA_BLOCK) * MOBA_BLOCK
    nblk = L // MOBA_BLOCK
    topk = min(MOBA_TOPK, nblk)
    pad = ((0, 0), (0, 0), (0, L - S), (0, 0))
    qp, kp, vp = jnp.pad(q, pad), jnp.pad(k, pad), jnp.pad(v, pad)
    kblocks = kp.reshape(B, H, nblk, MOBA_BLOCK, Dh)
    vblocks = vp.reshape(B, H, nblk, MOBA_BLOCK, Dh)
    kmean = jnp.mean(kblocks, axis=3)
    scale = Dh ** -0.5
    gather = jax.vmap(jax.vmap(lambda blocks, idx: blocks[idx]))

    def chunk(c):
        start = c * MOBA_QCHUNK
        qc = lax.dynamic_slice_in_dim(qp, start, MOBA_QCHUNK, axis=2)
        qpos = start + jnp.arange(MOBA_QCHUNK)
        own = start // MOBA_BLOCK
        gate = jnp.einsum('bhqd,bhnd->bhqn', qc, kmean)
        gate = jnp.where((jnp.arange(nblk) < own)[None, None, None, :], gate, -jnp.inf)
        _, idx = lax.top_k(gate, topk)
        valid = idx < own
        ksel = gather(kblocks, idx)
        vsel = gather(vblocks, idx)
        s_sel = jnp.einsum('bhqd,bhqjkd->bhqjk', qc, ksel) * scale
        s_sel = jnp.where(valid[..., None], s_sel, -jnp.inf).reshape(B, H, MOBA_QCHUNK, topk * MOBA_BLOCK)
        kown = lax.dynamic_index_in_dim(kblocks, own, axis=2, keepdims=False)
        vown = lax.dynamic_index_in_dim(vblocks, own, axis=2, keepdims=False)
        s_own = jnp.einsum('bhqd,bhkd->bhqk', qc, kown) * scale
        kpos = own * MOBA_BLOCK + jnp.arange(MOBA_BLOCK)
        s_own = jnp.where(kpos[None, :] <= qpos[:, None], s_own, -jnp.inf)
        p = jax.nn.softmax(jnp.concatenate([s_own, s_sel], axis=-1), axis=-1)
        p_own = p[..., :MOBA_BLOCK]
        p_sel = p[..., MOBA_BLOCK:].reshape(B, H, MOBA_QCHUNK, topk, MOBA_BLOCK)
        return (jnp.einsum('bhqk,bhkd->bhqd', p_own, vown)
                + jnp.einsum('bhqjk,bhqjkd->bhqd', p_sel, vsel))

    o = lax.map(chunk, jnp.arange(L // MOBA_QCHUNK))
    return jnp.moveaxis(o, 0, 2).reshape(B, H, L, Dh)[:, :, :S]

def stick_breaking_attention(q, k, v):
    B, H, S, Dh = q.shape
    scale = Dh ** -0.5
    outs = []
    for start in range(0, S, SB_QBLOCK):
        end = min(start + SB_QBLOCK, S)
        z = jnp.einsum('bhqd,bhkd->bhqk', q[:, :, start:end], k[:, :, :end]) * scale
        causal = jnp.arange(end)[None, :] < jnp.arange(start, end)[:, None]
        log_1m = jnp.where(causal, jax.nn.log_sigmoid(-z), 0.0)
        suffix = lax.cumsum(log_1m, axis=3, reverse=True) - log_1m
        a = jnp.where(causal, jnp.exp(jax.nn.log_sigmoid(z) + suffix), 0.0)
        outs.append(jnp.einsum('bhqk,bhkd->bhqd', a, v[:, :, :end]))
    return jnp.concatenate(outs, axis=2)

def hybrid_layer(x, norm_mix, w_in, w_out_a, w_out_b, w_out_c, w_o, norm_mlp, w_up, w_down, pos):
    B, S, D = x.shape
    h = rmsnorm(x, norm_mix)
    proj = h @ w_in

    def heads(t):
        return t.reshape(B, S, N_HEADS, HEAD_DIM).transpose(0, 2, 1, 3).astype(jnp.float32)

    q = heads(proj[..., :MIX_WIDTH])
    k = heads(proj[..., MIX_WIDTH:2 * MIX_WIDTH])
    v = heads(proj[..., 2 * MIX_WIDTH:3 * MIX_WIDTH])
    gates = jax.nn.sigmoid(proj[..., 3 * MIX_WIDTH:]).reshape(B, S, N_BRANCHES, D)

    n_rot = N_HEADS_A + N_HEADS_B
    q = jnp.concatenate([partial_rope(q[:, :n_rot], pos), q[:, n_rot:]], axis=1)
    k = jnp.concatenate([partial_rope(k[:, :n_rot], pos), k[:, n_rot:]], axis=1)

    a_sl = slice(0, N_HEADS_A)
    b_sl = slice(N_HEADS_A, N_HEADS_A + N_HEADS_B)
    c_sl = slice(N_HEADS_A + N_HEADS_B, N_HEADS)
    o_a = dilated_mixture(q[:, a_sl], k[:, a_sl], v[:, a_sl])
    o_b = moba_attention(q[:, b_sl], k[:, b_sl], v[:, b_sl])
    o_c = stick_breaking_attention(q[:, c_sl], k[:, c_sl], v[:, c_sl])

    def flat(o):
        return o.transpose(0, 2, 1, 3).reshape(B, S, -1).astype(x.dtype)

    y_a = flat(o_a) @ w_out_a
    y_b = flat(o_b) @ w_out_b
    y_c = flat(o_c) @ w_out_c
    merged = gates[:, :, 0] * y_a + gates[:, :, 1] * y_b + gates[:, :, 2] * y_c
    x = x + merged @ w_o

    h = rmsnorm(x, norm_mlp)
    return x + jnp.square(jax.nn.relu(h @ w_up)) @ w_down

def second_inputs(seed: int = 0) -> dict:
    key = jax.random.key(seed)
    ks = jax.random.split(key, 12)
    f32 = jnp.float32

    def nrm(k, shape, fan_in):
        return jax.random.normal(k, shape, f32) * (fan_in ** -0.5)

    x = jax.random.normal(ks[0], (BATCH, SEQ, D_MODEL), f32)
    norm_mix = 1.0 + 0.05 * jax.random.normal(ks[1], (DEPTH, D_MODEL), f32)
    w_in = nrm(ks[2], (DEPTH, D_MODEL, IN_COLS_2), D_MODEL)
    w_out_a = nrm(ks[3], (DEPTH, WIDTH_A, D_MODEL), WIDTH_A)
    w_out_b = nrm(ks[4], (DEPTH, WIDTH_B, D_MODEL), WIDTH_B)
    w_out_c = nrm(ks[5], (DEPTH, WIDTH_C, D_MODEL), WIDTH_C)
    w_o = nrm(ks[6], (DEPTH, D_MODEL, D_MODEL), D_MODEL)
    norm_mlp = 1.0 + 0.05 * jax.random.normal(ks[7], (DEPTH, D_MODEL), f32)
    w_up = nrm(ks[8], (DEPTH, D_MODEL, D_FF_2), D_MODEL)
    w_down = nrm(ks[9], (DEPTH, D_FF_2, D_MODEL), D_FF_2)
    norm_final = 1.0 + 0.05 * jax.random.normal(ks[10], (D_MODEL,), f32)
    return {"x": x, "norm_mix": norm_mix, "w_in": w_in, "w_out_a": w_out_a,
            "w_out_b": w_out_b, "w_out_c": w_out_c, "w_o": w_o, "norm_mlp": norm_mlp,
            "w_up": w_up, "w_down": w_down, "norm_final": norm_final}

def second_block(x, norm_mix, w_in, w_out_a, w_out_b, w_out_c, w_o, norm_mlp, w_up, w_down, norm_final):
    pos = jnp.arange(x.shape[1], dtype=jnp.float32)
    for layer in range(DEPTH):
        x = hybrid_layer(x, norm_mix[layer], w_in[layer], w_out_a[layer], w_out_b[layer],
                         w_out_c[layer], w_o[layer], norm_mlp[layer], w_up[layer],
                         w_down[layer], pos)
    return rmsnorm(x, norm_final)


def setup_inputs(seed=0):
    out = dict(first_inputs(seed))
    for name, value in second_inputs(seed + 1).items():
        if name != "x":
            out[name + "_2"] = value
    return out


def reference(
    x, c, ada_w, ada_b, norm_g, ffn1_w_in, ffn1_w_out, ffn2_w_in, ffn2_w_out, w_in, w_out,
    diff_qk_g, diff_lambda, diff_out_g, conv_w, conv_b, conv_norm_g, conv_norm_b, gmlp_norm_g,
    gmlp_norm_b, gmlp_ws, gmlp_bs, fox_qk_g, fox_fb, norm_mix_2, w_in_2, w_out_a_2, w_out_b_2,
    w_out_c_2, w_o_2, norm_mlp_2, w_up_2, w_down_2, norm_final_2,
):
    x = first_block(
        x, c, ada_w, ada_b, norm_g, ffn1_w_in, ffn1_w_out, ffn2_w_in, ffn2_w_out, w_in, w_out,
        diff_qk_g, diff_lambda, diff_out_g, conv_w, conv_b, conv_norm_g, conv_norm_b,
        gmlp_norm_g, gmlp_norm_b, gmlp_ws, gmlp_bs, fox_qk_g, fox_fb,
    )
    return second_block(
        x, norm_mix_2, w_in_2, w_out_a_2, w_out_b_2, w_out_c_2, w_o_2, norm_mlp_2, w_up_2,
        w_down_2, norm_final_2,
    )


_drawn_inputs = setup_inputs


def setup_inputs(seed=0):
    import zlib

    import numpy as np

    out = dict(_drawn_inputs(seed))
    spreads = {}
    factors = {'diff_qk_g': 7.763,
     'diff_out_g': 5.028,
     'conv_b': 7.022,
     'conv_norm_g': 5.49,
     'conv_norm_b': 8.0,
     'gmlp_norm_g': 8.0,
     'gmlp_norm_b': 8.0,
     'gmlp_bs': 3.074,
     'fox_qk_g': 8.0}
    for name, (base, spread) in spreads.items():
        noise = np.random.default_rng([zlib.crc32(name.encode()), seed]).standard_normal(out[name].shape)
        drawn = base * np.exp(spread * noise) if base else spread * noise
        out[name] = jnp.asarray(drawn.astype(out[name].dtype))
    for name, factor in factors.items():
        out[name] = (out[name] * factor).astype(out[name].dtype)
    return out
```

```python
from contextlib import ExitStack, contextmanager
import math

import numpy as np
import concourse.bass as bass
from concourse import mybir

F32 = mybir.dt.float32
ALU = mybir.AluOpType
ACT = mybir.ActivationFunctionType
AX = mybir.AxisListType

P = 128
D = 1024
S = 256
L = 2
KT = D // P
D_FF = ((8 * D // 3 + 127) // 128) * 128
FT = D_FF // P
PAIRS = D_FF // 256
D_FF_2 = 4 * D
EPS = 1e-6
NEG = -1e30
MOD_TILES = 9 * KT
ADA_COLS = 512
ADA_CHUNKS = 9 * D // ADA_COLS
ADA_FIRST = 2 * D // ADA_COLS
RING = 4
SCW = 384
CONV_K = 31
MIXW2 = 24 * 64

R_ADA_B, R_NORM_G, R_CONV_B, R_CONV_G, R_CONV_NB = 0, 72, 96, 98, 100
R_DQ, R_DK, R_FQ, R_FK, R_DO = 102, 103, 104, 105, 106
N_ROWS = 107
O_CW = 128
O_WST = O_CW + 64
O_BS = O_WST + 512
O_GG = O_BS + 256
O_LAM = O_GG + 512
O_WF = O_LAM + 128
O_FB = O_WF + 32
N_PAR = O_FB + 4


def constant_tables():
    at, parts = {}, []

    def put(name, a):
        at[name] = sum(p.shape[1] for p in parts)
        parts.append(np.asarray(a, np.float32).reshape(P, -1))

    r = np.arange(P)
    put("ident", np.eye(P))
    put("ones", np.ones((P, P)))
    put("group32", r[:, None] // 32 == r[None, :] // 32)
    put("group64", r[:, None] // 64 == r[None, :] // 64)
    rot = np.zeros((P, P))
    for base in (0, 64):
        for j in range(8):
            rot[base + 8 + j, base + j] = -1
            rot[base + j, base + 8 + j] = 1
    put("rotate", rot)
    put("neg_suffix", -(r[:, None] >= r[None, :]).astype(np.float32))
    put("neg_ones", -np.ones((P, P)))
    freq = np.exp(-math.log(500000.0) * np.arange(0, 16, 2, dtype=np.float32) / np.float32(16)).astype(np.float32)
    ang = (np.arange(S, dtype=np.float32)[None, :] * freq[:, None]).astype(np.float32).astype(np.float64)
    cos, sin = np.ones((P, S)), np.zeros((P, S))
    for base in (0, 64):
        for half in (0, 8):
            cos[base + half:base + half + 8] = np.cos(ang)
            sin[base + half:base + half + 8] = np.sin(ang)
    put("cos", cos)
    put("sin", sin)

    def by_query(seen):
        m = seen(np.arange(S)[:, None] - np.arange(S)[None, :])
        m = np.where(m, 0.0, NEG)
        return np.concatenate([m[:P, :P], m[P:, :]], axis=1)

    put("causal", by_query(lambda d: d >= 0))
    put("window0", by_query(lambda d: (d >= 0) & (d <= 128)))
    put("window1", by_query(lambda d: (d >= 0) & (d % 4 == 0)))
    put("window2", by_query(lambda d: (d >= 0) & (d % 16 == 0)))
    k, q = np.arange(S)[:, None], np.arange(S)[None, :]
    before = (k < q).astype(np.float32)
    before = np.concatenate([before[:P, :], before[P:, P:]], axis=1)
    put("before", before)
    put("before_neg", np.where(before > 0, 0.0, NEG))
    put("mix_seen", r[:, None] <= r[None, :])
    put("in32", r[:, None] // 32 == np.arange(4)[None, :])
    put("in64", r[:, None] // 64 == np.arange(2)[None, :])
    put("in64_eighth", (r[:, None] // 64 == np.arange(2)[None, :]) * 0.125)
    put("cum_row", r[:, None] == 32 * np.arange(4)[None, :])
    put("one_row", r[:, None] == 32 * np.arange(4)[None, :] + 1)
    put("neg_cum_rows", -(r[:, None] % 32 == 1).astype(np.float32))
    put("one_rows", r[:, None] % 32 == 0)
    put("eps", np.full((P, 1), EPS))
    init = [0.8 - 0.6 * math.exp(-0.3 * l) for l in range(L)]
    put("lam_init", np.tile([[x, 1 - x] for x in init], (P, 1, 1)).reshape(P, 2 * L))
    table = np.concatenate(parts, axis=1)
    return np.ascontiguousarray(table), at


class Plan:

    def __init__(self):
        self.totals, self.bodies, self.marks = {}, {}, {}


PARTS = ("pre", "one", "two", "post")
TIMES = {"pre": 1, "one": L, "two": L, "post": 1}


class Engine:

    def __init__(self, e, own, plan, old):
        self.e, self.own, self.plan, self.old = e, own, plan, old
        self.part, self.layer = "pre", None
        self.loop, self.turn = None, None
        self.count = {}

    @contextmanager
    def layers(self, part):
        self._close()
        self.part, self.count = part, {}
        with self.e.Fori(0, L) as layer:
            self.layer = layer
            yield layer
            self._close()
        self.layer = None
        self.part, self.count = PARTS[PARTS.index(part) + 1], {}

    def _close(self):
        for k, v in self.count.items():
            self.plan.totals[k, self.part] = v

    def step(self, mark=None, sem=None, by=1):
        s = sem or self.own
        k = s.name
        self.count[k] = self.count.get(k, 0) + by
        if mark:
            self.plan.marks[mark] = (s, self.part, self.count[k], self.loop)
        return by

    def _value(self, s, part, local, loop, back=0):
        old, k = self.old, s.name
        value = sum(old.totals.get((k, q), 0) * TIMES[q] for q in PARTS[:PARTS.index(part)]) + local
        least = value
        if TIMES[part] > 1:
            total = old.totals.get((k, part), 0)
            value = value + (self.layer * total if part == self.part else (L - 1) * total)
        if loop:
            body = old.bodies.get((k, part, loop), 0)
            if loop == self.loop:
                value = value + self.turn * body
                least -= back * body
                if back:
                    value = value - back * body
            else:
                value = value + (old.bodies.get(loop, 1) - 1) * body
        if not old.totals:
            return 1
        assert least > 0, (k, part, local, loop)
        return value

    def at(self, mark=None, back=0):
        if mark is None:
            return self._value(self.own, self.part, self.count.get(self.own.name, 0), self.loop)
        if not self.old.marks:
            return 1
        s, part, local, loop = self.old.marks[mark]
        return self._value(s, part, local, loop, back)

    @contextmanager
    def turns(self, name, n):
        start = dict(self.count)
        with self.e.Fori(0, n) as turn:
            self.loop, self.turn = name, turn
            yield turn
        for k, v in list(self.count.items()):
            body = v - start.get(k, 0)
            self.plan.bodies[k, self.part, name] = body
            self.count[k] = v + (n - 1) * body
        self.plan.bodies[name] = n
        self.loop = self.turn = None


ONE = {"f1in": 2 * PAIRS, "f1out": 16, "z": 12, "o": 4, "f2in": 2 * PAIRS, "f2out": 16}
TWO = {"z2": 32, "y": 4, "wo": 4, "up": 16, "dn": 16}
CHUNKS = {"one": sum(ONE.values()), "two": sum(TWO.values())}
assert CHUNKS["one"] % RING == 0 and CHUNKS["two"] % RING == 0
START = {}
for _phases in (ONE, TWO):
    _at = 0
    for _name, _n in _phases.items():
        START[_name] = _at
        _at += _n
FF_PARTS = ((0, 6), (6, 6), (12, 5), (17, 5))
DN_PARTS = ((0, 8), (8, 8), (16, 8), (24, 8))
assert sum(n for _, n in FF_PARTS) == FT

Z_UNITS = (("dq", (0, 1), 0, False), ("dk", (2, 3), 256, False), ("dv", (4,), 512, True),
           ("fq", (5,), 1792, False), ("fk", (6,), 2048, False), ("fv", (7,), 2304, True),
           ("ca", (8,), 768, False), ("cg", (9,), 1024, False), ("gu", (10,), 1280, False),
           ("gv", (11,), 1536, True))
FOX_F0 = 2560
Z2_UNITS = tuple((f"{'qkvgg'[i // 6]}{i if i >= 18 else i % 6}", (2 * i, 2 * i + 1) if i < 2 else (i + 2,),
                  256 * i, 12 <= i < 18) for i in range(30))


def slot_of(phase, i):
    return (START[phase] + i) % RING


class Head:

    def __init__(self, name, kind, maps, out_tile, half):
        self.name, self.kind, self.maps, self.out_tile, self.half = name, kind, maps, out_tile, half


HEADS_ONE = [Head(f"d{h}", "diff", [(4 * (h // 2) + 2 * (h % 2) + c, h // 2, h // 2, "causal") for c in range(2)],
                  h // 2, h % 2) for h in range(4)]
HEADS_ONE += [Head(f"x{h}", "fox", [(h, h // 2, h // 2, "causal")], h // 2, h % 2) for h in range(4)]
HEADS_TWO = [Head(f"a{j}", "soft", [(4 * g + j, (4 * g + j) // 2, (4 * g + j) // 2, f"window{g}") for g in range(3)],
                  j // 2, j % 2) for j in range(4)]
HEADS_TWO += [Head(f"b{j}", "soft", [(12 + j, (12 + j) // 2, (12 + j) // 2, "causal")], 2 + j // 2, j % 2)
              for j in range(6)]
HEADS_TWO += [Head(f"c{j}", "stick", [(18 + j, (18 + j) // 2, (18 + j) // 2, None)], 5 + j // 2, j % 2)
              for j in range(6)]
SLOTS = 6


def place_heads(heads):
    n = {"sb": 0, "tp": 0, "pb": 0, "ps": 0}
    last = {}

    def take(kind, size, frees):
        i = n[kind] % size
        n[kind] += 1
        before = last.get((kind, i))
        last[kind, i] = frees
        return i, before

    for u, h in enumerate(heads):
        h.u, h.pair = u, u // 2
        if h.kind == "stick":
            h.sb = [take("sb", 2, f"sp {h.name}")]
            h.tp = [take("tp", SLOTS, f"copied {h.name} 0"), take("tp", SLOTS, f"arg {h.name}")]
            h.pb = [take("pb", 2, f"argm {h.name}")]
            h.ps = [take("ps", SLOTS, f"out {h.name}")]
        else:
            turned = 1 if h.kind == "diff" else len(h.maps)
            h.sb = [take("sb", 2, f"max {h.name} {m}") for m in range(len(h.maps))]
            h.tp = [take("tp", SLOTS, f"turned {h.name} {min(m, turned - 1)}") for m in range(len(h.maps))]
            h.pb = [take("pb", 2, f"copied {h.name} {m}") for m in range(turned)]
            h.ps = [take("ps", SLOTS, f"out {h.name}") for m in range(turned)]
    return heads


place_heads(HEADS_ONE)
place_heads(HEADS_TWO)

IN_NAMES = ["x", "c", "ada_w", "ada_b", "norm_g", "ffn1_w_in", "ffn1_w_out", "ffn2_w_in", "ffn2_w_out", "w_in",
            "w_out", "diff_qk_g", "diff_lambda", "diff_out_g", "conv_w", "conv_b", "conv_norm_g", "conv_norm_b",
            "gmlp_norm_g", "gmlp_norm_b", "gmlp_ws", "gmlp_bs", "fox_qk_g", "fox_fb", "norm_mix_2", "w_in_2",
            "w_out_a_2", "w_out_b_2", "w_out_c_2", "w_o_2", "norm_mlp_2", "w_up_2", "w_down_2", "norm_final_2"]


def build(nc, dram, out, at, old):
    plan = Plan()
    with ExitStack() as ctx:
        def sb(name, *shape):
            return ctx.enter_context(nc.sbuf_tensor(name, [P, *shape], F32))

        def sem(name):
            return ctx.enter_context(nc.semaphore(name))

        bank = ctx.enter_context(nc.psum_tensor("bank", [P, 8, 512], F32))
        ring = sb("ring", RING, 8, 256)
        h = sb("h", KT, S)
        hn = sb("hn", KT, S)
        sq = sb("sq", KT, S)
        rstd = sb("rstd", S)
        act_tmp = sb("act_tmp", 2, 512)
        n_const = dram["constants"].shape[1]
        const = sb("const", n_const)
        par_all = sb("par_all", L, N_PAR)
        par = sb("par", N_PAR)
        mod_first = sb("mod_first", L, 16)
        mod = sb("mod", MOD_TILES)
        der = sb("der", 64)
        cond = sb("cond", KT)
        norm2 = sb("norm2", 40)
        stat = sb("stat", 4, 16)
        small = sb("small", 64)
        ada_acc = sb("ada_acc", 2, ADA_COLS)
        arena = sb("arena", 26688)

        def view(start, *dims):
            n = int(np.prod(dims))
            v = arena[:, start:start + n]
            names = " ".join(f"d{i}" for i in range(len(dims)))
            if len(dims) == 1:
                return v
            return v.rearrange(f"p ({names}) -> p {names}", **{f"d{i}": d for i, d in enumerate(dims[1:], 1)})

        ada = view(0, 2, 8, ADA_COLS)
        gated = view(8192, FT, S)
        tile1, turned1 = view(8192, SLOTS, SCW), view(8192 + SLOTS * SCW, SLOTS, SCW)
        wfx = view(8192 + 2 * SLOTS * SCW, KT, P)
        o = 8192 + FT * S
        place = {}
        for name, dims in (("qd", (8, S)), ("kd", (2, S)), ("vd", (2, S)), ("qf", (4, S)), ("kf", (2, S)),
                           ("vf", (2, S)), ("fa", (4, S)), ("fb", (S,)), ("yp", (2, 288)), ("cv", (2, S)),
                           ("u", (2, S)), ("vg", (2, S)), ("mix", (8, S)), ("ft", (3, S)), ("od", (2, S)),
                           ("cg", (2, S)), ("cd", (2, S))):
            place[name] = view(o, *dims)
            o += int(np.prod(dims))
        assert o <= 26688, o
        qd, kd, vd, qf, kf, vf, fa, fb, yp, cv, u_, vg, mix, ft, od, cg, cd = place.values()
        qs = sq[:, 0:4, :].rearrange("p (a b) s -> p a (b s)", a=2)
        rr = sq[:, 4:8, :].rearrange("p (a b) s -> p a (b s)", a=2)
        rows = view(8192, L, P)
        rows_cw = view(8192 + 256, L, P)
        rows_ws = view(8192 + 512, L, 4, P)
        rows_n2 = view(8192 + 1536, P)
        rows_c = view(8192 + 1664, P)
        q2 = view(0, 24, S)
        k2 = view(6144, 12, S)
        v2 = view(9216, 2, MIXW2)
        merged = view(9216, KT, S)
        up2 = view(0, 32, S)
        gates = view(12288, 24, S)
        o2 = view(18432, KT, S)
        tile2, turned2 = view(20480, SLOTS, SCW), view(20480 + SLOTS * SCW, SLOTS, SCW)
        raw = sq[:, 0:4, :].rearrange("p (a b) s -> p a (b s)", a=2)
        rot_tmp = sq[:, 4:8, :].rearrange("p (a b) s -> p a (b s)", a=2)

        def tab(name, n=P, off=0):
            return const[:, at[name] + off:at[name] + off + n]

        ident, ones = tab("ident"), tab("ones")
        eps = tab("eps", 1)

        tensor_done, scalar_done = sem("tensor_done"), sem("scalar_done")
        vector_done, pool_done = sem("vector_done"), sem("pool_done")
        weights_used = sem("weights_used")
        weights_in = [sem(f"weights_in_{i}") for i in range(RING)]
        ada_in = [sem("ada_in_0"), sem("ada_in_1")]
        ada_summed, ada_reduced = sem("ada_summed"), sem("ada_reduced")
        x_in, params_in, tables_in, stored = sem("x_in"), sem("params_in"), sem("tables_in"), sem("stored")

        passed = [sem("tensor_passed"), sem("vector_passed")]

        def done_by(mark):
            return {"turned": tensor_done, "arg": tensor_done, "out": tensor_done, "copied": scalar_done,
                    "max": vector_done, "sp": vector_done, "argm": vector_done}[mark.split()[0]]

        block = ctx.enter_context(nc.Block())

        ADA_PRE = L * ADA_FIRST
        ADA_REST = ADA_CHUNKS - ADA_FIRST
        n_params = [0]
        n_params_total = 1 + L * (4 + 1 + 5 + 1 + 1 + 1 + 4 + 2 + 1 + 1) + 3

        @block.sync
        def _(sp):
            eng = Engine(sp, weights_used, plan, old)
            sp.dma_start(sq[:].rearrange("p (t k) s -> p t (k s)", t=2),
                         dram["x"][0].rearrange("(t p) d -> p t d", p=P)).then_inc(x_in, 16)

            def fill(phase, i, before, nk, *sources):
                s = slot_of(phase, i)
                sp.wait_ge(weights_used, before + 1)
                k = 0
                for src in sources:
                    n = src.shape[1]
                    assert k + n <= nk
                    sp.dma_start(ring[:, s, k:k + n, :], src) \
                        .then_inc(weights_in[s], eng.step(f"full {phase} {i}", weights_in[s], 16))
                    k += n

            def chunk(w, layer, k0, nk, col):
                return w[bass.ds(layer, 1), k0 * P:(k0 + nk) * P, col].rearrange("o (k p) n -> p (o k) n", p=P)

            def ffn(s, w_in, w_out, layer, before):
                b = before + START[s + "in"]
                with eng.turns(s + "in", PAIRS // 2) as t:
                    for i in range(4):
                        fill(s + "in", i, b + t * 4 + i, 8,
                             chunk(w_in, layer, 0, 8, bass.ds(t * 512 + (i // 2) * 256 + (i % 2) * D_FF, 256)))
                for i in (2 * PAIRS - 2, 2 * PAIRS - 1):
                    c = 256 * (PAIRS - 1) + (i % 2) * D_FF
                    fill(s + "in", i, b + i, 8, chunk(w_in, layer, 0, 8, slice(c, c + 256)))
                b = before + START[s + "out"]
                with eng.turns(s + "out", 2) as t:
                    for i in range(8):
                        k0, nk = FF_PARTS[i % 4]
                        fill(s + "out", i, b + t * 8 + i, nk,
                             chunk(w_out, layer, k0, nk, bass.ds(t * 512 + (i // 4) * 256, 256)))

            with eng.layers("one") as layer:
                before = layer * CHUNKS["one"]
                ffn("f1", dram["ffn1_w_in"], dram["ffn1_w_out"], layer, before)
                b = before + START["z"]
                for _, chunks, col, _ in Z_UNITS:
                    for j, i in enumerate(chunks):
                        nk = 8 // len(chunks)
                        fill("z", i, b + i, nk, chunk(dram["w_in"], layer, nk * j, nk, slice(col, col + 256)))
                b = before + START["o"]
                for i in range(4):
                    fill("o", i, b + i, 8, chunk(dram["w_out"], layer, 0, 8, slice(256 * i, 256 * i + 256)))
                ffn("f2", dram["ffn2_w_in"], dram["ffn2_w_out"], layer, before)
            with eng.layers("two") as layer:
                before = layer * CHUNKS["two"] + L * CHUNKS["one"]
                b = before + START["z2"]
                for _, chunks, col, _ in Z2_UNITS:
                    for j, i in enumerate(chunks):
                        nk = 8 // len(chunks)
                        fill("z2", i, b + i, nk, chunk(dram["w_in_2"], layer, nk * j, nk, slice(col, col + 256)))
                b = before + START["y"]
                for i in range(4):
                    c = slice(256 * i, 256 * i + 256)
                    fill("y", i, b + i, 8, chunk(dram["w_out_a_2"], layer, 0, 2, c),
                         chunk(dram["w_out_b_2"], layer, 0, 3, c), chunk(dram["w_out_c_2"], layer, 0, 3, c))
                b = before + START["wo"]
                for i in range(4):
                    fill("wo", i, b + i, 8, chunk(dram["w_o_2"], layer, 0, 8, slice(256 * i, 256 * i + 256)))
                b = before + START["up"]
                with eng.turns("up", 4) as t:
                    for i in range(4):
                        fill("up", i, b + t * 4 + i, 8,
                             chunk(dram["w_up_2"], layer, 0, 8, bass.ds(t * 1024 + i * 256, 256)))
                b = before + START["dn"]
                with eng.turns("dn", 2) as t:
                    for i in range(8):
                        k0, nk = DN_PARTS[i % 4]
                        fill("dn", i, b + t * 8 + i, nk,
                             chunk(dram["w_down_2"], layer, k0, nk, bass.ds(t * 512 + (i // 4) * 256, 256)))
            for t in range(2):
                sp.wait_ge(scalar_done, eng.at(f"result {t}"))
                sp.dma_start(out[0, t * P:(t + 1) * P, :],
                             sq[:, 4 * t:4 * t + 4, :].rearrange("p k s -> p (k s)")).then_inc(stored, 16)
            sp.wait_ge(stored, 32)

        @block.gpsimd
        def _(pool):
            eng = Engine(pool, pool_done, plan, old)

            def fill(j, layer, col):
                pool.dma_start(ada[:, j], dram["ada_w"][bass.ds(layer, 1), :, col]
                               .rearrange("o (k p) n -> p (o k) n", p=P)) \
                    .then_inc(ada_in[j], eng.step(None, ada_in[j], 16))

            pool.memset(yp[:, :, 0:CONV_K - 1], 0.0).then_inc(pool_done, eng.step("conv pad"))
            for n in range(ADA_PRE):
                layer, i = divmod(n, ADA_FIRST)
                if n >= 2:
                    pool.wait_ge(ada_summed, n - 1)
                pool.dma_start(ada[:, n % 2], dram["ada_w"][layer, :, i * ADA_COLS:(i + 1) * ADA_COLS]
                               .rearrange("(k p) n -> p k n", p=P)).then_inc(ada_in[n % 2], 16)
            with eng.layers("one") as layer:
                n0 = layer * ADA_REST + ADA_PRE
                with eng.turns("f1in", PAIRS // 2) as t:
                    for j in range(2):
                        pool.wait_ge(ada_summed, n0 + t * 2 + j - 1)
                        fill(j, layer, bass.ds(t * (2 * ADA_COLS) + (ADA_FIRST + j) * ADA_COLS, ADA_COLS))
                with eng.turns("f1out", 2) as t:
                    for j in range(2):
                        pool.wait_ge(ada_summed, n0 + t * 2 + 10 + j - 1)
                        fill(j, layer, bass.ds(t * (2 * ADA_COLS) + (ADA_FIRST + 10 + j) * ADA_COLS, ADA_COLS))

        @block.tensor
        def _(pe):
            eng = Engine(pe, tensor_done, plan, old)
            mm = pe.matmul
            pe.sem_inc(weights_used, RING)
            eng.count[weights_used.name] = RING

            def turn(dst, src, mark=None):
                n = src.shape[0]
                i = pe.transpose(dst, src, ident[0:n, 0:n])
                if mark:
                    i.then_inc(tensor_done, eng.step(mark))

            def product(phase, chunks, x, outs, token_major=False, done=None, parts=None, free=()):
                parts = parts or [(j * (8 // len(chunks)), 8 // len(chunks)) for j in range(len(chunks))]
                total = sum(n for _, n in parts)
                for c in range(2):
                    for by, mark, back in free[c:c + 1]:
                        pe.wait_ge(by, eng.at(mark, back))
                    step = 0
                    for i, (k0, nk) in zip(chunks, parts):
                        s = slot_of(phase, i)
                        if c == 0:
                            pe.wait_ge(weights_in[s], eng.at(f"full {phase} {i}"))
                        for k in range(nk):
                            if token_major:
                                a, b = x[:, k0 + k, c * P:(c + 1) * P], ring[:, s, k, :]
                            else:
                                a, b = ring[:, s, k, c * P:(c + 1) * P], x[:, k0 + k, :]
                            last = mm(outs[c], a, b, start=(step == 0), stop=(step == total - 1))
                            step += 1
                        if c == 1:
                            last.then_inc(weights_used, eng.step(f"used {phase} {i}", weights_used))
                    if c == 0 and done:
                        last.then_inc(tensor_done, eng.step(done))

            def norm_sum(n):
                pe.wait_ge(scalar_done, eng.at(f"squares a {n}"))
                for k in range(KT):
                    if k == 4:
                        pe.wait_ge(vector_done, eng.at(f"squares b {n}"))
                    last = mm(bank[:, 4, 0:S], ones, sq[:, k, :], start=(k == 0), stop=(k == KT - 1))
                last.then_inc(tensor_done, eng.step(f"sum {n}"))

            def ada_reduce(n, slot, col):
                pe.wait_ge(ada_summed, n + 1)
                for j in range(4):
                    last = mm(bank[:, 7, bass.ds(col + j, 1)], ada_acc[:, slot, j * P:(j + 1) * P], ones[:, 0:1],
                              start=True, stop=True)
                last.then_inc(ada_reduced, 1)

            pe.wait_ge(tables_in, 16)
            pe.wait_ge(x_in, 16)
            x_tm = sq[:].rearrange("p (t k) s -> p t (k s)", t=2)
            for k in range(KT):
                for t in range(2):
                    turn(bank[:, k // 2, (k % 2) * S + t * P:(k % 2) * S + (t + 1) * P], x_tm[:, t, k * P:(k + 1) * P],
                         f"x turned {k // 2}" if k % 2 and t else None)
            pe.wait_ge(params_in, 16 * n_params_total)
            turn(bank[:, 4, 0:KT], rows_c[0:KT], "c turned")
            for l in range(L):
                turn(bank[:, 5, l * P:l * P + N_ROWS], rows[0:N_ROWS, l])
                turn(bank[:, 5, 256 + l * 64:256 + l * 64 + 62], rows_cw[0:62, l])
            turn(bank[:, 5, 384:424], rows_n2[0:40], "rows turned")
            for l in range(L):
                if l:
                    pe.wait_ge(vector_done, eng.at("mix weights 0"))
                for j in range(4):
                    turn(bank[:, 6, j * P:(j + 1) * P], rows_ws[:, l, j], f"ws turned {l}" if j == 3 else None)
            for n in range(ADA_PRE):
                ada_reduce(n, n % 2, 4 * n)

            def ffn(s, w_ada, n0):
                pe.wait_ge(scalar_done, eng.at(f"normed {s}"))
                pe.sem_inc(passed[0], 1)
                with eng.turns(s + "in", PAIRS // 2) as t:
                    for j in range(2):
                        for r in range(2):
                            b = bank[:, 2 * j + r].rearrange("p (c s) -> p c s", c=2)
                            product(s + "in", (2 * j + r,), hn, (b[:, 0], b[:, 1]),
                                    free=(((scalar_done, f"{s} silu {j}", 1), (vector_done, f"{s} gated {j}", 1))[r],))
                        if w_ada:
                            ada_reduce(n0 + t * 2 + j, j, t * 8 + 16 + 4 * j)
                for r in range(2):
                    b = bank[:, r].rearrange("p (c s) -> p c s", c=2)
                    product(s + "in", (2 * PAIRS - 2 + r,), hn, (b[:, 0], b[:, 1]),
                            free=(((scalar_done, f"{s} silu 0", 0), (vector_done, f"{s} gated 0", 0))[r],))
                pe.wait_ge(vector_done, eng.at(f"{s} gated last"))
                pe.sem_inc(passed[0], 1)
                with eng.turns(s + "out", 2) as t:
                    for j in range(2):
                        product(s + "out", tuple(range(4 * j, 4 * j + 4)), gated,
                                (bank[:, 2 * j, 0:S], bank[:, 2 * j + 1, 0:S]), parts=FF_PARTS,
                                done=f"{s} out {j}", free=((vector_done, f"{s} h {j} 0", 1), (vector_done, f"{s} h {j} 1", 1)))
                        if w_ada:
                            ada_reduce(n0 + t * 2 + 10 + j, j, t * 8 + 56 + 4 * j)

            def scores(hd, q, k):
                for m, (qi, ki, _, _) in enumerate(hd.maps):
                    sbk, free = hd.sb[m]
                    if free:
                        pe.wait_ge(vector_done, eng.at(free))
                    b = bank[:, 2 + sbk]
                    if hd.kind == "stick":
                        mm(b[:, 0:256], k[:, ki, 0:P], q[:, qi, :], start=True, stop=True)
                        last = mm(b[:, 256:384], k[:, ki, P:S], q[:, qi, P:S], start=True, stop=True)
                    else:
                        fox = hd.kind == "fox"
                        for c0, c1, n in ((0, P, P), (P, SCW, S)):
                            qq = slice(0, P) if c0 == 0 else slice(P, S)
                            last = mm(b[:, c0:c1], q[:, qi, qq], k[:, ki, 0:n], start=True, stop=not fox)
                            if fox:
                                last = mm(b[:, c0:c1], fa[:, qi, qq], fb[:, 0:n], start=False, stop=True)
                    last.then_inc(tensor_done, eng.step(f"scores {hd.name} {m}"))

            def turned(hd, q, k, tile):
                if hd.kind == "stick":
                    (qi, ki, _, _), (pb, free) = hd.maps[0], hd.pb[0]
                    if free:
                        pe.wait_ge(done_by(free), eng.at(free))
                    b, sp_ = bank[:, 4 + pb], tile[:, hd.tp[1][0], :]
                    mm(b[:, 0:256], k[:, ki, 0:P], q[:, qi, :], start=True, stop=False)
                    pe.wait_ge(vector_done, eng.at(f"sp {hd.name}"))
                    mm(b[:, 0:256], tab("neg_suffix"), sp_[:, 0:256], start=False, stop=False)
                    mm(b[:, 128:256], tab("neg_ones"), sp_[:, 256:384], start=False, stop=True)
                    mm(b[:, 256:384], k[:, ki, P:S], q[:, qi, P:S], start=True, stop=False)
                    mm(b[:, 256:384], tab("neg_suffix"), sp_[:, 256:384], start=False, stop=True) \
                        .then_inc(tensor_done, eng.step(f"arg {hd.name}"))
                    return
                pe.wait_ge(vector_done, eng.at(f"scaled {hd.name}"))
                for m in range(len(hd.pb)):
                    pb, free = hd.pb[m]
                    if free:
                        pe.wait_ge(scalar_done, eng.at(free))
                    for j in range(3):
                        turn(bank[:, 4 + pb, j * P:(j + 1) * P], tile[:, hd.tp[m][0], j * P:(j + 1) * P],
                             f"turned {hd.name} {m}" if j == 2 else None)

            def outputs(hd, v, tt, evacuated):
                if evacuated and hd.half == 0:
                    pe.wait_ge(vector_done, eng.at(evacuated))
                b = bank[:, 6 + hd.pair % 2].rearrange("p (a s) -> p a s", a=2)[:, hd.half]
                n = len(hd.ps)
                for m in range(n):
                    pe.wait_ge(scalar_done, eng.at(f"copied {hd.name} {m}"))
                    vt = hd.maps[m][2]
                    p_ = tt[:, hd.ps[m][0]]
                    mm(b[:, 0:S], v[:, 0, vt * P:(vt + 1) * P], p_[:, 0:S], start=(m == 0), stop=False)
                    last = mm(b[:, P:S], v[:, 1, vt * P:(vt + 1) * P], p_[:, S:SCW], start=False, stop=(m == n - 1))
                last.then_inc(tensor_done, eng.step(f"out {hd.name}"))

            def attention(heads, q_of, tile, tt, filler):
                for i in range(len(heads) + 2):
                    if i < len(heads):
                        scores(heads[i], *q_of(heads[i])[:2])
                    if filler:
                        filler(i)
                    if 0 <= i - 1 < len(heads):
                        turned(heads[i - 1], *q_of(heads[i - 1])[:2], tile)
                    if i >= 2:
                        hd = heads[i - 2]
                        outputs(hd, q_of(hd)[2], tt, f"heads {heads[0].name} {hd.pair - 2}" if hd.pair >= 2 else None)

            with eng.layers("one") as layer:
                n0 = layer * ADA_REST + ADA_PRE
                norm_sum("f1")
                ffn("f1", True, n0)
                norm_sum("z")
                z_free = {"fk": (vector_done, "dq scaled", 0), "fv": (vector_done, "dk scaled", 0),
                          "ca": (scalar_done, "dv copied", 0), "cg": (vector_done, "fq scaled", 0),
                          "gu": (vector_done, "fk scaled", 0), "gv": (scalar_done, "fv copied", 0)}

                def z_unit(i):
                    name, chunks, _, tm = Z_UNITS[i]
                    b = bank[:, i % 4].rearrange("p (c s) -> p c s", c=2)
                    product("z", chunks, hn, (b[:, 0], b[:, 1]), token_major=tm,
                            free=(z_free[name],) if name in z_free else ())

                def group_sum(name, group, b):
                    pe.wait_ge(scalar_done, eng.at(f"{name} squares"))
                    mm(bank[:, b], tab(group), qs[:, 0 if name in ("dq", "fq", "od") else 1, :],
                       start=True, stop=True).then_inc(tensor_done, eng.step(f"{name} sum"))

                pe.wait_ge(scalar_done, eng.at("normed z"))
                z_unit(0)
                z_unit(1)
                group_sum("dq", "group32", 5)
                z_unit(2)
                group_sum("dk", "group32", 6)
                z_unit(3)
                z_unit(4)
                pe.wait_ge(scalar_done, eng.at("dq rstd"))
                group_sum("fq", "group64", 5)
                z_unit(5)
                pe.wait_ge(scalar_done, eng.at("dk rstd"))
                group_sum("fk", "group64", 6)
                pe.wait_ge(vector_done, eng.at("forget weights"))
                for k in range(KT):
                    last = mm(bank[:, 4, 0:S], wfx[:, k, :], hn[:, k, :], start=(k == 0), stop=(k == KT - 1))
                last.then_inc(tensor_done, eng.step("forget sum"))
                for i in range(6, 10):
                    z_unit(i)
                pe.wait_ge(vector_done, eng.at("gate normed"))
                pe.wait_ge(scalar_done, eng.at("u"))
                for j in range(4):
                    for c in range(2):
                        last = mm(bank[:, j // 2].rearrange("p (a c s) -> p a c s", a=2, c=2)[:, j % 2, c],
                                  vg[:, c, (j // 2) * P:(j // 2 + 1) * P],
                                  par[:, O_WST + j * P:O_WST + (j + 1) * P], start=True, stop=True)
                    if j % 2:
                        last.then_inc(tensor_done, eng.step(f"mixed {j // 2}"))
                pe.wait_ge(vector_done, eng.at("conv in"))
                pe.wait_ge(vector_done, eng.at("forget rows"))
                pe.wait_ge(vector_done, eng.at("fk scaled"))
                attention(HEADS_ONE, lambda hd: (qd, kd, vd) if hd.kind == "diff" else (qf, kf, vf),
                          tile1, turned1, None)
                pe.wait_ge(vector_done, eng.at("heads d0 0"))
                pe.wait_ge(vector_done, eng.at("heads d0 1"))
                pe.wait_ge(scalar_done, eng.at("od squares"))
                group_sum("od", "group64", 5)
                pe.wait_ge(vector_done, eng.at("conv out"))
                pe.wait_ge(vector_done, eng.at("mixed out"))
                for i in range(2):
                    last = mm(bank[:, 0, 0:S], ones, cv[:, i, :], start=(i == 0), stop=(i == 1))
                last.then_inc(tensor_done, eng.step("conv mean"))
                pe.wait_ge(scalar_done, eng.at("conv squares"))
                for i in range(2):
                    last = mm(bank[:, 1, 0:S], ones, cg[:, i, :], start=(i == 0), stop=(i == 1))
                last.then_inc(tensor_done, eng.step("conv var"))
                pe.wait_ge(vector_done, eng.at("heads d0 3"))
                pe.wait_ge(vector_done, eng.at("od normed"))
                pe.wait_ge(scalar_done, eng.at("conv done"))
                for i in range(4):
                    b = bank[:, i].rearrange("p (c s) -> p c s", c=2)
                    product("o", (i,), mix, (b[:, 0], b[:, 1]))
                norm_sum("f2")
                ffn("f2", False, None)

            def group_of(i):
                return bank[:, i % 2].rearrange("p (c s) -> p c s", c=2)

            with eng.layers("two") as layer:
                norm_sum("z2")
                pe.wait_ge(vector_done, eng.at("normed z2"))

                def z2_unit(i):
                    name, chunks, _, tm = Z2_UNITS[i]
                    b = bank[:, i % 4] if i < 18 else bank[:, i % 2]
                    b = b.rearrange("p (c s) -> p c s", c=2)
                    free = ()
                    if 4 <= i:
                        free = ((scalar_done, f"z2 out {i - 4 if i < 18 else i - 2}", 0),)
                    product("z2", chunks, hn, (b[:, 0], b[:, 1]), token_major=tm, free=free)

                def rotate(i):
                    pe.wait_ge(scalar_done, eng.at(f"z2 out {i}"))
                    if i >= 2 and i not in (6, 7):
                        pe.wait_ge(vector_done, eng.at(f"rotated {i - 2}"))
                    if i in (6, 7):
                        pe.wait_ge(vector_done, eng.at(f"rotated {i - 3}"))
                    mm(bank[:, 5 + i % 2], tab("rotate"), raw[:, i % 2, :], start=True, stop=True) \
                        .then_inc(tensor_done, eng.step(f"rotary {i}"))

                for i in range(18):
                    z2_unit(i)
                    if 1 <= i <= 12 and (i - 1) not in (5, 11):
                        rotate(i - 1)
                pe.wait_ge(vector_done, eng.at("rotated 10"))
                pe.wait_ge(scalar_done, eng.at("z2 out 17"))
                for g in range(2):
                    z2_unit(18 + g)
                done = [20]

                def filler(i):
                    if done[0] < 30:
                        z2_unit(done[0])
                        done[0] += 1

                attention(HEADS_TWO, lambda hd: (q2, k2, v2), tile2, turned2, filler)
                pe.wait_ge(vector_done, eng.at("heads a0 7"))
                y_parts = (("a", 0, 2), ("b", 2, 3), ("c", 5, 3))
                for i in range(4):
                    s = slot_of("y", i)
                    pe.wait_ge(weights_in[s], eng.at(f"full y {i}"))
                    if i == 0:
                        pe.wait_ge(scalar_done, eng.at("z2 out 29"))
                    if i >= 2:
                        pe.wait_ge(vector_done, eng.at(f"merged {i - 2}"))
                    for br, (_, k0, nk) in enumerate(y_parts):
                        b = bank[:, 3 * (i % 2) + br].rearrange("p (c s) -> p c s", c=2)
                        for c in range(2):
                            for k in range(nk):
                                last = mm(b[:, c], ring[:, s, k0 + k, c * P:(c + 1) * P], o2[:, k0 + k, :],
                                          start=(k == 0), stop=(k == nk - 1))
                    last.then_inc(weights_used, eng.step(f"used y {i}", weights_used))
                pe.wait_ge(vector_done, eng.at("merged 3"))
                for i in range(4):
                    b = bank[:, i].rearrange("p (c s) -> p c s", c=2)
                    product("wo", (i,), merged, (b[:, 0], b[:, 1]))
                norm_sum("up")
                pe.wait_ge(vector_done, eng.at("normed up"))
                pe.sem_inc(passed[0], 1)
                with eng.turns("up", 4) as t:
                    for i in range(4):
                        b = bank[:, i].rearrange("p (c s) -> p c s", c=2)
                        product("up", (i,), hn, (b[:, 0], b[:, 1]), free=((scalar_done, f"up relu {i}", 1),))
                pe.wait_ge(vector_done, eng.at("up squared 3"))
                pe.sem_inc(passed[0], 1)
                with eng.turns("dn", 2) as t:
                    for j in range(2):
                        product("dn", tuple(range(4 * j, 4 * j + 4)), up2,
                                (bank[:, 2 * j, 0:S], bank[:, 2 * j + 1, 0:S]), parts=DN_PARTS,
                                done=f"dn out {j}", free=((vector_done, f"dn h {j} 0", 1), (vector_done, f"dn h {j} 1", 1)))

            norm_sum("final")
            for t in range(2):
                for k in range(KT):
                    pe.wait_ge(vector_done, eng.at(f"normed k final {k}"))
                    b = 2 * t + k // 4
                    turn(bank[:, b, (k % 4) * P:(k % 4 + 1) * P], hn[:, k, t * P:(t + 1) * P],
                         f"result turned {t} {k // 4}" if k % 4 == 3 else None)
            eng._close()

        @block.scalar
        def _(act):
            eng = Engine(act, scalar_done, plan, old)
            f = act.activation

            def load(dst, src, s=params_in):
                act.dma_start(dst, src).then_inc(s, 16)
                if s is params_in:
                    n_params[0] += 1

            load(const[:], dram["constants"], tables_in)
            load(rows_c[0:KT], dram["c"].rearrange("o (k p) -> (o k) p", p=P))
            for l in range(L):
                for r, name in ((R_ADA_B, "ada_b"), (R_CONV_B, "conv_b"), (R_CONV_G, "conv_norm_g"),
                                (R_CONV_NB, "conv_norm_b")):
                    src = dram[name][l].rearrange("(k p) -> k p", p=P)
                    load(rows[r:r + src.shape[0], l], src)
                load(rows[R_NORM_G:R_NORM_G + 24, l], dram["norm_g"][l].rearrange("a (k p) -> (a k) p", p=P))
                for r, src, n in ((R_DQ, dram["diff_qk_g"][l, 0:1], 4), (R_DK, dram["diff_qk_g"][l, 1:2], 4),
                                  (R_FQ, dram["fox_qk_g"][l, 0:1], 2), (R_FK, dram["fox_qk_g"][l, 1:2], 2),
                                  (R_DO, dram["diff_out_g"][l:l + 1], 2)):
                    w = P // n
                    load(rows[r:r + 1, l].rearrange("o (a b) -> o a b", a=n),
                         src.rearrange("o (a b) -> o a b", a=1).to_broadcast([1, n, w]))
                load(par_all[:, l, O_FB:O_FB + 4], dram["fox_fb"][l:l + 1].to_broadcast([P, 4]))
                load(rows_cw[0:62, l], dram["conv_w"][l].rearrange("j (t p) -> (j t) p", p=P))
                load(rows_ws[:, l], dram["gmlp_ws"][l].rearrange("h t s -> t h s"))
                bs = par_all[:, l, O_BS:O_BS + 256].rearrange("p (i t) -> p i t", i=2)
                for j in range(4):
                    load(bs[64 * (j % 2):64 * (j % 2) + 64, j // 2],
                         dram["gmlp_bs"][l, j:j + 1].to_broadcast([64, P]))
                for k, name in ((0, "gmlp_norm_g"), (1, "gmlp_norm_b")):
                    load(par_all[:, l, O_GG + k * 256:O_GG + (k + 1) * 256],
                         dram[name][l:l + 1].to_broadcast([P, 256]))
                load(par_all[:, l, O_LAM:O_LAM + 128],
                     dram["diff_lambda"][l:l + 1].rearrange("o a b -> o (a b)").to_broadcast([P, 128]))
                load(par_all[:, l, O_WF:O_WF + 32].rearrange("p (k h) -> p k h", k=KT),
                     dram["w_in"][l, :, FOX_F0:FOX_F0 + 4].rearrange("(k p) h -> p k h", p=P))
            load(rows_n2[0:16], dram["norm_mix_2"].rearrange("l (k p) -> (l k) p", p=P))
            load(rows_n2[16:32], dram["norm_mlp_2"].rearrange("l (k p) -> (l k) p", p=P))
            load(rows_n2[32:40], dram["norm_final_2"].rearrange("(k p) -> k p", p=P))

            act.wait_ge(tensor_done, eng.at("c turned"))
            f(cond[:], bank[:, 4, 0:KT], ACT.Silu).then_inc(scalar_done, eng.step("cond"))

            def norm(n, shift=None):
                if n == "f1":
                    act.wait_ge(vector_done, eng.at("layer params"))
                else:
                    act.wait_ge(vector_done, eng.at(f"h {n}"))
                f(sq[:, 0:4, :], h[:, 0:4, :], ACT.Square).then_inc(scalar_done, eng.step(f"squares a {n}"))
                act.wait_ge(tensor_done, eng.at(f"sum {n}"))
                f(rstd[:], bank[:, 4, 0:S], ACT.Ln, bias=eps, scale=1.0 / D).then_inc(scalar_done, eng.step())
                act.wait_ge(scalar_done, eng.at())
                f(rstd[:], rstd[:], ACT.Exp, scale=-0.5).then_inc(scalar_done, eng.step(f"rstd {n}"))
                if shift is not None:
                    for k in range(KT):
                        act.wait_ge(vector_done, eng.at(f"normed k {n} {k}"))
                        f(hn[:, k, :], hn[:, k, :], ACT.Identity, bias=mod[:, shift + k:shift + k + 1]) \
                            .then_inc(scalar_done, eng.step(f"normed {n}" if k == KT - 1 else f"shifted {n} {k}"))

            def ffn(s):
                with eng.turns(s + "in", PAIRS // 2):
                    for j in range(2):
                        act.wait_ge(weights_used, eng.at(f"used {s}in {2 * j}"))
                        act.wait_ge(vector_done, eng.at(f"{s} gated {j}", 1))
                        f(act_tmp[:, j], bank[:, 2 * j], ACT.Silu).then_inc(scalar_done, eng.step(f"{s} silu {j}"))
                act.wait_ge(weights_used, eng.at(f"used {s}in {2 * PAIRS - 2}"))
                act.wait_ge(vector_done, eng.at(f"{s} gated 0"))
                f(act_tmp[:, 0], bank[:, 0], ACT.Silu).then_inc(scalar_done, eng.step(f"{s} silu last"))

            def squares(name, b, j, chunk):
                act.wait_ge(weights_used, eng.at(chunk))
                f(qs[:, j], bank[:, b], ACT.Square).then_inc(scalar_done, eng.step(f"{name} squares"))

            def group_rstd(name, b, j, width, after=None):
                act.wait_ge(tensor_done, eng.at(f"{name} sum"))
                if after:
                    act.wait_ge(vector_done, eng.at(after))
                f(rr[:, j], bank[:, b], ACT.Ln, bias=eps, scale=1.0 / width).then_inc(scalar_done, eng.step())
                act.wait_ge(scalar_done, eng.at())
                f(rr[:, j], rr[:, j], ACT.Exp, scale=-0.5).then_inc(scalar_done, eng.step(f"{name} rstd"))

            def exps(hd, tile):
                st = stat[:, hd.u % 4]
                if hd.kind == "stick":
                    t = tile[:, hd.tp[0][0]]
                    act.wait_ge(tensor_done, eng.at(f"scores {hd.name} 0"))
                    if hd.tp[0][1]:
                        act.wait_ge(done_by(hd.tp[0][1]), eng.at(hd.tp[0][1]))
                    f(t, bank[:, 2 + hd.sb[0][0], 0:SCW], ACT.Abs).then_inc(scalar_done, eng.step())
                    act.wait_ge(scalar_done, eng.at())
                    f(t, t, ACT.Exp, scale=-1.0).then_inc(scalar_done, eng.step())
                    act.wait_ge(scalar_done, eng.at())
                    f(t, t, ACT.Ln, bias=ones[:, 0:1]).then_inc(scalar_done, eng.step(f"ln {hd.name}"))
                    return
                act.wait_ge(vector_done, eng.at(f"neg {hd.name}"))
                scale = 32 ** -0.5 if hd.kind == "diff" else 1.0
                n = len(hd.maps)
                for m in range(n):
                    b = 6 + (2 * m if hd.kind == "diff" else 0)
                    for j, (c0, c1) in enumerate(((0, P), (P, SCW))):
                        t = tile[:, hd.tp[m][0], c0:c1]
                        f(t, t, ACT.Exp, bias=st[:, b + j:b + j + 1], scale=scale,
                          accum_out=st[:, 10 + 2 * m + j:11 + 2 * m + j]) \
                            .then_inc(scalar_done, eng.step(f"exp {hd.name}" if m == n - 1 and j else None))

            def copies(hd, tile, tt):
                if hd.kind == "stick":
                    act.wait_ge(vector_done, eng.at(f"argm {hd.name}"))
                    if hd.ps[0][1]:
                        act.wait_ge(tensor_done, eng.at(hd.ps[0][1]))
                    f(tt[:, hd.ps[0][0]], tile[:, hd.tp[0][0]], ACT.Exp) \
                        .then_inc(scalar_done, eng.step(f"copied {hd.name} 0"))
                    return
                for m in range(len(hd.pb)):
                    act.wait_ge(tensor_done, eng.at(f"turned {hd.name} {m}"))
                    if hd.ps[m][1]:
                        act.wait_ge(tensor_done, eng.at(hd.ps[m][1]))
                    f(tt[:, hd.ps[m][0]], bank[:, 4 + hd.pb[m][0], 0:SCW], ACT.Copy) \
                        .then_inc(scalar_done, eng.step(f"copied {hd.name} {m}"))

            def attention(heads, tile, tt, filler=None):
                for i in range(len(heads) + 2):
                    if filler:
                        filler(i)
                    if i < len(heads):
                        exps(heads[i], tile)
                    if 0 <= i - 1 < len(heads):
                        copies(heads[i - 1], tile, tt)

            with eng.layers("one"):
                norm("f1", 0)
                ffn("f1")
                norm("z", 24)
                squares("dq", 0, 0, "used z 1")
                squares("dk", 1, 1, "used z 3")
                group_rstd("dq", 5, 0, 32)
                act.wait_ge(weights_used, eng.at("used z 4"))
                f(vd[:], bank[:, 2].rearrange("p (c s) -> p c s", c=2), ACT.Copy) \
                    .then_inc(scalar_done, eng.step("dv copied"))
                group_rstd("dk", 6, 1, 32)
                squares("fq", 3, 0, "used z 5")
                squares("fk", 0, 1, "used z 6")
                group_rstd("fq", 5, 0, 64, "dq scaled")
                act.wait_ge(weights_used, eng.at("used z 7"))
                f(vf[:], bank[:, 1].rearrange("p (c s) -> p c s", c=2), ACT.Copy) \
                    .then_inc(scalar_done, eng.step("fv copied"))
                group_rstd("fk", 6, 1, 64, "dk scaled")
                act.wait_ge(vector_done, eng.at("lambda sums"))
                f(small[:, 2:4], small[:, 0:2], ACT.Exp).then_inc(scalar_done, eng.step("lambda exp"))
                act.wait_ge(tensor_done, eng.at("forget sum"))
                fbc = small[:, 8:9]
                f(ft[:, 0, :], bank[:, 4, 0:S], ACT.Abs, bias=fbc).then_inc(scalar_done, eng.step())
                act.wait_ge(scalar_done, eng.at())
                f(ft[:, 0, :], ft[:, 0, :], ACT.Exp, scale=-1.0).then_inc(scalar_done, eng.step())
                act.wait_ge(scalar_done, eng.at())
                f(ft[:, 0, :], ft[:, 0, :], ACT.Ln, bias=ones[:, 0:1]).then_inc(scalar_done, eng.step("forget ln"))
                act.wait_ge(weights_used, eng.at("used z 9"))
                f(cg[:], bank[:, 3].rearrange("p (c s) -> p c s", c=2), ACT.Sigmoid) \
                    .then_inc(scalar_done, eng.step("conv gate"))
                act.wait_ge(weights_used, eng.at("used z 10"))
                f(u_[:], bank[:, 0].rearrange("p (c s) -> p c s", c=2), ACT.Gelu_apprx_tanh) \
                    .then_inc(scalar_done, eng.step("u"))
                act.wait_ge(weights_used, eng.at("used z 11"))
                f(vg[:], bank[:, 1].rearrange("p (c s) -> p c s", c=2), ACT.Gelu_apprx_tanh) \
                    .then_inc(scalar_done, eng.step("gate gelu"))
                act.wait_ge(vector_done, eng.at("gate stats"))
                f(small[:, 20:22], small[:, 16:20].rearrange("p (c b) -> p c b", c=2)[:, :, 1], ACT.Ln, bias=eps) \
                    .then_inc(scalar_done, eng.step())
                act.wait_ge(scalar_done, eng.at())
                f(small[:, 20:22], small[:, 20:22], ACT.Exp, scale=-0.5) \
                    .then_inc(scalar_done, eng.step("gate rstd"))
                attention(HEADS_ONE, tile1, turned1)
                act.wait_ge(vector_done, eng.at("heads d0 1"))
                f(qs[:, 0], od[:].rearrange("p a s -> p (a s)"), ACT.Square) \
                    .then_inc(scalar_done, eng.step("od squares"))
                group_rstd("od", 5, 0, 64)
                act.wait_ge(vector_done, eng.at("conv centred"))
                f(cg[:], cd[:], ACT.Square).then_inc(scalar_done, eng.step("conv squares"))
                act.wait_ge(tensor_done, eng.at("conv var"))
                f(rstd[:], bank[:, 1, 0:S], ACT.Ln, bias=eps, scale=1.0 / 256).then_inc(scalar_done, eng.step())
                act.wait_ge(scalar_done, eng.at())
                f(rstd[:], rstd[:], ACT.Exp, scale=-0.5).then_inc(scalar_done, eng.step("conv rstd"))
                act.wait_ge(vector_done, eng.at("conv normed"))
                for i in range(2):
                    f(mix[:, 2 + i, :], cd[:, i, :], ACT.Silu,
                      bias=par[:, R_CONV_NB + i:R_CONV_NB + i + 1],
                      scale=par[:, R_CONV_G + i:R_CONV_G + i + 1]) \
                        .then_inc(scalar_done, eng.step("conv done" if i else None))
                norm("f2", 48)
                ffn("f2")

            with eng.layers("two"):
                norm("z2")
                for i in range(18):
                    chunks = Z2_UNITS[i][1]
                    act.wait_ge(weights_used, eng.at(f"used z2 {chunks[-1]}"))
                    b = bank[:, i % 4]
                    if i in (5, 11):
                        if i == 5:
                            for a in range(2):
                                f(q2[:, 4 * i:4 * i + 4, :].rearrange("p (t a) s -> p t a s", a=2)[:, :, a],
                                  b.rearrange("p (t s) -> p t s", t=2), ACT.Identity,
                                  scale=tab("in64_eighth", 1, a)) \
                                    .then_inc(scalar_done, eng.step(f"z2 out {i}" if a else None))
                        else:
                            f(k2[:, 10:12, :], b.rearrange("p (t s) -> p t s", t=2), ACT.Copy) \
                                .then_inc(scalar_done, eng.step(f"z2 out {i}"))
                    elif i < 12:
                        j = i % 2
                        if i >= 2:
                            act.wait_ge(vector_done, eng.at(f"rotated {i - 2 if i not in (7,) else i - 3}"))
                            if i == 6:
                                act.wait_ge(vector_done, eng.at("rotated 4"))
                        f(raw[:, j], b, ACT.Copy).then_inc(scalar_done, eng.step(f"z2 out {i}"))
                    else:
                        c = 256 * (i - 12)
                        f(v2[:, :, c:c + 256], b.rearrange("p (t s) -> p t s", t=2), ACT.Copy) \
                            .then_inc(scalar_done, eng.step(f"z2 out {i}"))

                def gate_copy(i):
                    act.wait_ge(weights_used, eng.at(f"used z2 {Z2_UNITS[i][1][-1]}"))
                    c = 2 * (i - 18)
                    f(gates[:, c:c + 2, :], bank[:, i % 2].rearrange("p (t s) -> p t s", t=2), ACT.Copy) \
                        .then_inc(scalar_done, eng.step(f"z2 out {i}"))

                for g in range(2):
                    gate_copy(18 + g)
                done = [20]

                def filler(i):
                    if i and done[0] < 30:
                        gate_copy(done[0])
                        done[0] += 1

                attention(HEADS_TWO, tile2, turned2, filler)
                for i in range(4):
                    for br in range(3):
                        g = gates[:, 8 * br + 2 * i:8 * br + 2 * i + 2, :]
                        f(g, g, ACT.Sigmoid).then_inc(scalar_done, eng.step(f"gate {i}" if br == 2 else None))
                norm("up")
                with eng.turns("up", 4):
                    for i in range(4):
                        act.wait_ge(weights_used, eng.at(f"used up {i}"))
                        if i < 2:
                            act.wait_ge(vector_done, eng.at(f"up squared {i + 2}", 1))
                        else:
                            act.wait_ge(vector_done, eng.at(f"up squared {i - 2}"))
                        f(act_tmp[:, i % 2], bank[:, i], ACT.Relu).then_inc(scalar_done, eng.step(f"up relu {i}"))
            norm("final")
            for t in range(2):
                for j in range(2):
                    act.wait_ge(tensor_done, eng.at(f"result turned {t} {j}"))
                    f(sq[:, 4 * t + 2 * j:4 * t + 2 * j + 2, :].rearrange("p k s -> p (k s)"),
                      bank[:, 2 * t + j], ACT.Copy).then_inc(scalar_done, eng.step(f"result {t}" if j else None))
            eng._close()

        assert n_params[0] in (0, n_params_total), n_params

        @block.vector
        def _(dve):
            eng = Engine(dve, vector_done, plan, old)
            tt, ts, stt = dve.tensor_tensor, dve.tensor_scalar, dve.scalar_tensor_tensor

            def col(t, i):
                return t[:, i:i + 1]

            def ada_sum(j, n, half, first=False):
                dve.wait_ge(ada_in[j], half * 16 + 16)
                if not first:
                    dve.wait_ge(ada_reduced, n - 1)
                ts(ada_acc[:, j], ada[:, j, 0], col(cond, 0), None, ALU.mult).then_inc(vector_done, eng.step())
                for k in range(1, KT - 1):
                    dve.wait_ge(vector_done, eng.at())
                    stt(ada_acc[:, j], ada[:, j, k], col(cond, k), ada_acc[:, j], ALU.mult, ALU.add) \
                        .then_inc(vector_done, eng.step())
                dve.wait_ge(vector_done, eng.at())
                stt(ada_acc[:, j], ada[:, j, KT - 1], col(cond, KT - 1), ada_acc[:, j], ALU.mult, ALU.add) \
                    .then_inc(ada_summed, 1)

            for k in range(4):
                dve.wait_ge(tensor_done, eng.at(f"x turned {k}"))
                dve.tensor_copy(h[:, 2 * k:2 * k + 2, :].rearrange("p k s -> p (k s)"), bank[:, k]) \
                    .then_inc(vector_done, eng.step("x" if k == 3 else None))
            dve.wait_ge(tensor_done, eng.at("rows turned"))
            for l in range(L):
                dve.tensor_copy(par_all[:, l, 0:N_ROWS], bank[:, 5, l * P:l * P + N_ROWS])
                dve.tensor_copy(par_all[:, l, O_CW:O_CW + 62], bank[:, 5, 256 + l * 64:256 + l * 64 + 62])
                dve.memset(par_all[:, l, N_ROWS:O_CW], 0.0)
                dve.memset(par_all[:, l, O_CW + 62:O_WST], 0.0)
            dve.tensor_copy(norm2[:], bank[:, 5, 384:424]).then_inc(vector_done, eng.step("columns"))
            for l in range(L):
                dve.wait_ge(tensor_done, eng.at(f"ws turned {l}"))
                tt(par_all[:, l, O_WST:O_WST + 512].rearrange("p (h t) -> p h t", h=4),
                   bank[:, 6].rearrange("p (h t) -> p h t", h=4),
                   tab("mix_seen").rearrange("p (o t) -> p o t", o=1).to_broadcast([P, 4, P]), ALU.mult) \
                    .then_inc(vector_done, eng.step(f"mix weights {l}"))
            dve.wait_ge(scalar_done, eng.at("cond"))
            for n in range(ADA_PRE):
                ada_sum(n % 2, n, n // 2, first=n < 2)
            dve.wait_ge(ada_reduced, ADA_PRE)
            dve.wait_ge(vector_done, eng.at("columns"))
            tt(mod_first[:], bank[:, 7, 0:32].rearrange("p (l c) -> p l c", l=L), par_all[:, :, 0:16], ALU.add) \
                .then_inc(vector_done, eng.step())
            dve.wait_ge(vector_done, eng.at())

            def scale_norm(n, gains):
                tt(sq[:, 4:8, :], h[:, 4:8, :], h[:, 4:8, :], ALU.mult) \
                    .then_inc(vector_done, eng.step(f"squares b {n}"))
                dve.wait_ge(scalar_done, eng.at(f"rstd {n}"))
                for k in range(KT):
                    m = f"normed k {n} {k}"
                    stt(hn[:, k, :], h[:, k, :], gains(k), rstd[:], ALU.mult, ALU.mult) \
                        .then_inc(vector_done, eng.step(m))
                    if k == KT - 1:
                        plan.marks.setdefault(f"normed {n}", plan.marks[m])
                        if n in ("z2", "up"):
                            plan.marks[f"normed {n}"] = plan.marks[m]

            def gated_scale(dst, scale_at, gain_at):
                return stt(der[:, dst:dst + 8], mod[:, scale_at:scale_at + 8], 1.0,
                           par[:, gain_at:gain_at + 8], ALU.add, ALU.mult)

            def ffn(s, gate_at, n0, half0):
                with eng.turns(s + "in", PAIRS // 2) as t:
                    for j in range(2):
                        if n0 is not None:
                            ada_sum(j, n0 + t * 2 + j, half0 + t)
                        dve.wait_ge(scalar_done, eng.at(f"{s} silu {j}"))
                        dve.wait_ge(weights_used, eng.at(f"used {s}in {2 * j + 1}"))
                        tt(gated[:, bass.ds(t * 4 + 2 * j, 2), :].rearrange("p c s -> p (c s)"),
                           act_tmp[:, j], bank[:, 2 * j + 1], ALU.mult) \
                            .then_inc(vector_done, eng.step(f"{s} gated {j}"))
                dve.wait_ge(scalar_done, eng.at(f"{s} silu last"))
                dve.wait_ge(weights_used, eng.at(f"used {s}in {2 * PAIRS - 1}"))
                tt(gated[:, FT - 2:FT, :].rearrange("p c s -> p (c s)"), act_tmp[:, 0], bank[:, 1], ALU.mult) \
                    .then_inc(vector_done, eng.step(f"{s} gated last"))
                if n0 is not None:
                    dve.wait_ge(ada_reduced, n0 + 10)
                    tt(mod[:, 16:56], bank[:, 7, 16:56], par[:, 16:56], ALU.add).then_inc(vector_done, eng.step())
                    dve.wait_ge(vector_done, eng.at())
                ts(der[:, 24:32], mod[:, gate_at:gate_at + 8], 0.5, None, ALU.mult) \
                    .then_inc(vector_done, eng.step())
                dve.wait_ge(vector_done, eng.at())
                dve.sem_inc(passed[1], 1)
                with eng.turns(s + "out", 2) as t:
                    for j in range(2):
                        if n0 is not None:
                            ada_sum(j, n0 + t * 2 + 10 + j, half0 + t + PAIRS // 2)
                        for c in range(2):
                            if c == 0:
                                dve.wait_ge(tensor_done, eng.at(f"{s} out {j}"))
                            else:
                                dve.wait_ge(weights_used, eng.at(f"used {s}out {4 * j + 3}"))
                            k = t * 4 + 2 * j + c
                            hk = h[:, bass.ds(k, 1), :].rearrange("p o s -> p (o s)")
                            stt(hk, bank[:, 2 * j + c, 0:S], der[:, bass.ds(k + 24, 1)], hk,
                                ALU.mult, ALU.add).then_inc(vector_done, eng.step(f"{s} h {j} {c}"))

            def maxima(hd, tile):
                st = stat[:, hd.u % 4]
                if hd.kind == "stick":
                    t, sp_ = tile[:, hd.tp[0][0]], tile[:, hd.tp[1][0]]
                    if hd.tp[1][1]:
                        dve.wait_ge(tensor_done, eng.at(hd.tp[1][1]))
                    dve.wait_ge(scalar_done, eng.at(f"ln {hd.name}"))
                    stt(sp_, bank[:, 2 + hd.sb[0][0], 0:SCW], 0.0, t, ALU.max, ALU.add) \
                        .then_inc(vector_done, eng.step())
                    dve.wait_ge(vector_done, eng.at())
                    tt(sp_, sp_, tab("before", SCW), ALU.mult).then_inc(vector_done, eng.step(f"sp {hd.name}"))
                    return
                for m, (_, _, _, mask) in enumerate(hd.maps):
                    dve.wait_ge(tensor_done, eng.at(f"scores {hd.name} {m}"))
                    dve.sem_inc(passed[1], 1)
                    for j, (c0, c1) in enumerate(((0, P), (P, SCW))):
                        dve.tensor_tensor_reduce(
                            out=tile[:, hd.tp[m][0], c0:c1], in0=bank[:, 2 + hd.sb[m][0], c0:c1],
                            in1=tab(mask, c1 - c0, c0), scale=1.0, scalar=-3e38, op0=ALU.add, op1=ALU.max,
                            accum_out=st[:, 2 * m + j:2 * m + j + 1]) \
                            .then_inc(vector_done, eng.step(f"max {hd.name} {m}" if j else None))
                dve.wait_ge(vector_done, eng.at())
                if hd.kind == "diff":
                    i = ts(st[:, 6:10], st[:, 0:4], -(32 ** -0.5), None, ALU.mult)
                elif len(hd.maps) == 1:
                    i = ts(st[:, 6:8], st[:, 0:2], -1.0, None, ALU.mult)
                else:
                    i = dve.tensor_reduce(st[:, 6:8], st[:, 0:6].rearrange("p (m j) -> p j m", j=2), AX.X, ALU.max,
                                          negate=True)
                i.then_inc(vector_done, eng.step(f"neg {hd.name}"))

            def scaling(hd, tile):
                st = stat[:, hd.u % 4]
                if hd.kind == "stick":
                    dve.wait_ge(tensor_done, eng.at(f"arg {hd.name}"))
                    tt(tile[:, hd.tp[0][0]], bank[:, 4 + hd.pb[0][0], 0:SCW], tab("before_neg", SCW), ALU.add) \
                        .then_inc(vector_done, eng.step(f"argm {hd.name}"))
                    return
                dve.wait_ge(scalar_done, eng.at(f"exp {hd.name}"))
                n = len(hd.maps)
                if n == 3:
                    dve.tensor_reduce(st[:, 8:10], st[:, 10:16].rearrange("p (m j) -> p j m", j=2),
                                      AX.X, ALU.add).then_inc(vector_done, eng.step())
                    dve.wait_ge(vector_done, eng.at())
                r0, r1 = (8, 10) if n == 3 else (10, 14) if n == 2 else (10, 12)
                dve.reciprocal(st[:, r0:r1], st[:, r0:r1]).then_inc(vector_done, eng.step())
                dve.wait_ge(vector_done, eng.at())
                if hd.kind == "diff":
                    ts(st[:, 12:14], st[:, 12:14], small[:, 4:5], None, ALU.mult).then_inc(vector_done, eng.step())
                    dve.wait_ge(vector_done, eng.at())
                    for j, (c0, c1) in enumerate(((0, P), (P, SCW))):
                        a, b = (tile[:, hd.tp[m][0], c0:c1] for m in range(2))
                        ts(a, a, st[:, 10 + j:11 + j], None, ALU.mult).then_inc(vector_done, eng.step())
                        dve.wait_ge(vector_done, eng.at())
                        stt(a, b, st[:, 12 + j:13 + j], a, ALU.mult, ALU.add) \
                            .then_inc(vector_done, eng.step(f"scaled {hd.name}" if j else None))
                    return
                for m in range(n):
                    for j, (c0, c1) in enumerate(((0, P), (P, SCW))):
                        a = tile[:, hd.tp[m][0], c0:c1]
                        ts(a, a, st[:, r0 + j:r0 + j + 1], None, ALU.mult) \
                            .then_inc(vector_done, eng.step(f"scaled {hd.name}" if m == n - 1 and j else None))

            def pair_out(heads, i, dst):
                hd = heads[i]
                if hd.half == 0:
                    return
                dve.wait_ge(tensor_done, eng.at(f"out {hd.name}"))
                b = bank[:, 6 + hd.pair % 2].rearrange("p (a s) -> p a s", a=2)
                for a in range(2):
                    dve.tensor_copy(dst(hd)[64 * a:64 * a + 64], b[64 * a:64 * a + 64, a]) \
                        .then_inc(vector_done, eng.step(f"heads {heads[0].name} {hd.pair}" if a else None))

            def attention(heads, tile, dst):
                for i in range(len(heads) + 2):
                    if i < len(heads):
                        maxima(heads[i], tile)
                    if 0 <= i - 1 < len(heads):
                        scaling(heads[i - 1], tile)
                    if i >= 2:
                        pair_out(heads, i - 2, dst)

            with eng.layers("one") as layer:
                n0 = layer * ADA_REST + ADA_PRE
                half0 = layer * (ADA_REST // 2) + ADA_PRE // 2
                dve.wait_ge(vector_done, eng.at())
                dve.tensor_copy(par[:], par_all[:, bass.ds(layer, 1), :].rearrange("p o n -> p (o n)"))
                dve.tensor_copy(small[:, 6:8], const[:, bass.ds(layer * 2 + at["lam_init"], 2)])
                dve.tensor_copy(mod[:, 0:16], mod_first[:, bass.ds(layer, 1), :].rearrange("p o n -> p (o n)")) \
                    .then_inc(vector_done, eng.step("layer params"))
                dve.wait_ge(vector_done, eng.at())
                gated_scale(0, 8, R_NORM_G).then_inc(vector_done, eng.step())
                scale_norm("f1", lambda k: col(der, k))
                ffn("f1", 16, n0, half0)
                plan.marks["h z"] = plan.marks["f1 h 1 1"]
                dve.wait_ge(ada_reduced, n0 + ADA_REST)
                dve.wait_ge(vector_done, eng.at())
                tt(mod[:, 56:72], bank[:, 7, 56:72], par[:, 56:72], ALU.add).then_inc(vector_done, eng.step())
                dve.wait_ge(vector_done, eng.at())
                gated_scale(8, 32, R_NORM_G + 8).then_inc(vector_done, eng.step())
                gated_scale(16, 56, R_NORM_G + 16).then_inc(vector_done, eng.step())
                ts(der[:, 32:36], tab("in32", 4), col(par, R_DQ), None, ALU.mult).then_inc(vector_done, eng.step())
                ts(der[:, 36:38], tab("in64_eighth", 2), col(par, R_FQ), None, ALU.mult) \
                    .then_inc(vector_done, eng.step())
                ts(der[:, 38:39], col(par, R_DO), small[:, 7:8], None, ALU.mult).then_inc(vector_done, eng.step())
                tt(small[:, 40:44], tab("in32", 4), par[:, O_FB:O_FB + 4], ALU.mult) \
                    .then_inc(vector_done, eng.step())
                dve.wait_ge(vector_done, eng.at())
                dve.tensor_reduce(small[:, 8:9], small[:, 40:44], AX.X, ALU.add).then_inc(vector_done, eng.step())
                lam = par[:, O_LAM:O_LAM + 128].rearrange("p (a b c) -> p a b c", a=2, b=2)
                tt(ft[:, 2, 0:64].rearrange("p (a c) -> p a c", a=2), lam[:, :, 0], lam[:, :, 1], ALU.mult) \
                    .then_inc(vector_done, eng.step())
                dve.wait_ge(vector_done, eng.at())
                dve.tensor_reduce(small[:, 0:2], ft[:, 2, 0:64].rearrange("p (a c) -> p a c", a=2), AX.X, ALU.add) \
                    .then_inc(vector_done, eng.step("lambda sums"))
                scale_norm("z", lambda k: col(der, 8 + k))
                dve.tensor_copy(
                    wfx.rearrange("p k (h r) -> p (k h) r", h=4),
                    par[:, O_WF:O_WF + 32].rearrange("p (k o) -> p k o", o=1).to_broadcast([P, 32, 32])) \
                    .then_inc(vector_done, eng.step("forget weights"))

                def scale_q(name, b, j, dst, gain, maps):
                    dve.wait_ge(scalar_done, eng.at(f"{name} rstd"))
                    for i in range(2):
                        for m in range(maps):
                            stt(dst[:, maps * i + m, :], bank[:, b, i * S:(i + 1) * S], gain(m),
                                rr[:, j, i * S:(i + 1) * S], ALU.mult, ALU.mult) \
                                .then_inc(vector_done, eng.step(f"{name} scaled" if i and m == maps - 1 else None))

                scale_q("dq", 0, 0, qd, lambda m: col(der, 32 + m), 4)
                scale_q("dk", 1, 1, kd, lambda m: col(par, R_DK), 1)
                scale_q("fq", 3, 0, qf, lambda m: col(der, 36 + m), 2)
                scale_q("fk", 0, 1, kf, lambda m: col(par, R_FK), 1)
                dve.wait_ge(scalar_done, eng.at("lambda exp"))
                tt(small[:, 4:5], small[:, 3:4], small[:, 2:3], ALU.subtract).then_inc(vector_done, eng.step())
                dve.wait_ge(vector_done, eng.at())
                tt(small[:, 4:5], small[:, 4:5], small[:, 6:7], ALU.subtract).then_inc(vector_done, eng.step())
                dve.wait_ge(vector_done, eng.at())
                dve.wait_ge(scalar_done, eng.at("forget ln"))
                ts(ft[:, 1, :], bank[:, 4, 0:S], col(small, 8), 0.0, ALU.add, ALU.min) \
                    .then_inc(vector_done, eng.step())
                dve.wait_ge(vector_done, eng.at())
                tt(ft[:, 1, :], ft[:, 1, :], ft[:, 0, :], ALU.subtract).then_inc(vector_done, eng.step())
                dve.wait_ge(vector_done, eng.at())
                dve.tensor_tensor_scan(ft[:, 2, :], ones[:, 0:1].to_broadcast([P, S]), ft[:, 1, :], 0.0,
                                         ALU.mult, ALU.add).then_inc(vector_done, eng.step())
                dve.wait_ge(vector_done, eng.at())
                for m in range(4):
                    ts(fa[:, m, :], ft[:, 2, :], tab("cum_row", 1, m), tab("one_row", 1, m), ALU.mult, ALU.add) \
                        .then_inc(vector_done, eng.step())
                ts(fb[:], ft[:, 2, :], tab("neg_cum_rows", 1), tab("one_rows", 1), ALU.mult, ALU.add) \
                    .then_inc(vector_done, eng.step("forget rows"))
                dve.wait_ge(scalar_done, eng.at("conv gate"))
                dve.wait_ge(weights_used, eng.at("used z 8"))
                tt(yp[:, :, CONV_K - 1:CONV_K - 1 + S], bank[:, 2].rearrange("p (c s) -> p c s", c=2), cg[:],
                   ALU.mult).then_inc(vector_done, eng.step("conv in"))
                dve.wait_ge(scalar_done, eng.at("gate gelu"))
                for c in range(2):
                    dve.bn_stats(small[:, 24 + 6 * c:30 + 6 * c], vg[:, c, :]).then_inc(vector_done, eng.step())
                dve.wait_ge(vector_done, eng.at())
                dve.sem_inc(passed[1], 1)
                for c in range(2):
                    dve.bn_aggr(small[:, 16 + 2 * c:18 + 2 * c], small[:, 24 + 6 * c:30 + 6 * c]) \
                        .then_inc(vector_done, eng.step("gate stats" if c else None))
                dve.wait_ge(scalar_done, eng.at("gate rstd"))
                for c in range(2):
                    ts(vg[:, c, :], vg[:, c, :], small[:, 16 + 2 * c:17 + 2 * c], small[:, 20 + c:21 + c],
                       ALU.subtract, ALU.mult).then_inc(vector_done, eng.step())
                dve.wait_ge(vector_done, eng.at())
                gain = par[:, O_GG:O_GG + 512].rearrange("p (k s) -> p k s", k=2)
                for k, op in ((0, ALU.mult), (1, ALU.add)):
                    i = tt(vg[:], vg[:], gain[:, k:k + 1].to_broadcast([P, 2, 256]), op)
                    i.then_inc(vector_done, eng.step("gate normed" if k else None))
                    if not k:
                        dve.wait_ge(vector_done, eng.at())
                for j in range(4):
                    dve.wait_ge(tensor_done, eng.at(f"mixed {j // 2}"))
                    r = slice(64 * (j % 2), 64 * (j % 2) + 64)
                    dst = mix[r, 4 + j // 2, :].rearrange("p (c t) -> p c t", c=2)
                    b = bank[:, j // 2].rearrange("p (a c s) -> p a c s", a=2, c=2)[r, j % 2]
                    bias = par[r, O_BS + (j // 2) * P:O_BS + (j // 2 + 1) * P].rearrange("p (o t) -> p o t", o=1)
                    tt(dst, b, bias.to_broadcast([64, 2, P]), ALU.add).then_inc(vector_done, eng.step())
                    dve.wait_ge(vector_done, eng.at())
                    tt(dst, dst, u_[r, j // 2, :].rearrange("p (c t) -> p c t", c=2), ALU.mult) \
                        .then_inc(vector_done, eng.step("mixed out" if j == 3 else None))
                attention(HEADS_ONE, tile1,
                          lambda hd: od[:, hd.out_tile, :] if hd.kind == "diff" else mix[:, 6 + hd.out_tile, :])
                dve.wait_ge(pool_done, eng.at("conv pad"))
                for j in range(CONV_K):
                    for i in range(2):
                        w = col(par, O_CW + 2 * j + i)
                        src = yp[:, i, j:j + S]
                        if j == 0:
                            ins = ts(cv[:, i, :], src, w, col(par, R_CONV_B + i), ALU.mult, ALU.add)
                        else:
                            if i == 0:
                                dve.wait_ge(vector_done, eng.at())
                            ins = stt(cv[:, i, :], src, w, cv[:, i, :], ALU.mult, ALU.add)
                        ins.then_inc(vector_done, eng.step("conv out" if j == CONV_K - 1 and i else None))
                dve.wait_ge(scalar_done, eng.at("od rstd"))
                for i in range(2):
                    stt(mix[:, i, :], od[:, i, :], col(der, 38), rr[:, 0, i * S:(i + 1) * S], ALU.mult, ALU.mult) \
                        .then_inc(vector_done, eng.step("od normed" if i else None))
                dve.wait_ge(tensor_done, eng.at("conv mean"))
                for i in range(2):
                    stt(cd[:, i, :], bank[:, 0, 0:S], -1.0 / 256, cv[:, i, :], ALU.mult, ALU.add) \
                        .then_inc(vector_done, eng.step("conv centred" if i else None))
                dve.wait_ge(scalar_done, eng.at("conv rstd"))
                for i in range(2):
                    tt(cd[:, i, :], cd[:, i, :], rstd[:], ALU.mult) \
                        .then_inc(vector_done, eng.step("conv normed" if i else None))
                for i in range(4):
                    dve.wait_ge(weights_used, eng.at(f"used o {i}"))
                    for c in range(2):
                        k = 2 * i + c
                        stt(h[:, k, :], bank[:, i, c * S:(c + 1) * S], col(mod, 40 + k), h[:, k, :],
                            ALU.mult, ALU.add).then_inc(vector_done, eng.step("h f2" if k == 7 else None))
                dve.wait_ge(vector_done, eng.at())
                scale_norm("f2", lambda k: col(der, 16 + k))
                ffn("f2", 64, None, None)

            with eng.layers("two") as layer:
                dve.wait_ge(vector_done, eng.at())
                dve.tensor_copy(der[:, 0:8], norm2[:, bass.ds(layer * 8, 8)])
                dve.tensor_copy(der[:, 8:16], norm2[:, bass.ds(layer * 8 + 16, 8)]) \
                    .then_inc(vector_done, eng.step("h z2"))
                dve.wait_ge(vector_done, eng.at())
                scale_norm("z2", lambda k: col(der, k))
                cosb = tab("cos", S).rearrange("p (o s) -> p o s", o=1).to_broadcast([P, 2, S])
                sinb = tab("sin", S).rearrange("p (o s) -> p o s", o=1).to_broadcast([P, 2, S])
                for i in [x for x in range(12) if x not in (5, 11)]:
                    dve.wait_ge(tensor_done, eng.at(f"rotary {i}"))
                    a = rot_tmp[:, 0].rearrange("p (c s) -> p c s", c=2)
                    b = rot_tmp[:, 1].rearrange("p (c s) -> p c s", c=2)
                    src = raw[:, i % 2].rearrange("p (c s) -> p c s", c=2)
                    rot = bank[:, 5 + i % 2].rearrange("p (c s) -> p c s", c=2)
                    half = i % 6 == 4
                    n = 1 if half else 2
                    tt(a[:, 0:n], rot[:, 0:n], sinb[:, 0:n], ALU.mult).then_inc(vector_done, eng.step())
                    tt(b[:, 0:n], src[:, 0:n], cosb[:, 0:n], ALU.mult).then_inc(vector_done, eng.step())
                    dve.wait_ge(vector_done, eng.at())
                    if i < 6:
                        tt(a[:, 0:n], a[:, 0:n], b[:, 0:n], ALU.add).then_inc(vector_done, eng.step())
                        if half:
                            dve.tensor_copy(a[:, 1], src[:, 1]).then_inc(vector_done, eng.step())
                        dve.wait_ge(vector_done, eng.at())
                        dst = q2[:, 4 * i:4 * i + 4, :].rearrange("p (t a) s -> p t a s", a=2)
                        for m in range(2):
                            ts(dst[:, :, m], a, tab("in64_eighth", 1, m), None, ALU.mult) \
                                .then_inc(vector_done, eng.step(f"rotated {i}" if m else None))
                    else:
                        k0 = 2 * (i - 6)
                        if half:
                            dve.tensor_copy(k2[:, k0 + 1, :], src[:, 1]).then_inc(vector_done, eng.step())
                        tt(k2[:, k0:k0 + n, :], a[:, 0:n], b[:, 0:n], ALU.add) \
                            .then_inc(vector_done, eng.step(f"rotated {i}"))
                    dve.wait_ge(vector_done, eng.at())
                attention(HEADS_TWO, tile2, lambda hd: o2[:, hd.out_tile, :])
                for i in range(4):
                    dve.wait_ge(weights_used, eng.at(f"used y {i}"))
                    dve.wait_ge(scalar_done, eng.at(f"gate {i}"))
                    dst = merged[:, 2 * i:2 * i + 2, :]
                    t = act_tmp[:, 0].rearrange("p (c s) -> p c s", c=2)
                    for br in range(3):
                        b = bank[:, 3 * (i % 2) + br].rearrange("p (c s) -> p c s", c=2)
                        g = gates[:, 8 * br + 2 * i:8 * br + 2 * i + 2, :]
                        tt(t if br else dst, b, g, ALU.mult).then_inc(vector_done, eng.step())
                        dve.wait_ge(vector_done, eng.at())
                        if br:
                            tt(dst, dst, t, ALU.add) \
                                .then_inc(vector_done, eng.step(f"merged {i}" if br == 2 else None))
                            dve.wait_ge(vector_done, eng.at())
                for i in range(4):
                    dve.wait_ge(weights_used, eng.at(f"used wo {i}"))
                    hk = h[:, 2 * i:2 * i + 2, :].rearrange("p k s -> p (k s)")
                    tt(hk, bank[:, i], hk, ALU.add).then_inc(vector_done, eng.step("h up" if i == 3 else None))
                dve.wait_ge(vector_done, eng.at())
                scale_norm("up", lambda k: col(der, 8 + k))
                with eng.turns("up", 4) as t:
                    for i in range(4):
                        dve.wait_ge(scalar_done, eng.at(f"up relu {i}"))
                        tt(up2[:, bass.ds(t * 8 + 2 * i, 2), :].rearrange("p c s -> p (c s)"),
                           act_tmp[:, i % 2], act_tmp[:, i % 2], ALU.mult) \
                            .then_inc(vector_done, eng.step(f"up squared {i}"))
                with eng.turns("dn", 2) as t:
                    for j in range(2):
                        for c in range(2):
                            if c == 0:
                                dve.wait_ge(tensor_done, eng.at(f"dn out {j}"))
                            else:
                                dve.wait_ge(weights_used, eng.at(f"used dn {4 * j + 3}"))
                            hk = h[:, bass.ds(t * 4 + 2 * j + c, 1), :].rearrange("p o s -> p (o s)")
                            tt(hk, bank[:, 2 * j + c, 0:S], hk, ALU.add) \
                                .then_inc(vector_done, eng.step(f"dn h {j} {c}"))
            plan.marks["h final"] = plan.marks["dn h 1 1"]
            dve.wait_ge(vector_done, eng.at())
            scale_norm("final", lambda k: col(norm2, 32 + k))
            eng._close()
    return plan


def kernel(**inputs):
    import concourse.bacc as bacc
    from concourse.bass_utils import run_bass_kernel_spmd

    table, at = constant_tables()
    arrays = {name: np.ascontiguousarray(inputs[name]) for name in IN_NAMES}
    arrays["constants"] = table

    def program(old):
        nc = bacc.Bacc("TRN2", target_bir_lowering=False, num_devices=1)
        dram = {n: nc.dram_tensor(f"in_{n}", a.shape, mybir.dt.from_np(a.dtype), kind="ExternalInput").ap()
                for n, a in arrays.items()}
        out = nc.dram_tensor("out_0", (1, S, D), F32, kind="ExternalOutput").ap()
        return nc, build(nc, dram, out, at, old)

    _, counted = program(Plan())
    nc, _ = program(counted)
    r = run_bass_kernel_spmd(nc, [{f"in_{n}": a for n, a in arrays.items()}], core_ids=[0])
    return r.results[0]["out_0"]
```

```python
from contextlib import ExitStack, contextmanager
import math

import numpy as np
import concourse.bass as bass
from concourse import mybir

F32 = mybir.dt.float32
F32R = mybir.dt.float32r
ALU = mybir.AluOpType
ACT = mybir.ActivationFunctionType
AX = mybir.AxisListType

P = 128
D = 1024
S = 256
L = 2
KT = D // P
D_FF = ((8 * D // 3 + 127) // 128) * 128
FT = D_FF // P
PAIRS = D_FF // 256
D_FF_2 = 4 * D
EPS = 1e-6
NEG = -1e30
MOD_TILES = 9 * KT
ADA_COLS = 512
ADA_CHUNKS = 9 * D // ADA_COLS
ADA_FIRST = 2 * D // ADA_COLS
RING = 4
SCW = 384
CONV_K = 31
MIXW2 = 24 * 64

R_ADA_B, R_NORM_G, R_CONV_B, R_CONV_G, R_CONV_NB = 0, 72, 96, 98, 100
R_DQ, R_DK, R_FQ, R_FK, R_DO = 102, 103, 104, 105, 106
N_ROWS = 107
O_CW = 128
O_WST = O_CW + 64
O_BS = O_WST + 512
O_GG = O_BS + 256
O_LAM = O_GG + 512
O_WF = O_LAM + 128
O_FB = O_WF + 32
N_PAR = O_FB + 4


def constant_tables():
    at, parts = {}, []

    def put(name, a):
        at[name] = sum(p.shape[1] for p in parts)
        parts.append(np.asarray(a, np.float32).reshape(P, -1))

    r = np.arange(P)
    put("ident", np.eye(P))
    put("ones", np.ones((P, P)))
    put("group32", r[:, None] // 32 == r[None, :] // 32)
    put("group64", r[:, None] // 64 == r[None, :] // 64)
    rot = np.zeros((P, P))
    for base in (0, 64):
        for j in range(8):
            rot[base + 8 + j, base + j] = -1
            rot[base + j, base + 8 + j] = 1
    put("rotate", rot)
    put("neg_suffix", -(r[:, None] >= r[None, :]).astype(np.float32))
    put("neg_ones", -np.ones((P, P)))
    freq = np.exp(-math.log(500000.0) * np.arange(0, 16, 2, dtype=np.float32) / np.float32(16)).astype(np.float32)
    ang = (np.arange(S, dtype=np.float32)[None, :] * freq[:, None]).astype(np.float32).astype(np.float64)
    cos, sin = np.ones((P, S)), np.zeros((P, S))
    for base in (0, 64):
        for half in (0, 8):
            cos[base + half:base + half + 8] = np.cos(ang)
            sin[base + half:base + half + 8] = np.sin(ang)
    put("cos", cos)
    put("sin", sin)

    def by_query(seen):
        m = seen(np.arange(S)[:, None] - np.arange(S)[None, :])
        m = np.where(m, 0.0, NEG)
        return np.concatenate([m[:P, :P], m[P:, :]], axis=1)

    put("causal", by_query(lambda d: d >= 0))
    put("window0", by_query(lambda d: (d >= 0) & (d <= 128)))
    put("window1", by_query(lambda d: (d >= 0) & (d % 4 == 0)))
    put("window2", by_query(lambda d: (d >= 0) & (d % 16 == 0)))
    k, q = np.arange(S)[:, None], np.arange(S)[None, :]
    before = (k < q).astype(np.float32)
    before = np.concatenate([before[:P, :], before[P:, P:]], axis=1)
    put("before", before)
    put("before_neg", np.where(before > 0, 0.0, NEG))
    put("mix_seen", r[:, None] <= r[None, :])
    put("in32", r[:, None] // 32 == np.arange(4)[None, :])
    put("in64", r[:, None] // 64 == np.arange(2)[None, :])
    put("in64_eighth", (r[:, None] // 64 == np.arange(2)[None, :]) * 0.125)
    put("cum_row", r[:, None] == 32 * np.arange(4)[None, :])
    put("one_row", r[:, None] == 32 * np.arange(4)[None, :] + 1)
    put("neg_cum_rows", -(r[:, None] % 32 == 1).astype(np.float32))
    put("one_rows", r[:, None] % 32 == 0)
    put("eps", np.full((P, 1), EPS))
    init = [0.8 - 0.6 * math.exp(-0.3 * l) for l in range(L)]
    put("lam_init", np.tile([[x, 1 - x] for x in init], (P, 1, 1)).reshape(P, 2 * L))
    table = np.concatenate(parts, axis=1)
    return np.ascontiguousarray(table), at


class Plan:

    def __init__(self):
        self.totals, self.bodies, self.marks = {}, {}, {}


PARTS = ("pre", "one", "two", "post")
TIMES = {"pre": 1, "one": L, "two": L, "post": 1}


class Engine:

    def __init__(self, e, own, plan, old):
        self.e, self.own, self.plan, self.old = e, own, plan, old
        self.part, self.layer = "pre", None
        self.loop, self.turn = None, None
        self.count = {}

    @contextmanager
    def layers(self, part):
        self._close()
        self.part, self.count = part, {}
        with self.e.Fori(0, L) as layer:
            self.layer = layer
            yield layer
            self._close()
        self.layer = None
        self.part, self.count = PARTS[PARTS.index(part) + 1], {}

    def _close(self):
        for k, v in self.count.items():
            self.plan.totals[k, self.part] = v

    def step(self, mark=None, sem=None, by=1):
        s = sem or self.own
        k = s.name
        self.count[k] = self.count.get(k, 0) + by
        if mark:
            self.plan.marks[mark] = (s, self.part, self.count[k], self.loop)
        return by

    def _value(self, s, part, local, loop, back=0):
        old, k = self.old, s.name
        value = sum(old.totals.get((k, q), 0) * TIMES[q] for q in PARTS[:PARTS.index(part)]) + local
        least = value
        if TIMES[part] > 1:
            total = old.totals.get((k, part), 0)
            value = value + (self.layer * total if part == self.part else (L - 1) * total)
        if loop:
            body = old.bodies.get((k, part, loop), 0)
            if loop == self.loop:
                value = value + self.turn * body
                least -= back * body
                if back:
                    value = value - back * body
            else:
                value = value + (old.bodies.get(loop, 1) - 1 - back) * body
        if not old.totals:
            return 1
        assert least > 0, (k, part, local, loop)
        return value

    def _count(self, phase, n, per_layer, before, per_turn):
        n = n + (before if phase in TWO else 0)
        if self.layer is not None:
            n = self.layer * per_layer + n
        return n if self.loop is None else self.turn * per_turn + n

    def split_chunk(self, phase, i):
        return self._count(phase, SPLIT_START[phase] + i, SPLIT_CHUNKS["one" if phase in ONE else "two"],
                           L * SPLIT_CHUNKS["one"], PER_TURN.get(self.loop))

    def freed(self, phase, i, before=False):
        return self._count(phase, (START[phase] + i) // RING + (1 if before else 2),
                           CHUNKS["one" if phase in ONE else "two"] // RING, L * CHUNKS["one"] // RING,
                           PER_TURN.get(self.loop, 0) // RING)

    def arrived(self, phase, i):
        n = START[phase] + i
        y = 2 if phase in TWO else 0
        loads = n // RING + 1 + (y if phase in TWO and n >= START["y"] else 0)
        return self._count(phase, 16 * loads, 16 * (CHUNKS["one" if phase in ONE else "two"] // RING + y),
                           16 * (L * CHUNKS["one"] // RING), 16 * PER_TURN.get(self.loop, 0) // RING)

    def at(self, mark=None, back=0):
        if mark is None:
            return self._value(self.own, self.part, self.count.get(self.own.name, 0), self.loop)
        if not self.old.marks:
            return 1
        s, part, local, loop = self.old.marks[mark]
        return self._value(s, part, local, loop, back)

    @contextmanager
    def turns(self, name, n):
        start = dict(self.count)
        with self.e.Fori(0, n) as turn:
            self.loop, self.turn = name, turn
            yield turn
        for k, v in list(self.count.items()):
            body = v - start.get(k, 0)
            self.plan.bodies[k, self.part, name] = body
            self.count[k] = v + (n - 1) * body
        self.plan.bodies[name] = max(n, self.plan.bodies.get(name, 0))
        self.loop = self.turn = None


ONE = {"f1in": 2 * PAIRS, "f1out": 16, "z": 12, "o": 4, "f2in": 2 * PAIRS, "f2out": 16}
TWO = {"z2": 32, "y": 4, "wo": 4, "up": 16, "dn": 16}
CHUNKS = {"one": sum(ONE.values()), "two": sum(TWO.values())}
assert CHUNKS["one"] % RING == 0 and CHUNKS["two"] % RING == 0
START = {}
for _phases in (ONE, TWO):
    _at = 0
    for _name, _n in _phases.items():
        START[_name] = _at
        _at += _n
FF_PARTS = ((0, 6), (6, 6), (12, 5), (17, 5))
DN_PARTS = ((0, 8), (8, 8), (16, 8), (24, 8))
assert sum(n for _, n in FF_PARTS) == FT

SPLIT_START = {"f1in": 0, "z": ONE["f1in"], "f2in": ONE["f1in"] + ONE["z"], "z2": 0, "up": TWO["z2"]}
SPLIT_CHUNKS = {"one": 2 * ONE["f1in"] + ONE["z"], "two": TWO["z2"] + TWO["up"]}
PER_TURN = {"f1in": 4, "f1out": 8, "f2in": 4, "f2out": 8, "up": 4, "dn": 8}

Z_UNITS = (("dq", (0, 1), 0, False), ("dk", (2, 3), 256, False), ("dv", (4,), 512, True),
           ("fq", (5,), 1792, False), ("fk", (6,), 2048, False), ("fv", (7,), 2304, True),
           ("ca", (8,), 768, False), ("cg", (9,), 1024, False), ("gu", (10,), 1280, False),
           ("gv", (11,), 1536, True))
FOX_F0 = 2560
Z2_UNITS = tuple((f"{'qkvgg'[i // 6]}{i if i >= 18 else i % 6}", (2 * i, 2 * i + 1) if i < 2 else (i + 2,),
                  256 * i, 12 <= i < 18) for i in range(30))


def slot_of(phase, i):
    return (START[phase] + i) % RING


def split_slot(phase, i):
    return (SPLIT_START[phase] + i) % 2


def k_tiles(phase, i):
    return 4 if phase[0] == "z" and i < 4 else 8


class Head:

    def __init__(self, name, kind, maps, out_tile, half):
        self.name, self.kind, self.maps, self.out_tile, self.half = name, kind, maps, out_tile, half


HEADS_ONE = [Head(f"d{h}", "diff", [(4 * (h // 2) + 2 * (h % 2) + c, h // 2, h // 2, "causal") for c in range(2)],
                  h // 2, h % 2) for h in range(4)]
HEADS_ONE += [Head(f"x{h}", "fox", [(h, h // 2, h // 2, "causal")], h // 2, h % 2) for h in range(4)]
HEADS_TWO = [Head(f"a{j}", "soft", [(4 * g + j, (4 * g + j) // 2, (4 * g + j) // 2, f"window{g}") for g in range(3)],
                  j // 2, j % 2) for j in range(4)]
HEADS_TWO += [Head(f"b{j}", "soft", [(12 + j, (12 + j) // 2, (12 + j) // 2, "causal")], 2 + j // 2, j % 2)
              for j in range(6)]
HEADS_TWO += [Head(f"c{j}", "stick", [(18 + j, (18 + j) // 2, (18 + j) // 2, None)], 5 + j // 2, j % 2)
              for j in range(6)]
ARENA = 20480 + 2 * 6 * SCW
SLOTS = 6


def place_heads(heads):
    n = {"sb": 0, "tp": 0, "pb": 0, "ps": 0}
    last = {}

    def take(kind, size, frees):
        i = n[kind] % size
        n[kind] += 1
        before = last.get((kind, i))
        last[kind, i] = frees
        return i, before

    for u, h in enumerate(heads):
        h.u, h.pair = u, u // 2
        if h.kind == "stick":
            h.sb = [take("sb", 2, f"sp {h.name}")]
            h.tp = [take("tp", SLOTS, f"copied {h.name} 0"), take("tp", SLOTS, f"arg {h.name}")]
            h.pb = [take("pb", 2, f"argm {h.name}")]
            h.ps = [take("ps", SLOTS, f"out {h.name}")]
        else:
            turned = 1 if h.kind == "diff" else len(h.maps)
            h.sb = [take("sb", 2, f"max {h.name} {m}") for m in range(len(h.maps))]
            h.tp = [take("tp", SLOTS, f"turned {h.name} {min(m, turned - 1)}") for m in range(len(h.maps))]
            h.pb = [take("pb", 2, f"copied {h.name} {m}") for m in range(turned)]
            h.ps = [take("ps", SLOTS, f"out {h.name}") for m in range(turned)]
    return heads


place_heads(HEADS_ONE)
place_heads(HEADS_TWO)

IN_NAMES = ["x", "c", "ada_w", "ada_b", "norm_g", "ffn1_w_in", "ffn1_w_out", "ffn2_w_in", "ffn2_w_out", "w_in",
            "w_out", "diff_qk_g", "diff_lambda", "diff_out_g", "conv_w", "conv_b", "conv_norm_g", "conv_norm_b",
            "gmlp_norm_g", "gmlp_norm_b", "gmlp_ws", "gmlp_bs", "fox_qk_g", "fox_fb", "norm_mix_2", "w_in_2",
            "w_out_a_2", "w_out_b_2", "w_out_c_2", "w_o_2", "norm_mlp_2", "w_up_2", "w_down_2", "norm_final_2"]


def build(nc, dram, out, at, old):
    plan = Plan()
    with ExitStack() as ctx:
        def sb(name, *shape, dtype=F32):
            return ctx.enter_context(nc.sbuf_tensor(name, [P, *shape], dtype))

        def sem(name):
            return ctx.enter_context(nc.semaphore(name))

        bank = ctx.enter_context(nc.psum_tensor("bank", [P, 8, 512], F32))
        ring = sb("ring", RING, 8, 256)
        w_hi, w_lo = sb("w_hi", 2, 8, 256, dtype=F32R), sb("w_lo", 2, 8, 256, dtype=F32R)
        h = sb("h", KT, S)
        hn, hn_lo = sb("hn", KT, S, dtype=F32R), sb("hn_lo", KT, S, dtype=F32R)
        normed = sb("normed", 2, S)
        square_sum = sb("square_sum", S)
        rstd = sb("rstd", S)
        n_const = dram["constants"].shape[1]
        const = sb("const", n_const)
        mod_first = sb("mod_first", L, 16)
        mod = sb("mod", MOD_TILES)
        der = sb("der", 64)
        cond = sb("cond", KT)
        norm2 = sb("norm2", 40)
        stat = sb("stat", 4, 16)
        small = sb("small", 64)
        arena = sb("arena", ARENA)

        def view(start, *dims):
            n = int(np.prod(dims))
            assert start + n <= ARENA
            v = arena[:, start:start + n]
            names = " ".join(f"d{i}" for i in range(len(dims)))
            if len(dims) == 1:
                return v
            return v.rearrange(f"p ({names}) -> p {names}", **{f"d{i}": d for i, d in enumerate(dims[1:], 1)})

        act_tmp = view(ARENA - 1024, 2, 512)
        ada_acc = view(ARENA - 2048, 2, ADA_COLS)
        wfx = view(ARENA - 2048, KT, P)
        par_at = ARENA - 2048 - L * N_PAR
        par_all = view(par_at, L, N_PAR)
        par = par_all[:, 0]
        ada = view(0, 2, 8, ADA_COLS)
        gated = view(8192, FT, S)
        x_rows = view(8192 + 2048, 2, D)
        tile1, turned1 = view(0, SLOTS, SCW), view(SLOTS * SCW, SLOTS, SCW)
        o = 2 * SLOTS * SCW
        place = {}
        for name, dims in (("qd", (8, S)), ("kd", (2, S)), ("vd", (2, S)), ("qf", (4, S)), ("kf", (2, S)),
                           ("vf", (2, S)), ("mix", (8, S)), ("fa", (4, S)), ("fb", (S,)), ("yp", (2, 288)), ("cv", (2, S)),
                           ("u", (2, S)), ("vg", (2, S)), ("ft", (3, S)), ("od", (2, S)),
                           ("cg", (2, S)), ("cd", (2, S)), ("qs", (2, 2 * S)), ("rr", (2, 2 * S))):
            place[name] = view(o, *dims)
            o += int(np.prod(dims))
        assert o <= par_at, o
        qd, kd, vd, qf, kf, vf, mix, fa, fb, yp, cv, u_, vg, ft, od, cg, cd, qs, rr = place.values()
        rows = view(8192, L, P)
        rows_cw = view(8192 + 256, L, P)
        rows_ws = view(8192 + 512, L, 4, P)
        rows_n2 = view(8192 + 1536, P)
        rows_c = view(8192 + 1664, P)
        q2 = view(0, 24, S)
        k2 = view(6144, 12, S)
        v2 = view(9216, 2, MIXW2)
        gates = view(12288, 24, S)
        o2 = view(18432, KT, S)
        merged = view(9216, KT, S)
        up2 = view(0, 32, S)
        tile2, turned2 = view(20480, SLOTS, SCW), view(20480 + SLOTS * SCW, SLOTS, SCW)
        raw, rot_tmp = view(20480, 2, 2 * S), view(20480 + 4 * S, 2, 2 * S)
        result, result_rows = view(0, KT, S), view(KT * S, 2, D)

        def tab(name, n=P, off=0):
            return const[:, at[name] + off:at[name] + off + n]

        ident, ones = tab("ident"), tab("ones")
        eps = tab("eps", 1)

        tensor_done, scalar_done = sem("tensor_done"), sem("scalar_done")
        vector_done, pool_done = sem("vector_done"), sem("pool_done")
        weights_used = sem("weights_used")
        weights_rounded, weights_split = sem("weights_rounded"), sem("weights_split")
        weights_free = [sem(f"weights_free_{i}") for i in range(RING)]
        weights_in = [sem(f"weights_in_{i}") for i in range(RING)]
        ada_in = [sem("ada_in_0"), sem("ada_in_1")]
        first_ada_in = [sem("first_ada_in_0"), sem("first_ada_in_1")]
        ada_summed, ada_reduced = sem("ada_summed"), sem("ada_reduced")
        x_in, params_in, tables_in, stored = sem("x_in"), sem("params_in"), sem("tables_in"), sem("stored")

        passed = [sem("tensor_passed"), sem("vector_passed")]

        def done_by(mark):
            return {"turned": tensor_done, "arg": tensor_done, "out": tensor_done, "copied": scalar_done,
                    "max": vector_done, "sp": vector_done, "argm": vector_done}[mark.split()[0]]

        block = ctx.enter_context(nc.Block())

        ADA_PRE = L * ADA_FIRST
        ADA_REST = ADA_CHUNKS - ADA_FIRST
        n_params = [0]
        n_params_total = 1 + L * (4 + 1 + 5 + 1 + 1 + 1 + 4 + 2 + 1 + 1) + 3

        @block.sync
        def _(sp):
            eng = Engine(sp, weights_used, plan, old)
            sp.dma_start(x_rows,
                         dram["x"][0].rearrange("(t p) d -> p t d", p=P)).then_inc(x_in, 16)

            def ada_fill(n, j, layer, first_col):
                sp.wait_ge(ada_summed, n - 1)
                sp.dma_start(ada[:, j], dram["ada_w"][bass.ds(layer, 1), :, bass.ds(first_col, ADA_COLS)]
                             .rearrange("o (k p) n -> p (o k) n", p=P)).then_inc(ada_in[j], 16)

            def fill(phase, i, nk, *sources):
                s = slot_of(phase, i)
                sp.wait_ge(weights_free[s], eng.freed(phase, i, before=True))
                k = 0
                for src in sources:
                    n = src.shape[1]
                    assert k + n <= nk
                    sp.dma_start(ring[:, s, k:k + n, :], src).then_inc(weights_in[s], 16)
                    k += n

            def chunk(w, layer, k0, nk, col):
                return w[bass.ds(layer, 1), k0 * P:(k0 + nk) * P, col].rearrange("o (k p) n -> p (o k) n", p=P)

            def ffn(s, w_in, w_out, layer, n0):
                with eng.turns(s + "in", PAIRS // 2) as t:
                    for i in range(4):
                        if n0 is not None and i % 2 == 0:
                            ada_fill(n0 + t * 2 + i // 2, i // 2, layer,
                                     t * (2 * ADA_COLS) + (ADA_FIRST + i // 2) * ADA_COLS)
                        fill(s + "in", i, 8,
                             chunk(w_in, layer, 0, 8, bass.ds(t * 512 + (i // 2) * 256 + (i % 2) * D_FF, 256)))
                for i in (2 * PAIRS - 2, 2 * PAIRS - 1):
                    c = 256 * (PAIRS - 1) + (i % 2) * D_FF
                    fill(s + "in", i, 8, chunk(w_in, layer, 0, 8, slice(c, c + 256)))
                with eng.turns(s + "out", 2) as t:
                    for i in range(8):
                        if n0 is not None and i % 4 == 0:
                            ada_fill(n0 + t * 2 + 10 + i // 4, i // 4, layer,
                                     t * (2 * ADA_COLS) + (ADA_FIRST + 10 + i // 4) * ADA_COLS)
                        k0, nk = FF_PARTS[i % 4]
                        fill(s + "out", i, nk,
                             chunk(w_out, layer, k0, nk, bass.ds(t * 512 + (i // 4) * 256, 256)))

            with eng.layers("one") as layer:
                ffn("f1", dram["ffn1_w_in"], dram["ffn1_w_out"], layer, layer * ADA_REST + ADA_PRE)
                for _, chunks, col, _ in Z_UNITS:
                    for j, i in enumerate(chunks):
                        nk = 8 // len(chunks)
                        fill("z", i, nk, chunk(dram["w_in"], layer, nk * j, nk, slice(col, col + 256)))
                for i in range(4):
                    fill("o", i, 8, chunk(dram["w_out"], layer, 0, 8, slice(256 * i, 256 * i + 256)))
                ffn("f2", dram["ffn2_w_in"], dram["ffn2_w_out"], layer, None)
            with eng.layers("two") as layer:
                for _, chunks, col, _ in Z2_UNITS:
                    for j, i in enumerate(chunks):
                        nk = 8 // len(chunks)
                        fill("z2", i, nk, chunk(dram["w_in_2"], layer, nk * j, nk, slice(col, col + 256)))
                for i in range(4):
                    c = slice(256 * i, 256 * i + 256)
                    fill("y", i, 8, chunk(dram["w_out_a_2"], layer, 0, 2, c),
                         chunk(dram["w_out_b_2"], layer, 0, 3, c), chunk(dram["w_out_c_2"], layer, 0, 3, c))
                for i in range(4):
                    fill("wo", i, 8, chunk(dram["w_o_2"], layer, 0, 8, slice(256 * i, 256 * i + 256)))
                with eng.turns("up", 4) as t:
                    for i in range(4):
                        fill("up", i, 8,
                             chunk(dram["w_up_2"], layer, 0, 8, bass.ds(t * 1024 + i * 256, 256)))
                with eng.turns("dn", 2) as t:
                    for i in range(8):
                        k0, nk = DN_PARTS[i % 4]
                        fill("dn", i, nk,
                             chunk(dram["w_down_2"], layer, k0, nk, bass.ds(t * 512 + (i // 4) * 256, 256)))
            for t in range(2):
                sp.wait_ge(scalar_done, eng.at(f"result {t}"))
                sp.dma_start(out[0, t * P:(t + 1) * P, :],
                             result_rows[:, t]).then_inc(stored, 16)
            sp.wait_ge(stored, 32)

        @block.gpsimd
        def _(pool):
            eng = Engine(pool, pool_done, plan, old)
            for n in range(ADA_PRE):
                layer, i = divmod(n, ADA_FIRST)
                if n >= 2:
                    pool.wait_ge(ada_summed, n - 1)
                pool.dma_start(ada[:, n % 2], dram["ada_w"][layer, :, i * ADA_COLS:(i + 1) * ADA_COLS]
                               .rearrange("(k p) n -> p k n", p=P)).then_inc(first_ada_in[n % 2], 16)

            def split(phase, i):
                r, q, n = slot_of(phase, i), split_slot(phase, i), k_tiles(phase, i) // 2
                for half, done in enumerate((weights_split, weights_free[r])):
                    ks = slice(half * 4, half * 4 + n)
                    pool.wait_ge(weights_rounded, eng.split_chunk(phase, i) * 2 + half + 1)
                    pool.tensor_tensor(w_lo[:, q, ks], ring[:, r, half * n:half * n + n], w_hi[:, q, ks], ALU.subtract) \
                        .then_inc(done, 1)

            def ffn_in(phase):
                with eng.turns(phase, PAIRS // 2):
                    for i in range(4):
                        split(phase, i)
                for i in (2 * PAIRS - 2, 2 * PAIRS - 1):
                    split(phase, i)

            with eng.layers("one"):
                ffn_in("f1in")
                for i in range(ONE["z"]):
                    split("z", i)
                ffn_in("f2in")
            with eng.layers("two"):
                for i in range(TWO["z2"]):
                    split("z2", i)
                with eng.turns("up", 4):
                    for i in range(4):
                        split("up", i)
            eng._close()

        @block.tensor
        def _(pe):
            eng = Engine(pe, tensor_done, plan, old)
            mm = pe.matmul
            for slot in weights_free:
                pe.sem_inc(slot, 1)
            pe.sem_inc(weights_used, eng.step(None, weights_used, 4))

            def turn(dst, src, mark=None):
                n = src.shape[0]
                i = pe.transpose(dst, src, ident[0:n, 0:n])
                if mark:
                    i.then_inc(tensor_done, eng.step(mark))

            def terms(out, w, w_lo, x, x_lo, token_major, start, stop):
                for i, (a, b) in enumerate(((w, x), (w, x_lo), (w_lo, x))):
                    if token_major:
                        a, b = b, a
                    last = mm(out, a, b, start=start and i == 0, stop=stop and i == 2)
                return last

            def product(phase, chunks, outs, token_major=False, free=(), first=None):
                for by, mark, back in free:
                    pe.wait_ge(by, eng.at(mark, back))
                for c in range(2):
                    ws, xs = (slice(0, 256), slice(c * P, (c + 1) * P)) if token_major \
                        else (slice(c * P, (c + 1) * P), slice(0, S))
                    for j, i in enumerate(chunks):
                        r, q, n = slot_of(phase, i), split_slot(phase, i), k_tiles(phase, i) // 2
                        for half in range(2):
                            if c == 0 and half == 0:
                                pe.wait_ge(weights_split, eng.split_chunk(phase, i) + 1)
                            elif c == 0:
                                pe.wait_ge(weights_free[r], eng.freed(phase, i))
                            for k in range(half * n, half * n + n):
                                kx = 2 * n * j + k
                                if first and c == 0:
                                    pe.wait_ge(vector_done, eng.at(f"split {first} {kx}"))
                                kw = half * 4 + k - half * n
                                last = terms(outs[c], w_hi[:, q, kw, ws], w_lo[:, q, kw, ws], hn[:, kx, xs],
                                             hn_lo[:, kx, xs], token_major, kx == 0, kx == KT - 1)
                            if c == 1:
                                last.then_inc(weights_used, eng.step(f"used {phase} {i}" if half else
                                                                     f"half used {phase} {i}", weights_used))

            def plain_product(phase, chunks, x, outs, done, parts=((0, KT),), free=()):
                total = sum(n for _, n in parts)
                for i, (k0, nk) in zip(chunks, parts):
                    s = slot_of(phase, i)
                    for c in range(2):
                        if i == chunks[0]:
                            for by, mark, back in free[c:c + 1]:
                                pe.wait_ge(by, eng.at(mark, back))
                        if c == 0:
                            pe.wait_ge(weights_in[s], eng.arrived(phase, i))
                        for k in range(nk):
                            last = mm(outs[c], ring[:, s, k, c * P:(c + 1) * P], x[:, k0 + k, :],
                                      start=(k0 + k == 0), stop=(k0 + k == total - 1))
                        if c == 1:
                            last.then_inc(weights_free[s], 1)
                        elif i == chunks[-1]:
                            last.then_inc(tensor_done, eng.step(done))

            def norm_sum(n):
                pe.wait_ge(vector_done, eng.at("layer params" if n == "f1" else f"h {n}"))
                mm(bank[:, 4, 0:S], ones, square_sum[:], start=True, stop=True) \
                    .then_inc(tensor_done, eng.step(f"sum {n}"))

            def ada_reduce(n, slot, col):
                pe.wait_ge(ada_summed, n + 1)
                for j in range(4):
                    last = mm(bank[:, 7, bass.ds(col + j, 1)], ada_acc[:, slot, j * P:(j + 1) * P], ones[:, 0:1],
                              start=True, stop=True)
                last.then_inc(ada_reduced, 1)

            pe.wait_ge(tables_in, 16)
            pe.wait_ge(x_in, 16)
            for k in range(KT):
                for t in range(2):
                    turn(bank[:, k // 2, (k % 2) * S + t * P:(k % 2) * S + (t + 1) * P], x_rows[:, t, k * P:(k + 1) * P],
                         f"x turned {k // 2}" if k % 2 and t else None)
            pe.wait_ge(params_in, 16 * n_params_total)
            turn(bank[:, 4, 0:KT], rows_c[0:KT], "c turned")
            for l in range(L):
                turn(bank[:, 5, l * P:l * P + N_ROWS], rows[0:N_ROWS, l])
                turn(bank[:, 5, 256 + l * 64:256 + l * 64 + 62], rows_cw[0:62, l])
            turn(bank[:, 5, 384:424], rows_n2[0:40], "rows turned")
            for l in range(L):
                if l:
                    pe.wait_ge(vector_done, eng.at("mix weights 0"))
                for j in range(4):
                    turn(bank[:, 6, j * P:(j + 1) * P], rows_ws[:, l, j], f"ws turned {l}" if j == 3 else None)
            for n in range(ADA_PRE):
                ada_reduce(n, n % 2, 4 * n)

            def ffn(s, w_ada, n0):
                with eng.turns(s + "in", PAIRS // 2) as t:
                    for j in range(2):
                        for r in range(2):
                            b = bank[:, 2 * j + r].rearrange("p (c s) -> p c s", c=2)
                            product(s + "in", (2 * j + r,), (b[:, 0], b[:, 1]),
                                    first=None if j or r else s,
                                    free=(((scalar_done, f"{s} silu {j}", 1), (vector_done, f"{s} gated {j}", 1))[r],))
                        if w_ada:
                            ada_reduce(n0 + t * 2 + j, j, t * 8 + 16 + 4 * j)
                for r in range(2):
                    b = bank[:, r].rearrange("p (c s) -> p c s", c=2)
                    product(s + "in", (2 * PAIRS - 2 + r,), (b[:, 0], b[:, 1]),
                            free=(((scalar_done, f"{s} silu 0", 0), (vector_done, f"{s} gated 0", 0))[r],))
                pe.wait_ge(vector_done, eng.at(f"{s} gated last"))
                pe.sem_inc(passed[0], 1)
                with eng.turns(s + "out", 2) as t:
                    for j in range(2):
                        plain_product(s + "out", tuple(range(4 * j, 4 * j + 4)), gated,
                                (bank[:, 2 * j, 0:S], bank[:, 2 * j + 1, 0:S]), f"{s} out {j}", parts=FF_PARTS,
                                free=((vector_done, f"{s} h {j} 0", 1), (vector_done, f"{s} h {j} 1", 1)))
                        if w_ada:
                            ada_reduce(n0 + t * 2 + 10 + j, j, t * 8 + 56 + 4 * j)

            def scores(hd, q, k):
                for m, (qi, ki, _, _) in enumerate(hd.maps):
                    sbk, free = hd.sb[m]
                    if free:
                        pe.wait_ge(vector_done, eng.at(free))
                    b = bank[:, 2 + sbk]
                    if hd.kind == "stick":
                        mm(b[:, 0:256], k[:, ki, 0:P], q[:, qi, :], start=True, stop=True)
                        last = mm(b[:, 256:384], k[:, ki, P:S], q[:, qi, P:S], start=True, stop=True)
                    else:
                        fox = hd.kind == "fox"
                        for c0, c1, n in ((0, P, P), (P, SCW, S)):
                            qq = slice(0, P) if c0 == 0 else slice(P, S)
                            last = mm(b[:, c0:c1], q[:, qi, qq], k[:, ki, 0:n], start=True, stop=not fox)
                            if fox:
                                last = mm(b[:, c0:c1], fa[:, qi, qq], fb[:, 0:n], start=False, stop=True)
                    last.then_inc(tensor_done, eng.step(f"scores {hd.name} {m}"))

            def turned(hd, q, k, tile):
                if hd.kind == "stick":
                    (qi, ki, _, _), (pb, free) = hd.maps[0], hd.pb[0]
                    if free:
                        pe.wait_ge(done_by(free), eng.at(free))
                    b, sp_ = bank[:, 4 + pb], tile[:, hd.tp[1][0], :]
                    mm(b[:, 0:256], k[:, ki, 0:P], q[:, qi, :], start=True, stop=False)
                    pe.wait_ge(vector_done, eng.at(f"sp {hd.name}"))
                    mm(b[:, 0:256], tab("neg_suffix"), sp_[:, 0:256], start=False, stop=False)
                    mm(b[:, 128:256], tab("neg_ones"), sp_[:, 256:384], start=False, stop=True)
                    mm(b[:, 256:384], k[:, ki, P:S], q[:, qi, P:S], start=True, stop=False)
                    mm(b[:, 256:384], tab("neg_suffix"), sp_[:, 256:384], start=False, stop=True) \
                        .then_inc(tensor_done, eng.step(f"arg {hd.name}"))
                    return
                pe.wait_ge(vector_done, eng.at(f"scaled {hd.name}"))
                for m in range(len(hd.pb)):
                    pb, free = hd.pb[m]
                    if free:
                        pe.wait_ge(scalar_done, eng.at(free))
                    for j in range(3):
                        turn(bank[:, 4 + pb, j * P:(j + 1) * P], tile[:, hd.tp[m][0], j * P:(j + 1) * P],
                             f"turned {hd.name} {m}" if j == 2 else None)

            def outputs(hd, v, tt, evacuated):
                if evacuated and hd.half == 0:
                    pe.wait_ge(vector_done, eng.at(evacuated))
                b = bank[:, 6 + hd.pair % 2].rearrange("p (a s) -> p a s", a=2)[:, hd.half]
                n = len(hd.ps)
                for m in range(n):
                    pe.wait_ge(scalar_done, eng.at(f"copied {hd.name} {m}"))
                    vt = hd.maps[m][2]
                    p_ = tt[:, hd.ps[m][0]]
                    mm(b[:, 0:S], v[:, 0, vt * P:(vt + 1) * P], p_[:, 0:S], start=(m == 0), stop=False)
                    last = mm(b[:, P:S], v[:, 1, vt * P:(vt + 1) * P], p_[:, S:SCW], start=False, stop=(m == n - 1))
                last.then_inc(tensor_done, eng.step(f"out {hd.name}"))

            def attention(heads, q_of, tile, tt, filler):
                for i in range(len(heads) + 2):
                    if i < len(heads):
                        scores(heads[i], *q_of(heads[i])[:2])
                    if filler:
                        filler(i)
                    if 0 <= i - 1 < len(heads):
                        turned(heads[i - 1], *q_of(heads[i - 1])[:2], tile)
                    if i >= 2:
                        hd = heads[i - 2]
                        outputs(hd, q_of(hd)[2], tt, f"heads {heads[0].name} {hd.pair - 2}" if hd.pair >= 2 else None)

            with eng.layers("one") as layer:
                n0 = layer * ADA_REST + ADA_PRE
                norm_sum("f1")
                ffn("f1", True, n0)
                norm_sum("z")
                z_free = {"fk": (vector_done, "dq scaled", 0), "fv": (vector_done, "dk scaled", 0),
                          "ca": (scalar_done, "dv copied", 0), "cg": (vector_done, "fq scaled", 0),
                          "gu": (vector_done, "fk scaled", 0), "gv": (scalar_done, "fv copied", 0)}

                def z_unit(i):
                    name, chunks, _, tm = Z_UNITS[i]
                    b = bank[:, i % 4].rearrange("p (c s) -> p c s", c=2)
                    product("z", chunks, (b[:, 0], b[:, 1]), token_major=tm,
                            first="z" if i == 0 else None,
                            free=(z_free[name],) if name in z_free else ())

                def group_sum(name, group, b):
                    pe.wait_ge(scalar_done, eng.at(f"{name} squares"))
                    mm(bank[:, b], tab(group), qs[:, 0 if name in ("dq", "fq", "od") else 1, :],
                       start=True, stop=True).then_inc(tensor_done, eng.step(f"{name} sum"))

                z_unit(0)
                z_unit(1)
                group_sum("dq", "group32", 5)
                z_unit(2)
                group_sum("dk", "group32", 6)
                z_unit(3)
                z_unit(4)
                pe.wait_ge(scalar_done, eng.at("dq rstd"))
                group_sum("fq", "group64", 5)
                z_unit(5)
                pe.wait_ge(scalar_done, eng.at("dk rstd"))
                group_sum("fk", "group64", 6)
                pe.wait_ge(vector_done, eng.at("forget weights"))
                for k in range(KT):
                    for i, x in enumerate((hn, hn_lo)):
                        last = mm(bank[:, 4, 0:S], wfx[:, k, :], x[:, k, :].bitcast(F32),
                                  start=(k == 0 and i == 0), stop=(k == KT - 1 and i == 1))
                last.then_inc(tensor_done, eng.step("forget sum"))
                for i in range(6, 10):
                    z_unit(i)
                pe.wait_ge(vector_done, eng.at("gate normed"))
                pe.wait_ge(scalar_done, eng.at("u"))
                for j in range(4):
                    for c in range(2):
                        last = mm(bank[:, j // 2].rearrange("p (a c s) -> p a c s", a=2, c=2)[:, j % 2, c],
                                  vg[:, c, (j // 2) * P:(j // 2 + 1) * P],
                                  par[:, O_WST + j * P:O_WST + (j + 1) * P], start=True, stop=True)
                    if j % 2:
                        last.then_inc(tensor_done, eng.step(f"mixed {j // 2}"))
                pe.wait_ge(vector_done, eng.at("conv in"))
                pe.wait_ge(vector_done, eng.at("forget rows"))
                pe.wait_ge(vector_done, eng.at("fk scaled"))
                attention(HEADS_ONE, lambda hd: (qd, kd, vd) if hd.kind == "diff" else (qf, kf, vf),
                          tile1, turned1, None)
                pe.wait_ge(vector_done, eng.at("heads d0 0"))
                pe.wait_ge(vector_done, eng.at("heads d0 1"))
                pe.wait_ge(scalar_done, eng.at("od squares"))
                group_sum("od", "group64", 5)
                pe.wait_ge(vector_done, eng.at("conv out"))
                pe.wait_ge(vector_done, eng.at("mixed out"))
                for i in range(2):
                    last = mm(bank[:, 0, 0:S], ones, cv[:, i, :], start=(i == 0), stop=(i == 1))
                last.then_inc(tensor_done, eng.step("conv mean"))
                pe.wait_ge(scalar_done, eng.at("conv squares"))
                for i in range(2):
                    last = mm(bank[:, 1, 0:S], ones, cg[:, i, :], start=(i == 0), stop=(i == 1))
                last.then_inc(tensor_done, eng.step("conv var"))
                pe.wait_ge(vector_done, eng.at("heads d0 3"))
                pe.wait_ge(vector_done, eng.at("od normed"))
                pe.wait_ge(scalar_done, eng.at("conv done"))
                for i in range(4):
                    plain_product("o", (i,), mix, (bank[:, 2 * (i % 2), 0:S], bank[:, 2 * (i % 2) + 1, 0:S]), f"o {i}",
                                  free=((vector_done, f"h o {2 * i - 4}", 0), (vector_done, f"h o {2 * i - 3}", 0))
                                  if i >= 2 else ())
                norm_sum("f2")
                ffn("f2", False, None)

            def group_of(i):
                return bank[:, i % 2].rearrange("p (c s) -> p c s", c=2)

            with eng.layers("two") as layer:
                norm_sum("z2")

                def z2_unit(i):
                    name, chunks, _, tm = Z2_UNITS[i]
                    b = bank[:, i % 4] if i < 18 else bank[:, i % 2]
                    b = b.rearrange("p (c s) -> p c s", c=2)
                    free = ()
                    if 4 <= i:
                        free = ((scalar_done, f"z2 out {i - 4 if i < 18 else i - 2}", 0),)
                    product("z2", chunks, (b[:, 0], b[:, 1]), token_major=tm, free=free,
                            first="z2" if i == 0 else None)

                def rotate(i):
                    pe.wait_ge(scalar_done, eng.at(f"z2 out {i}"))
                    if i >= 2 and i not in (6, 7):
                        pe.wait_ge(vector_done, eng.at(f"rotated {i - 2}"))
                    if i in (6, 7):
                        pe.wait_ge(vector_done, eng.at(f"rotated {i - 3}"))
                    mm(bank[:, 5 + i % 2], tab("rotate"), raw[:, i % 2, :], start=True, stop=True) \
                        .then_inc(tensor_done, eng.step(f"rotary {i}"))

                for i in range(18):
                    z2_unit(i)
                    if 1 <= i <= 12 and (i - 1) not in (5, 11):
                        rotate(i - 1)
                pe.wait_ge(vector_done, eng.at("rotated 10"))
                pe.wait_ge(scalar_done, eng.at("z2 out 17"))
                for g in range(2):
                    z2_unit(18 + g)
                done = [20]

                def filler(i):
                    if done[0] < 30:
                        z2_unit(done[0])
                        done[0] += 1

                attention(HEADS_TWO, lambda hd: (q2, k2, v2), tile2, turned2, filler)
                pe.wait_ge(vector_done, eng.at("heads a0 7"))
                y_parts = (("a", 0, 2), ("b", 2, 3), ("c", 5, 3))
                for i in range(4):
                    s = slot_of("y", i)
                    pe.wait_ge(weights_in[s], eng.arrived("y", i))
                    if i == 0:
                        pe.wait_ge(scalar_done, eng.at("z2 out 29"))
                    if i >= 2:
                        pe.wait_ge(vector_done, eng.at(f"merged {i - 2}"))
                    for br, (_, k0, nk) in enumerate(y_parts):
                        b = bank[:, 3 * (i % 2) + br].rearrange("p (c s) -> p c s", c=2)
                        for c in range(2):
                            for k in range(nk):
                                last = mm(b[:, c], ring[:, s, k0 + k, c * P:(c + 1) * P], o2[:, k0 + k, :],
                                          start=(k == 0), stop=(k == nk - 1))
                    last.then_inc(weights_free[s], 1)
                pe.wait_ge(vector_done, eng.at("merged 3"))
                for i in range(4):
                    plain_product("wo", (i,), merged, (bank[:, 2 * (i % 2), 0:S], bank[:, 2 * (i % 2) + 1, 0:S]),
                                  f"wo {i}", free=((vector_done, f"h wo {2 * i - 4}", 0),
                                                   (vector_done, f"h wo {2 * i - 3}", 0)) if i >= 2 else ())
                norm_sum("up")
                with eng.turns("up", 4) as t:
                    for i in range(4):
                        b = bank[:, i].rearrange("p (c s) -> p c s", c=2)
                        product("up", (i,), (b[:, 0], b[:, 1]), first=None if i else "up",
                                free=((scalar_done, f"up relu {i}", 1),))
                pe.wait_ge(vector_done, eng.at("up squared 3"))
                pe.sem_inc(passed[0], 1)
                with eng.turns("dn", 2) as t:
                    for j in range(2):
                        plain_product("dn", tuple(range(4 * j, 4 * j + 4)), up2,
                                (bank[:, 2 * j, 0:S], bank[:, 2 * j + 1, 0:S]), f"dn out {j}", parts=DN_PARTS,
                                free=((vector_done, f"dn h {j} 0", 1), (vector_done, f"dn h {j} 1", 1)))

            norm_sum("final")
            for t in range(2):
                for k in range(KT):
                    pe.wait_ge(vector_done, eng.at(f"normed k final {k}"))
                    b = 2 * t + k // 4
                    turn(bank[:, b, (k % 4) * P:(k % 4 + 1) * P], result[:, k, t * P:(t + 1) * P],
                         f"result turned {t} {k // 4}" if k % 4 == 3 else None)
            eng._close()

        @block.scalar
        def _(act):
            eng = Engine(act, scalar_done, plan, old)
            f = act.activation

            def load(dst, src, s=params_in):
                act.dma_start(dst, src).then_inc(s, 16)
                if s is params_in:
                    n_params[0] += 1

            load(const[:], dram["constants"], tables_in)
            load(rows_c[0:KT], dram["c"].rearrange("o (k p) -> (o k) p", p=P))
            for l in range(L):
                for r, name in ((R_ADA_B, "ada_b"), (R_CONV_B, "conv_b"), (R_CONV_G, "conv_norm_g"),
                                (R_CONV_NB, "conv_norm_b")):
                    src = dram[name][l].rearrange("(k p) -> k p", p=P)
                    load(rows[r:r + src.shape[0], l], src)
                load(rows[R_NORM_G:R_NORM_G + 24, l], dram["norm_g"][l].rearrange("a (k p) -> (a k) p", p=P))
                for r, src, n in ((R_DQ, dram["diff_qk_g"][l, 0:1], 4), (R_DK, dram["diff_qk_g"][l, 1:2], 4),
                                  (R_FQ, dram["fox_qk_g"][l, 0:1], 2), (R_FK, dram["fox_qk_g"][l, 1:2], 2),
                                  (R_DO, dram["diff_out_g"][l:l + 1], 2)):
                    w = P // n
                    load(rows[r:r + 1, l].rearrange("o (a b) -> o a b", a=n),
                         src.rearrange("o (a b) -> o a b", a=1).to_broadcast([1, n, w]))
                load(par_all[:, l, O_FB:O_FB + 4], dram["fox_fb"][l:l + 1].to_broadcast([P, 4]))
                load(rows_cw[0:62, l], dram["conv_w"][l].rearrange("j (t p) -> (j t) p", p=P))
                load(rows_ws[:, l], dram["gmlp_ws"][l].rearrange("h t s -> t h s"))
                bs = par_all[:, l, O_BS:O_BS + 256].rearrange("p (i t) -> p i t", i=2)
                for j in range(4):
                    load(bs[64 * (j % 2):64 * (j % 2) + 64, j // 2],
                         dram["gmlp_bs"][l, j:j + 1].to_broadcast([64, P]))
                for k, name in ((0, "gmlp_norm_g"), (1, "gmlp_norm_b")):
                    load(par_all[:, l, O_GG + k * 256:O_GG + (k + 1) * 256],
                         dram[name][l:l + 1].to_broadcast([P, 256]))
                load(par_all[:, l, O_LAM:O_LAM + 128],
                     dram["diff_lambda"][l:l + 1].rearrange("o a b -> o (a b)").to_broadcast([P, 128]))
                load(par_all[:, l, O_WF:O_WF + 32].rearrange("p (k h) -> p k h", k=KT),
                     dram["w_in"][l, :, FOX_F0:FOX_F0 + 4].rearrange("(k p) h -> p k h", p=P))
            load(rows_n2[0:16], dram["norm_mix_2"].rearrange("l (k p) -> (l k) p", p=P))
            load(rows_n2[16:32], dram["norm_mlp_2"].rearrange("l (k p) -> (l k) p", p=P))
            load(rows_n2[32:40], dram["norm_final_2"].rearrange("(k p) -> k p", p=P))

            ahead = [0]

            def round_chunk(phase, i):
                r, q, n = slot_of(phase, i), split_slot(phase, i), k_tiles(phase, i) // 2
                act.wait_ge(weights_in[r], eng.arrived(phase, i))
                for half in range(2):
                    act.wait_ge(weights_used, eng.split_chunk(phase, i) * 2 + half + 1)
                    f(w_hi[:, q, half * 4:half * 4 + n], ring[:, r, half * n:half * n + n], ACT.Copy).then_inc(weights_rounded, 1)

            def round_to(phase, n):
                for i in range(ahead[0], n + 1):
                    round_chunk(phase, i)
                ahead[0] = max(ahead[0], n + 1)

            act.wait_ge(tensor_done, eng.at("c turned"))
            f(cond[:], bank[:, 4, 0:KT], ACT.Silu).then_inc(scalar_done, eng.step("cond"))

            def norm(n, shift=None):
                act.wait_ge(tensor_done, eng.at(f"sum {n}"))
                f(rstd[:], bank[:, 4, 0:S], ACT.Ln, bias=eps, scale=1.0 / D).then_inc(scalar_done, eng.step())
                act.wait_ge(scalar_done, eng.at())
                f(rstd[:], rstd[:], ACT.Exp, scale=-0.5).then_inc(scalar_done, eng.step(f"rstd {n}"))
                if n == "final":
                    return
                for k in range(KT):
                    act.wait_ge(vector_done, eng.at(f"normed k {n} {k}"))
                    if shift is None:
                        i = f(hn[:, k, :], normed[:, k % 2], ACT.Copy)
                    else:
                        i = f(hn[:, k, :], normed[:, k % 2], ACT.Identity, bias=mod[:, shift + k:shift + k + 1])
                    i.then_inc(scalar_done, eng.step(f"hi {n} {k}"))

            def ffn(s):
                with eng.turns(s + "in", PAIRS // 2):
                    for j in range(2):
                        act.wait_ge(weights_used, eng.at(f"used {s}in {2 * j}"))
                        act.wait_ge(vector_done, eng.at(f"{s} gated {j}", 1))
                        f(act_tmp[:, j], bank[:, 2 * j], ACT.Silu).then_inc(scalar_done, eng.step(f"{s} silu {j}"))
                        round_chunk(s + "in", 2 * j + 2)
                        round_chunk(s + "in", 2 * j + 3)
                act.wait_ge(weights_used, eng.at(f"used {s}in {2 * PAIRS - 2}"))
                act.wait_ge(vector_done, eng.at(f"{s} gated 0"))
                f(act_tmp[:, 0], bank[:, 0], ACT.Silu).then_inc(scalar_done, eng.step(f"{s} silu last"))

            def squares(name, b, j, i):
                round_to("z", i + 1)
                act.wait_ge(weights_used, eng.at(f"used z {i}"))
                f(qs[:, j], bank[:, b], ACT.Square).then_inc(scalar_done, eng.step(f"{name} squares"))

            def group_rstd(name, b, j, width, after=None):
                act.wait_ge(tensor_done, eng.at(f"{name} sum"))
                if after:
                    act.wait_ge(vector_done, eng.at(after))
                f(rr[:, j], bank[:, b], ACT.Ln, bias=eps, scale=1.0 / width).then_inc(scalar_done, eng.step())
                act.wait_ge(scalar_done, eng.at())
                f(rr[:, j], rr[:, j], ACT.Exp, scale=-0.5).then_inc(scalar_done, eng.step(f"{name} rstd"))

            def exps(hd, tile):
                st = stat[:, hd.u % 4]
                if hd.kind == "stick":
                    t = tile[:, hd.tp[0][0]]
                    act.wait_ge(tensor_done, eng.at(f"scores {hd.name} 0"))
                    if hd.tp[0][1]:
                        act.wait_ge(done_by(hd.tp[0][1]), eng.at(hd.tp[0][1]))
                    f(t, bank[:, 2 + hd.sb[0][0], 0:SCW], ACT.Abs).then_inc(scalar_done, eng.step())
                    act.wait_ge(scalar_done, eng.at())
                    f(t, t, ACT.Exp, scale=-1.0).then_inc(scalar_done, eng.step())
                    act.wait_ge(scalar_done, eng.at())
                    f(t, t, ACT.Ln, bias=ones[:, 0:1]).then_inc(scalar_done, eng.step(f"ln {hd.name}"))
                    return
                act.wait_ge(vector_done, eng.at(f"neg {hd.name}"))
                scale = 32 ** -0.5 if hd.kind == "diff" else 1.0
                n = len(hd.maps)
                for m in range(n):
                    b = 6 + (2 * m if hd.kind == "diff" else 0)
                    for j, (c0, c1) in enumerate(((0, P), (P, SCW))):
                        t = tile[:, hd.tp[m][0], c0:c1]
                        f(t, t, ACT.Exp, bias=st[:, b + j:b + j + 1], scale=scale,
                          accum_out=st[:, 10 + 2 * m + j:11 + 2 * m + j]) \
                            .then_inc(scalar_done, eng.step(f"exp {hd.name}" if m == n - 1 and j else None))

            def copies(hd, tile, tt):
                if hd.kind == "stick":
                    act.wait_ge(vector_done, eng.at(f"argm {hd.name}"))
                    if hd.ps[0][1]:
                        act.wait_ge(tensor_done, eng.at(hd.ps[0][1]))
                    f(tt[:, hd.ps[0][0]], tile[:, hd.tp[0][0]], ACT.Exp) \
                        .then_inc(scalar_done, eng.step(f"copied {hd.name} 0"))
                    return
                for m in range(len(hd.pb)):
                    act.wait_ge(tensor_done, eng.at(f"turned {hd.name} {m}"))
                    if hd.ps[m][1]:
                        act.wait_ge(tensor_done, eng.at(hd.ps[m][1]))
                    f(tt[:, hd.ps[m][0]], bank[:, 4 + hd.pb[m][0], 0:SCW], ACT.Copy) \
                        .then_inc(scalar_done, eng.step(f"copied {hd.name} {m}"))

            def attention(heads, tile, tt, filler=None):
                for i in range(len(heads) + 2):
                    if filler:
                        filler(i)
                    if i < len(heads):
                        exps(heads[i], tile)
                    if 0 <= i - 1 < len(heads):
                        copies(heads[i - 1], tile, tt)

            with eng.layers("one"):
                ahead[0] = 0
                round_to("f1in", 1)
                norm("f1", 0)
                ffn("f1")
                ahead[0] = 0
                round_to("z", 1)
                norm("z", 24)
                squares("dq", 0, 0, 1)
                squares("dk", 1, 1, 3)
                group_rstd("dq", 5, 0, 32)
                round_to("z", 5)
                act.wait_ge(weights_used, eng.at("used z 4"))
                f(vd[:], bank[:, 2].rearrange("p (c s) -> p c s", c=2), ACT.Copy) \
                    .then_inc(scalar_done, eng.step("dv copied"))
                group_rstd("dk", 6, 1, 32)
                squares("fq", 3, 0, 5)
                squares("fk", 0, 1, 6)
                group_rstd("fq", 5, 0, 64, "dq scaled")
                round_to("z", 8)
                act.wait_ge(weights_used, eng.at("used z 7"))
                f(vf[:], bank[:, 1].rearrange("p (c s) -> p c s", c=2), ACT.Copy) \
                    .then_inc(scalar_done, eng.step("fv copied"))
                group_rstd("fk", 6, 1, 64, "dk scaled")
                act.wait_ge(vector_done, eng.at("lambda sums"))
                f(small[:, 2:4], small[:, 0:2], ACT.Exp).then_inc(scalar_done, eng.step("lambda exp"))
                act.wait_ge(tensor_done, eng.at("forget sum"))
                fbc = small[:, 8:9]
                f(ft[:, 0, :], bank[:, 4, 0:S], ACT.Abs, bias=fbc).then_inc(scalar_done, eng.step())
                act.wait_ge(scalar_done, eng.at())
                f(ft[:, 0, :], ft[:, 0, :], ACT.Exp, scale=-1.0).then_inc(scalar_done, eng.step())
                act.wait_ge(scalar_done, eng.at())
                f(ft[:, 0, :], ft[:, 0, :], ACT.Ln, bias=ones[:, 0:1]).then_inc(scalar_done, eng.step("forget ln"))
                round_to("z", 10)
                act.wait_ge(weights_used, eng.at("used z 9"))
                f(cg[:], bank[:, 3].rearrange("p (c s) -> p c s", c=2), ACT.Sigmoid) \
                    .then_inc(scalar_done, eng.step("conv gate"))
                round_to("z", 11)
                act.wait_ge(weights_used, eng.at("used z 10"))
                f(u_[:], bank[:, 0].rearrange("p (c s) -> p c s", c=2), ACT.Gelu_apprx_tanh) \
                    .then_inc(scalar_done, eng.step("u"))
                round_to("z", 11)
                act.wait_ge(weights_used, eng.at("used z 11"))
                f(vg[:], bank[:, 1].rearrange("p (c s) -> p c s", c=2), ACT.Gelu_apprx_tanh) \
                    .then_inc(scalar_done, eng.step("gate gelu"))
                act.wait_ge(vector_done, eng.at("gate stats"))
                f(small[:, 20:22], small[:, 16:20].rearrange("p (c b) -> p c b", c=2)[:, :, 1], ACT.Ln, bias=eps) \
                    .then_inc(scalar_done, eng.step())
                act.wait_ge(scalar_done, eng.at())
                f(small[:, 20:22], small[:, 20:22], ACT.Exp, scale=-0.5) \
                    .then_inc(scalar_done, eng.step("gate rstd"))
                attention(HEADS_ONE, tile1, turned1)
                act.wait_ge(vector_done, eng.at("heads d0 1"))
                f(qs[:, 0], od[:].rearrange("p a s -> p (a s)"), ACT.Square) \
                    .then_inc(scalar_done, eng.step("od squares"))
                group_rstd("od", 5, 0, 64)
                act.wait_ge(vector_done, eng.at("conv centred"))
                f(cg[:], cd[:], ACT.Square).then_inc(scalar_done, eng.step("conv squares"))
                act.wait_ge(tensor_done, eng.at("conv var"))
                f(rstd[:], bank[:, 1, 0:S], ACT.Ln, bias=eps, scale=1.0 / 256).then_inc(scalar_done, eng.step())
                act.wait_ge(scalar_done, eng.at())
                f(rstd[:], rstd[:], ACT.Exp, scale=-0.5).then_inc(scalar_done, eng.step("conv rstd"))
                act.wait_ge(vector_done, eng.at("conv normed"))
                for i in range(2):
                    f(mix[:, 2 + i, :], cd[:, i, :], ACT.Silu,
                      bias=par[:, R_CONV_NB + i:R_CONV_NB + i + 1],
                      scale=par[:, R_CONV_G + i:R_CONV_G + i + 1]) \
                        .then_inc(scalar_done, eng.step("conv done" if i else None))
                ahead[0] = 0
                round_to("f2in", 1)
                norm("f2", 48)
                ffn("f2")

            with eng.layers("two"):
                ahead[0] = 0
                round_to("z2", 1)
                norm("z2")
                for i in range(18):
                    chunks = Z2_UNITS[i][1]
                    round_to("z2", chunks[-1] + 1)
                    act.wait_ge(weights_used, eng.at(f"used z2 {chunks[-1]}"))
                    b = bank[:, i % 4]
                    if i in (5, 11):
                        if i == 5:
                            for a in range(2):
                                f(q2[:, 4 * i:4 * i + 4, :].rearrange("p (t a) s -> p t a s", a=2)[:, :, a],
                                  b.rearrange("p (t s) -> p t s", t=2), ACT.Identity,
                                  scale=tab("in64_eighth", 1, a)) \
                                    .then_inc(scalar_done, eng.step(f"z2 out {i}" if a else None))
                        else:
                            f(k2[:, 10:12, :], b.rearrange("p (t s) -> p t s", t=2), ACT.Copy) \
                                .then_inc(scalar_done, eng.step(f"z2 out {i}"))
                    elif i < 12:
                        j = i % 2
                        if i >= 2:
                            act.wait_ge(vector_done, eng.at(f"rotated {i - 2 if i not in (7,) else i - 3}"))
                            if i == 6:
                                act.wait_ge(vector_done, eng.at("rotated 4"))
                        f(raw[:, j], b, ACT.Copy).then_inc(scalar_done, eng.step(f"z2 out {i}"))
                    else:
                        c = 256 * (i - 12)
                        f(v2[:, :, c:c + 256], b.rearrange("p (t s) -> p t s", t=2), ACT.Copy) \
                            .then_inc(scalar_done, eng.step(f"z2 out {i}"))

                def gate_copy(i):
                    round_to("z2", min(Z2_UNITS[i][1][-1] + 1, TWO["z2"] - 1))
                    act.wait_ge(weights_used, eng.at(f"used z2 {Z2_UNITS[i][1][-1]}"))
                    c = 2 * (i - 18)
                    f(gates[:, c:c + 2, :], bank[:, i % 2].rearrange("p (t s) -> p t s", t=2), ACT.Copy) \
                        .then_inc(scalar_done, eng.step(f"z2 out {i}"))

                for g in range(2):
                    gate_copy(18 + g)
                done = [20]

                def filler(i):
                    if i and done[0] < 30:
                        gate_copy(done[0])
                        done[0] += 1

                attention(HEADS_TWO, tile2, turned2, filler)
                for i in range(4):
                    for br in range(3):
                        g = gates[:, 8 * br + 2 * i:8 * br + 2 * i + 2, :]
                        f(g, g, ACT.Sigmoid).then_inc(scalar_done, eng.step(f"gate {i}" if br == 2 else None))
                ahead[0] = 0
                round_to("up", 1)
                norm("up")

                def up_turn(last):
                    for i in range(4):
                        act.wait_ge(weights_used, eng.at(f"used up {i}"))
                        if i < 2:
                            act.wait_ge(vector_done, eng.at(f"up squared {i + 2}", 1))
                        else:
                            act.wait_ge(vector_done, eng.at(f"up squared {i - 2}"))
                        f(act_tmp[:, i % 2], bank[:, i], ACT.Relu) \
                            .then_inc(scalar_done, eng.step(None if last else f"up relu {i}"))
                        if not last:
                            round_chunk("up", i + 2)
                        elif i < 2:
                            round_chunk("up", 14 + i)

                with eng.turns("up", 3):
                    up_turn(False)
                up_turn(True)
            norm("final")
            for t in range(2):
                for j in range(2):
                    act.wait_ge(tensor_done, eng.at(f"result turned {t} {j}"))
                    f(result_rows[:, t, 512 * j:512 * (j + 1)],
                      bank[:, 2 * t + j], ACT.Copy).then_inc(scalar_done, eng.step(f"result {t}" if j else None))
            eng._close()

        assert n_params[0] in (0, n_params_total), n_params

        @block.vector
        def _(dve):
            eng = Engine(dve, vector_done, plan, old)
            tt, ts, stt = dve.tensor_tensor, dve.tensor_scalar, dve.scalar_tensor_tensor

            def col(t, i):
                return t[:, i:i + 1]

            def ada_sum(j, n, half, n0=None):
                if n0 is None:
                    dve.wait_ge(first_ada_in[j], half * 16 + 16)
                else:
                    dve.wait_ge(ada_in[j], half * 16 + 16)
                if n0 is not None or n >= 2:
                    dve.wait_ge(ada_reduced, n - 1)
                ts(ada_acc[:, j], ada[:, j, 0], col(cond, 0), None, ALU.mult).then_inc(vector_done, eng.step())
                for k in range(1, KT - 1):
                    dve.wait_ge(vector_done, eng.at())
                    stt(ada_acc[:, j], ada[:, j, k], col(cond, k), ada_acc[:, j], ALU.mult, ALU.add) \
                        .then_inc(vector_done, eng.step())
                dve.wait_ge(vector_done, eng.at())
                stt(ada_acc[:, j], ada[:, j, KT - 1], col(cond, KT - 1), ada_acc[:, j], ALU.mult, ALU.add) \
                    .then_inc(ada_summed, 1)

            def add_square(hk, mark):
                dve.wait_ge(vector_done, eng.at())
                tt(normed[:, 0], hk, hk, ALU.mult).then_inc(vector_done, eng.step())
                dve.wait_ge(vector_done, eng.at())
                tt(square_sum[:], square_sum[:], normed[:, 0], ALU.add).then_inc(vector_done, eng.step(mark))

            for k in range(4):
                dve.wait_ge(tensor_done, eng.at(f"x turned {k}"))
                dve.tensor_copy(h[:, 2 * k:2 * k + 2, :].rearrange("p k s -> p (k s)"), bank[:, k]) \
                    .then_inc(vector_done, eng.step("x" if k == 3 else None))
            dve.memset(square_sum[:], 0.0).then_inc(vector_done, eng.step())
            for k in range(KT):
                add_square(h[:, k, :], None)
            dve.wait_ge(tensor_done, eng.at("rows turned"))
            for l in range(L):
                dve.tensor_copy(par_all[:, l, 0:N_ROWS], bank[:, 5, l * P:l * P + N_ROWS])
                dve.tensor_copy(par_all[:, l, O_CW:O_CW + 62], bank[:, 5, 256 + l * 64:256 + l * 64 + 62])
                dve.memset(par_all[:, l, N_ROWS:O_CW], 0.0)
                dve.memset(par_all[:, l, O_CW + 62:O_WST], 0.0)
            dve.tensor_copy(norm2[:], bank[:, 5, 384:424]).then_inc(vector_done, eng.step("columns"))
            for l in range(L):
                dve.wait_ge(tensor_done, eng.at(f"ws turned {l}"))
                tt(par_all[:, l, O_WST:O_WST + 512].rearrange("p (h t) -> p h t", h=4),
                   bank[:, 6].rearrange("p (h t) -> p h t", h=4),
                   tab("mix_seen").rearrange("p (o t) -> p o t", o=1).to_broadcast([P, 4, P]), ALU.mult) \
                    .then_inc(vector_done, eng.step(f"mix weights {l}"))
            dve.wait_ge(scalar_done, eng.at("cond"))
            for n in range(ADA_PRE):
                ada_sum(n % 2, n, n // 2)
            dve.wait_ge(ada_reduced, ADA_PRE)
            dve.wait_ge(vector_done, eng.at("columns"))
            tt(mod_first[:], bank[:, 7, 0:32].rearrange("p (l c) -> p l c", l=L), par_all[:, :, 0:16], ALU.add) \
                .then_inc(vector_done, eng.step())
            dve.wait_ge(vector_done, eng.at())

            def scale_norm(n, gains, shift=None):
                dve.wait_ge(vector_done, eng.at())
                dve.wait_ge(scalar_done, eng.at(f"rstd {n}"))
                for k in range(KT + 1):
                    if k < KT:
                        if k >= 2 and n != "final":
                            dve.wait_ge(vector_done, eng.at())
                        stt(result[:, k] if n == "final" else normed[:, k % 2], h[:, k, :], gains(k), rstd[:],
                            ALU.mult, ALU.mult) \
                            .then_inc(vector_done, eng.step(f"normed k {n} {k}"))
                    if k and n != "final":
                        dve.wait_ge(scalar_done, eng.at(f"hi {n} {k - 1}"))
                        if shift is None:
                            i = tt(hn_lo[:, k - 1, :], normed[:, (k - 1) % 2], hn[:, k - 1, :], ALU.subtract)
                        else:
                            i = stt(hn_lo[:, k - 1, :], normed[:, (k - 1) % 2], col(mod, shift + k - 1),
                                    hn[:, k - 1, :], ALU.add, ALU.subtract)
                        i.then_inc(vector_done, eng.step(f"split {n} {k - 1}"))
                dve.memset(square_sum[:], 0.0).then_inc(vector_done, eng.step())

            def gated_scale(dst, scale_at, gain_at):
                return stt(der[:, dst:dst + 8], mod[:, scale_at:scale_at + 8], 1.0,
                           par[:, gain_at:gain_at + 8], ALU.add, ALU.mult)

            def ffn(s, gate_at, n0, half0):
                with eng.turns(s + "in", PAIRS // 2) as t:
                    for j in range(2):
                        if n0 is not None:
                            ada_sum(j, n0 + t * 2 + j, half0 + t, n0)
                        dve.wait_ge(scalar_done, eng.at(f"{s} silu {j}"))
                        dve.wait_ge(weights_used, eng.at(f"used {s}in {2 * j + 1}"))
                        tt(gated[:, bass.ds(t * 4 + 2 * j, 2), :].rearrange("p c s -> p (c s)"),
                           act_tmp[:, j], bank[:, 2 * j + 1], ALU.mult) \
                            .then_inc(vector_done, eng.step(f"{s} gated {j}"))
                dve.wait_ge(scalar_done, eng.at(f"{s} silu last"))
                dve.wait_ge(weights_used, eng.at(f"used {s}in {2 * PAIRS - 1}"))
                tt(gated[:, FT - 2:FT, :].rearrange("p c s -> p (c s)"), act_tmp[:, 0], bank[:, 1], ALU.mult) \
                    .then_inc(vector_done, eng.step(f"{s} gated last"))
                if n0 is not None:
                    dve.wait_ge(ada_reduced, n0 + 10)
                    tt(mod[:, 16:56], bank[:, 7, 16:56], par[:, 16:56], ALU.add).then_inc(vector_done, eng.step())
                    dve.wait_ge(vector_done, eng.at())
                ts(der[:, 24:32], mod[:, gate_at:gate_at + 8], 0.5, None, ALU.mult) \
                    .then_inc(vector_done, eng.step())
                dve.wait_ge(vector_done, eng.at())
                dve.sem_inc(passed[1], 1)
                with eng.turns(s + "out", 2) as t:
                    for j in range(2):
                        if n0 is not None:
                            ada_sum(j, n0 + t * 2 + 10 + j, half0 + t + PAIRS // 2, n0)
                        for c in range(2):
                            if c == 0:
                                dve.wait_ge(tensor_done, eng.at(f"{s} out {j}"))
                            else:
                                dve.wait_ge(weights_free[slot_of(s + "out", 4 * j + 3)], eng.freed(s + "out", 4 * j + 3))
                            k = t * 4 + 2 * j + c
                            hk = h[:, bass.ds(k, 1), :].rearrange("p o s -> p (o s)")
                            stt(hk, bank[:, 2 * j + c, 0:S], der[:, bass.ds(k + 24, 1)], hk,
                                ALU.mult, ALU.add).then_inc(vector_done, eng.step(f"{s} h {j} {c}"))
                            add_square(hk, f"{s} squares {j} {c}")

            def maxima(hd, tile):
                st = stat[:, hd.u % 4]
                if hd.kind == "stick":
                    t, sp_ = tile[:, hd.tp[0][0]], tile[:, hd.tp[1][0]]
                    if hd.tp[1][1]:
                        dve.wait_ge(tensor_done, eng.at(hd.tp[1][1]))
                    dve.wait_ge(scalar_done, eng.at(f"ln {hd.name}"))
                    stt(sp_, bank[:, 2 + hd.sb[0][0], 0:SCW], 0.0, t, ALU.max, ALU.add) \
                        .then_inc(vector_done, eng.step())
                    dve.wait_ge(vector_done, eng.at())
                    tt(sp_, sp_, tab("before", SCW), ALU.mult).then_inc(vector_done, eng.step(f"sp {hd.name}"))
                    return
                for m, (_, _, _, mask) in enumerate(hd.maps):
                    dve.wait_ge(tensor_done, eng.at(f"scores {hd.name} {m}"))
                    dve.sem_inc(passed[1], 1)
                    for j, (c0, c1) in enumerate(((0, P), (P, SCW))):
                        dve.tensor_tensor_reduce(
                            out=tile[:, hd.tp[m][0], c0:c1], in0=bank[:, 2 + hd.sb[m][0], c0:c1],
                            in1=tab(mask, c1 - c0, c0), scale=1.0, scalar=-3e38, op0=ALU.add, op1=ALU.max,
                            accum_out=st[:, 2 * m + j:2 * m + j + 1]) \
                            .then_inc(vector_done, eng.step(f"max {hd.name} {m}" if j else None))
                dve.wait_ge(vector_done, eng.at())
                if hd.kind == "diff":
                    i = ts(st[:, 6:10], st[:, 0:4], -(32 ** -0.5), None, ALU.mult)
                elif len(hd.maps) == 1:
                    i = ts(st[:, 6:8], st[:, 0:2], -1.0, None, ALU.mult)
                else:
                    i = dve.tensor_reduce(st[:, 6:8], st[:, 0:6].rearrange("p (m j) -> p j m", j=2), AX.X, ALU.max,
                                          negate=True)
                i.then_inc(vector_done, eng.step(f"neg {hd.name}"))

            def scaling(hd, tile):
                st = stat[:, hd.u % 4]
                if hd.kind == "stick":
                    dve.wait_ge(tensor_done, eng.at(f"arg {hd.name}"))
                    tt(tile[:, hd.tp[0][0]], bank[:, 4 + hd.pb[0][0], 0:SCW], tab("before_neg", SCW), ALU.add) \
                        .then_inc(vector_done, eng.step(f"argm {hd.name}"))
                    return
                dve.wait_ge(scalar_done, eng.at(f"exp {hd.name}"))
                n = len(hd.maps)
                if n == 3:
                    dve.tensor_reduce(st[:, 8:10], st[:, 10:16].rearrange("p (m j) -> p j m", j=2),
                                      AX.X, ALU.add).then_inc(vector_done, eng.step())
                    dve.wait_ge(vector_done, eng.at())
                r0, r1 = (8, 10) if n == 3 else (10, 14) if n == 2 else (10, 12)
                dve.reciprocal(st[:, r0:r1], st[:, r0:r1]).then_inc(vector_done, eng.step())
                dve.wait_ge(vector_done, eng.at())
                if hd.kind == "diff":
                    ts(st[:, 12:14], st[:, 12:14], small[:, 4:5], None, ALU.mult).then_inc(vector_done, eng.step())
                    dve.wait_ge(vector_done, eng.at())
                    for j, (c0, c1) in enumerate(((0, P), (P, SCW))):
                        a, b = (tile[:, hd.tp[m][0], c0:c1] for m in range(2))
                        ts(a, a, st[:, 10 + j:11 + j], None, ALU.mult).then_inc(vector_done, eng.step())
                        dve.wait_ge(vector_done, eng.at())
                        stt(a, b, st[:, 12 + j:13 + j], a, ALU.mult, ALU.add) \
                            .then_inc(vector_done, eng.step(f"scaled {hd.name}" if j else None))
                    return
                for m in range(n):
                    for j, (c0, c1) in enumerate(((0, P), (P, SCW))):
                        a = tile[:, hd.tp[m][0], c0:c1]
                        ts(a, a, st[:, r0 + j:r0 + j + 1], None, ALU.mult) \
                            .then_inc(vector_done, eng.step(f"scaled {hd.name}" if m == n - 1 and j else None))

            def pair_out(heads, i, dst):
                hd = heads[i]
                if hd.half == 0:
                    return
                dve.wait_ge(tensor_done, eng.at(f"out {hd.name}"))
                b = bank[:, 6 + hd.pair % 2].rearrange("p (a s) -> p a s", a=2)
                for a in range(2):
                    dve.tensor_copy(dst(hd)[64 * a:64 * a + 64], b[64 * a:64 * a + 64, a]) \
                        .then_inc(vector_done, eng.step(f"heads {heads[0].name} {hd.pair}" if a else None))
            tap = [0]

            def conv_taps(n):
                for j in range(tap[0], min(tap[0] + n, CONV_K)):
                    if j:
                        dve.wait_ge(vector_done, eng.at())
                    for i in range(2):
                        w = col(par, O_CW + 2 * j + i)
                        src = yp[:, i, j:j + S]
                        if j == 0:
                            ins = ts(cv[:, i, :], src, w, col(par, R_CONV_B + i), ALU.mult, ALU.add)
                        else:
                            ins = stt(cv[:, i, :], src, w, cv[:, i, :], ALU.mult, ALU.add)
                        ins.then_inc(vector_done, eng.step("conv out" if j == CONV_K - 1 and i else None))
                tap[0] += n

            def attention(heads, tile, dst, taps=0):
                tap[0] = 0
                for i in range(len(heads) + 2):
                    if i < len(heads):
                        maxima(heads[i], tile)
                    if taps:
                        conv_taps(taps)
                    if 0 <= i - 1 < len(heads):
                        scaling(heads[i - 1], tile)
                    if taps:
                        conv_taps(taps)
                    if i >= 2:
                        pair_out(heads, i - 2, dst)

            with eng.layers("one") as layer:
                n0 = layer * ADA_REST + ADA_PRE
                half0 = layer * (ADA_REST // 2)
                dve.wait_ge(vector_done, eng.at())
                dve.tensor_copy(small[:, 6:8], const[:, bass.ds(layer * 2 + at["lam_init"], 2)])
                dve.tensor_copy(mod[:, 0:16], mod_first[:, bass.ds(layer, 1), :].rearrange("p o n -> p (o n)")) \
                    .then_inc(vector_done, eng.step("layer params"))
                dve.wait_ge(vector_done, eng.at())
                gated_scale(0, 8, R_NORM_G).then_inc(vector_done, eng.step())
                scale_norm("f1", lambda k: col(der, k), 0)
                ffn("f1", 16, n0, half0)
                plan.marks["h z"] = plan.marks["f1 squares 1 1"]
                dve.wait_ge(ada_reduced, n0 + ADA_REST)
                dve.wait_ge(vector_done, eng.at())
                tt(mod[:, 56:72], bank[:, 7, 56:72], par[:, 56:72], ALU.add).then_inc(vector_done, eng.step())
                dve.wait_ge(vector_done, eng.at())
                gated_scale(8, 32, R_NORM_G + 8).then_inc(vector_done, eng.step())
                gated_scale(16, 56, R_NORM_G + 16).then_inc(vector_done, eng.step())
                ts(der[:, 32:36], tab("in32", 4), col(par, R_DQ), None, ALU.mult).then_inc(vector_done, eng.step())
                ts(der[:, 36:38], tab("in64_eighth", 2), col(par, R_FQ), None, ALU.mult) \
                    .then_inc(vector_done, eng.step())
                ts(der[:, 38:39], col(par, R_DO), small[:, 7:8], None, ALU.mult).then_inc(vector_done, eng.step())
                tt(small[:, 40:44], tab("in32", 4), par[:, O_FB:O_FB + 4], ALU.mult) \
                    .then_inc(vector_done, eng.step())
                dve.wait_ge(vector_done, eng.at())
                dve.tensor_reduce(small[:, 8:9], small[:, 40:44], AX.X, ALU.add).then_inc(vector_done, eng.step())
                lam = par[:, O_LAM:O_LAM + 128].rearrange("p (a b c) -> p a b c", a=2, b=2)
                tt(ft[:, 2, 0:64].rearrange("p (a c) -> p a c", a=2), lam[:, :, 0], lam[:, :, 1], ALU.mult) \
                    .then_inc(vector_done, eng.step())
                dve.wait_ge(vector_done, eng.at())
                dve.tensor_reduce(small[:, 0:2], ft[:, 2, 0:64].rearrange("p (a c) -> p a c", a=2), AX.X, ALU.add) \
                    .then_inc(vector_done, eng.step("lambda sums"))
                scale_norm("z", lambda k: col(der, 8 + k), 24)
                dve.tensor_copy(
                    wfx.rearrange("p k (h r) -> p (k h) r", h=4),
                    par[:, O_WF:O_WF + 32].rearrange("p (k o) -> p k o", o=1).to_broadcast([P, 32, 32])) \
                    .then_inc(vector_done, eng.step("forget weights"))
                dve.memset(yp[:, :, 0:CONV_K - 1], 0.0).then_inc(vector_done, eng.step())

                def scale_q(name, b, j, dst, gain, maps):
                    dve.wait_ge(scalar_done, eng.at(f"{name} rstd"))
                    for i in range(2):
                        for m in range(maps):
                            stt(dst[:, maps * i + m, :], bank[:, b, i * S:(i + 1) * S], gain(m),
                                rr[:, j, i * S:(i + 1) * S], ALU.mult, ALU.mult) \
                                .then_inc(vector_done, eng.step(f"{name} scaled" if i and m == maps - 1 else None))

                scale_q("dq", 0, 0, qd, lambda m: col(der, 32 + m), 4)
                scale_q("dk", 1, 1, kd, lambda m: col(par, R_DK), 1)
                scale_q("fq", 3, 0, qf, lambda m: col(der, 36 + m), 2)
                scale_q("fk", 0, 1, kf, lambda m: col(par, R_FK), 1)
                dve.wait_ge(scalar_done, eng.at("lambda exp"))
                tt(small[:, 4:5], small[:, 3:4], small[:, 2:3], ALU.subtract).then_inc(vector_done, eng.step())
                dve.wait_ge(vector_done, eng.at())
                tt(small[:, 4:5], small[:, 4:5], small[:, 6:7], ALU.subtract).then_inc(vector_done, eng.step())
                dve.wait_ge(vector_done, eng.at())
                dve.wait_ge(scalar_done, eng.at("forget ln"))
                ts(ft[:, 1, :], bank[:, 4, 0:S], col(small, 8), 0.0, ALU.add, ALU.min) \
                    .then_inc(vector_done, eng.step())
                dve.wait_ge(vector_done, eng.at())
                tt(ft[:, 1, :], ft[:, 1, :], ft[:, 0, :], ALU.subtract).then_inc(vector_done, eng.step())
                dve.wait_ge(vector_done, eng.at())
                dve.tensor_tensor_scan(ft[:, 2, :], ones[:, 0:1].to_broadcast([P, S]), ft[:, 1, :], 0.0,
                                         ALU.mult, ALU.add).then_inc(vector_done, eng.step())
                dve.wait_ge(vector_done, eng.at())
                for m in range(4):
                    ts(fa[:, m, :], ft[:, 2, :], tab("cum_row", 1, m), tab("one_row", 1, m), ALU.mult, ALU.add) \
                        .then_inc(vector_done, eng.step())
                ts(fb[:], ft[:, 2, :], tab("neg_cum_rows", 1), tab("one_rows", 1), ALU.mult, ALU.add) \
                    .then_inc(vector_done, eng.step("forget rows"))
                dve.wait_ge(scalar_done, eng.at("conv gate"))
                dve.wait_ge(weights_used, eng.at("used z 8"))
                tt(yp[:, :, CONV_K - 1:CONV_K - 1 + S], bank[:, 2].rearrange("p (c s) -> p c s", c=2), cg[:],
                   ALU.mult).then_inc(vector_done, eng.step("conv in"))
                dve.wait_ge(scalar_done, eng.at("gate gelu"))
                for c in range(2):
                    dve.bn_stats(small[:, 24 + 6 * c:30 + 6 * c], vg[:, c, :]).then_inc(vector_done, eng.step())
                dve.wait_ge(vector_done, eng.at())
                dve.sem_inc(passed[1], 1)
                for c in range(2):
                    dve.bn_aggr(small[:, 16 + 2 * c:18 + 2 * c], small[:, 24 + 6 * c:30 + 6 * c]) \
                        .then_inc(vector_done, eng.step("gate stats" if c else None))
                dve.wait_ge(scalar_done, eng.at("gate rstd"))
                for c in range(2):
                    ts(vg[:, c, :], vg[:, c, :], small[:, 16 + 2 * c:17 + 2 * c], small[:, 20 + c:21 + c],
                       ALU.subtract, ALU.mult).then_inc(vector_done, eng.step())
                dve.wait_ge(vector_done, eng.at())
                gain = par[:, O_GG:O_GG + 512].rearrange("p (k s) -> p k s", k=2)
                for k, op in ((0, ALU.mult), (1, ALU.add)):
                    i = tt(vg[:], vg[:], gain[:, k:k + 1].to_broadcast([P, 2, 256]), op)
                    i.then_inc(vector_done, eng.step("gate normed" if k else None))
                    if not k:
                        dve.wait_ge(vector_done, eng.at())
                for j in range(4):
                    dve.wait_ge(tensor_done, eng.at(f"mixed {j // 2}"))
                    r = slice(64 * (j % 2), 64 * (j % 2) + 64)
                    dst = mix[r, 4 + j // 2, :].rearrange("p (c t) -> p c t", c=2)
                    b = bank[:, j // 2].rearrange("p (a c s) -> p a c s", a=2, c=2)[r, j % 2]
                    bias = par[r, O_BS + (j // 2) * P:O_BS + (j // 2 + 1) * P].rearrange("p (o t) -> p o t", o=1)
                    tt(dst, b, bias.to_broadcast([64, 2, P]), ALU.add).then_inc(vector_done, eng.step())
                    dve.wait_ge(vector_done, eng.at())
                    tt(dst, dst, u_[r, j // 2, :].rearrange("p (c t) -> p c t", c=2), ALU.mult) \
                        .then_inc(vector_done, eng.step("mixed out" if j == 3 else None))
                attention(HEADS_ONE, tile1,
                          lambda hd: od[:, hd.out_tile, :] if hd.kind == "diff" else mix[:, 6 + hd.out_tile, :],
                          taps=2)
                dve.wait_ge(scalar_done, eng.at("od rstd"))
                for i in range(2):
                    stt(mix[:, i, :], od[:, i, :], col(der, 38), rr[:, 0, i * S:(i + 1) * S], ALU.mult, ALU.mult) \
                        .then_inc(vector_done, eng.step("od normed" if i else None))
                dve.wait_ge(tensor_done, eng.at("conv mean"))
                for i in range(2):
                    stt(cd[:, i, :], bank[:, 0, 0:S], -1.0 / 256, cv[:, i, :], ALU.mult, ALU.add) \
                        .then_inc(vector_done, eng.step("conv centred" if i else None))
                dve.wait_ge(scalar_done, eng.at("conv rstd"))
                for i in range(2):
                    tt(cd[:, i, :], cd[:, i, :], rstd[:], ALU.mult) \
                        .then_inc(vector_done, eng.step("conv normed" if i else None))
                for i in range(4):
                    for c in range(2):
                        k = 2 * i + c
                        if c == 0:
                            dve.wait_ge(tensor_done, eng.at(f"o {i}"))
                        else:
                            dve.wait_ge(weights_free[slot_of("o", i)], eng.freed("o", i))
                        stt(h[:, k, :], bank[:, 2 * (i % 2) + c, 0:S], col(mod, 40 + k), h[:, k, :],
                            ALU.mult, ALU.add).then_inc(vector_done, eng.step(f"h o {k}"))
                        add_square(h[:, k, :], "h f2" if k == KT - 1 else None)
                dve.wait_ge(vector_done, eng.at())
                scale_norm("f2", lambda k: col(der, 16 + k), 48)
                ffn("f2", 64, None, None)
                dve.tensor_copy(par, par_all[:, L - 1]).then_inc(vector_done, eng.step())

            with eng.layers("two") as layer:
                dve.wait_ge(vector_done, eng.at())
                dve.tensor_copy(der[:, 0:8], norm2[:, bass.ds(layer * 8, 8)])
                dve.tensor_copy(der[:, 8:16], norm2[:, bass.ds(layer * 8 + 16, 8)]) \
                    .then_inc(vector_done, eng.step("h z2"))
                dve.wait_ge(vector_done, eng.at())
                scale_norm("z2", lambda k: col(der, k))
                cosb = tab("cos", S).rearrange("p (o s) -> p o s", o=1).to_broadcast([P, 2, S])
                sinb = tab("sin", S).rearrange("p (o s) -> p o s", o=1).to_broadcast([P, 2, S])
                for i in [x for x in range(12) if x not in (5, 11)]:
                    dve.wait_ge(tensor_done, eng.at(f"rotary {i}"))
                    a = rot_tmp[:, 0].rearrange("p (c s) -> p c s", c=2)
                    b = rot_tmp[:, 1].rearrange("p (c s) -> p c s", c=2)
                    src = raw[:, i % 2].rearrange("p (c s) -> p c s", c=2)
                    rot = bank[:, 5 + i % 2].rearrange("p (c s) -> p c s", c=2)
                    half = i % 6 == 4
                    n = 1 if half else 2
                    tt(a[:, 0:n], rot[:, 0:n], sinb[:, 0:n], ALU.mult).then_inc(vector_done, eng.step())
                    tt(b[:, 0:n], src[:, 0:n], cosb[:, 0:n], ALU.mult).then_inc(vector_done, eng.step())
                    dve.wait_ge(vector_done, eng.at())
                    if i < 6:
                        tt(a[:, 0:n], a[:, 0:n], b[:, 0:n], ALU.add).then_inc(vector_done, eng.step())
                        if half:
                            dve.tensor_copy(a[:, 1], src[:, 1]).then_inc(vector_done, eng.step())
                        dve.wait_ge(vector_done, eng.at())
                        dst = q2[:, 4 * i:4 * i + 4, :].rearrange("p (t a) s -> p t a s", a=2)
                        for m in range(2):
                            ts(dst[:, :, m], a, tab("in64_eighth", 1, m), None, ALU.mult) \
                                .then_inc(vector_done, eng.step(f"rotated {i}" if m else None))
                    else:
                        k0 = 2 * (i - 6)
                        if half:
                            dve.tensor_copy(k2[:, k0 + 1, :], src[:, 1]).then_inc(vector_done, eng.step())
                        tt(k2[:, k0:k0 + n, :], a[:, 0:n], b[:, 0:n], ALU.add) \
                            .then_inc(vector_done, eng.step(f"rotated {i}"))
                    dve.wait_ge(vector_done, eng.at())
                attention(HEADS_TWO, tile2, lambda hd: o2[:, hd.out_tile, :])
                for i in range(4):
                    dve.wait_ge(weights_free[slot_of("y", i)], eng.freed("y", i))
                    dve.wait_ge(scalar_done, eng.at(f"gate {i}"))
                    dst = merged[:, 2 * i:2 * i + 2, :]
                    t = act_tmp[:, 0].rearrange("p (c s) -> p c s", c=2)
                    for br in range(3):
                        b = bank[:, 3 * (i % 2) + br].rearrange("p (c s) -> p c s", c=2)
                        g = gates[:, 8 * br + 2 * i:8 * br + 2 * i + 2, :]
                        tt(t if br else dst, b, g, ALU.mult).then_inc(vector_done, eng.step())
                        dve.wait_ge(vector_done, eng.at())
                        if br:
                            tt(dst, dst, t, ALU.add) \
                                .then_inc(vector_done, eng.step(f"merged {i}" if br == 2 else None))
                            dve.wait_ge(vector_done, eng.at())
                for i in range(4):
                    for c in range(2):
                        k = 2 * i + c
                        if c == 0:
                            dve.wait_ge(tensor_done, eng.at(f"wo {i}"))
                        else:
                            dve.wait_ge(weights_free[slot_of("wo", i)], eng.freed("wo", i))
                        tt(h[:, k, :], bank[:, 2 * (i % 2) + c, 0:S], h[:, k, :], ALU.add) \
                            .then_inc(vector_done, eng.step(f"h wo {k}"))
                        add_square(h[:, k, :], "h up" if k == KT - 1 else None)
                dve.wait_ge(vector_done, eng.at())
                scale_norm("up", lambda k: col(der, 8 + k))
                with eng.turns("up", 4) as t:
                    for i in range(4):
                        dve.wait_ge(scalar_done, eng.at(f"up relu {i}"))
                        tt(up2[:, bass.ds(t * 8 + 2 * i, 2), :].rearrange("p c s -> p (c s)"),
                           act_tmp[:, i % 2], act_tmp[:, i % 2], ALU.mult) \
                            .then_inc(vector_done, eng.step(f"up squared {i}"))
                with eng.turns("dn", 2) as t:
                    for j in range(2):
                        for c in range(2):
                            if c == 0:
                                dve.wait_ge(tensor_done, eng.at(f"dn out {j}"))
                            else:
                                dve.wait_ge(weights_free[slot_of("dn", 4 * j + 3)], eng.freed("dn", 4 * j + 3))
                            hk = h[:, bass.ds(t * 4 + 2 * j + c, 1), :].rearrange("p o s -> p (o s)")
                            tt(hk, bank[:, 2 * j + c, 0:S], hk, ALU.add) \
                                .then_inc(vector_done, eng.step(f"dn h {j} {c}"))
                            add_square(hk, f"dn squares {j} {c}")
            plan.marks["h final"] = plan.marks["dn squares 1 1"]
            dve.wait_ge(vector_done, eng.at())
            scale_norm("final", lambda k: col(norm2, 32 + k))
            eng._close()
    return plan


def kernel(**inputs):
    import concourse.bacc as bacc
    from concourse.bass_utils import run_bass_kernel_spmd

    table, at = constant_tables()
    arrays = {name: np.ascontiguousarray(inputs[name]) for name in IN_NAMES}
    arrays["constants"] = table

    def program(old):
        nc = bacc.Bacc("TRN2", target_bir_lowering=False, num_devices=1)
        dram = {n: nc.dram_tensor(f"in_{n}", a.shape, mybir.dt.from_np(a.dtype), kind="ExternalInput").ap()
                for n, a in arrays.items()}
        out = nc.dram_tensor("out_0", (1, S, D), F32, kind="ExternalOutput").ap()
        return nc, build(nc, dram, out, at, old)

    _, counted = program(Plan())
    nc, _ = program(counted)
    r = run_bass_kernel_spmd(nc, [{f"in_{n}": a for n, a in arrays.items()}], core_ids=[0])
    return r.results[0]["out_0"]
```

```python
from contextlib import ExitStack, contextmanager
import math

import numpy as np
import concourse.bass as bass
from concourse import mybir

F32 = mybir.dt.float32
F32R = mybir.dt.float32r
ALU = mybir.AluOpType
ACT = mybir.ActivationFunctionType
AX = mybir.AxisListType

P = 128
D = 1024
S = 256
L = 2
KT = D // P
D_FF = ((8 * D // 3 + 127) // 128) * 128
FT = D_FF // P
PAIRS = D_FF // 256
EPS = 1e-6
NEG = -1e30
MOD_TILES = 9 * KT
ADA_COLS = 512
ADA_CHUNKS = 9 * D // ADA_COLS
ADA_FIRST = 2 * D // ADA_COLS
RING = 4
SCW = 384
CONV_K = 31
MIXW2 = 24 * 64

R_ADA_B, R_NORM_G, R_CONV_B, R_CONV_G, R_CONV_NB = 0, 72, 96, 98, 100
R_DQ, R_DK, R_FQ, R_FK, R_DO = 102, 103, 104, 105, 106
N_ROWS = 107
O_CW = 128
O_WST = O_CW + 64
O_BS = O_WST + 512
O_GG = O_BS + 256
O_LAM = O_GG + 512
O_WF = O_LAM + 128
O_FB = O_WF + 32
N_PAR = O_FB + 4


def constant_tables():
    at, parts = {}, []

    def put(name, a):
        at[name] = sum(p.shape[1] for p in parts)
        parts.append(np.asarray(a, np.float32).reshape(P, -1))

    r = np.arange(P)
    put("ident", np.eye(P))
    put("ones", np.ones((P, P)))
    put("group32", r[:, None] // 32 == r[None, :] // 32)
    put("group64", r[:, None] // 64 == r[None, :] // 64)
    rot = np.zeros((P, P))
    for base in (0, 64):
        for j in range(8):
            rot[base + 8 + j, base + j] = -1
            rot[base + j, base + 8 + j] = 1
    put("rotate", rot)
    put("neg_suffix", -(r[:, None] >= r[None, :]).astype(np.float32))
    put("neg_ones", -np.ones((P, P)))
    freq = np.exp(-math.log(500000.0) * np.arange(0, 16, 2, dtype=np.float32) / np.float32(16)).astype(np.float32)
    ang = (np.arange(S, dtype=np.float32)[None, :] * freq[:, None]).astype(np.float32).astype(np.float64)
    cos, sin = np.ones((P, S)), np.zeros((P, S))
    for base in (0, 64):
        for half in (0, 8):
            cos[base + half:base + half + 8] = np.cos(ang)
            sin[base + half:base + half + 8] = np.sin(ang)
    put("cos", cos)
    put("sin", sin)

    def by_query(seen):
        m = seen(np.arange(S)[:, None] - np.arange(S)[None, :])
        m = np.where(m, 0.0, NEG)
        return np.concatenate([m[:P, :P], m[P:, :]], axis=1)

    put("causal", by_query(lambda d: d >= 0))
    put("window0", by_query(lambda d: (d >= 0) & (d <= 128)))
    put("window1", by_query(lambda d: (d >= 0) & (d % 4 == 0)))
    put("window2", by_query(lambda d: (d >= 0) & (d % 16 == 0)))
    k, q = np.arange(S)[:, None], np.arange(S)[None, :]
    before = (k < q).astype(np.float32)
    before = np.concatenate([before[:P, :], before[P:, P:]], axis=1)
    put("before", before)
    put("before_neg", np.where(before > 0, 0.0, NEG))
    put("mix_seen", r[:, None] <= r[None, :])
    put("in32", r[:, None] // 32 == np.arange(4)[None, :])
    put("in64", r[:, None] // 64 == np.arange(2)[None, :])
    put("in64_eighth", (r[:, None] // 64 == np.arange(2)[None, :]) * 0.125)
    put("cum_row", r[:, None] == 32 * np.arange(4)[None, :])
    put("one_row", r[:, None] == 32 * np.arange(4)[None, :] + 1)
    put("neg_cum_rows", -(r[:, None] % 32 == 1).astype(np.float32))
    put("one_rows", r[:, None] % 32 == 0)
    put("eps", np.full((P, 1), EPS))
    init = [0.8 - 0.6 * math.exp(-0.3 * l) for l in range(L)]
    put("lam_init", np.tile([[x, 1 - x] for x in init], (P, 1, 1)).reshape(P, 2 * L))
    table = np.concatenate(parts, axis=1)
    return np.ascontiguousarray(table), at


class Plan:

    def __init__(self):
        self.totals, self.bodies, self.marks = {}, {}, {}


PARTS = ("pre", "one", "two", "post")
TIMES = {"pre": 1, "one": L, "two": L, "post": 1}


class Engine:

    def __init__(self, e, own, plan, old):
        self.e, self.own, self.plan, self.old = e, own, plan, old
        self.part, self.layer = "pre", None
        self.loop, self.turn = None, None
        self.count = {}

    @contextmanager
    def layers(self, part):
        self._close()
        self.part, self.count = part, {}
        with self.e.Fori(0, L) as layer:
            self.layer = layer
            yield layer
            self._close()
        self.layer = None
        self.part, self.count = PARTS[PARTS.index(part) + 1], {}

    def _close(self):
        for k, v in self.count.items():
            self.plan.totals[k, self.part] = v

    def step(self, mark=None, sem=None, by=1):
        s = sem or self.own
        k = s.name
        self.count[k] = self.count.get(k, 0) + by
        if mark:
            self.plan.marks[mark] = (s, self.part, self.count[k], self.loop)
        return by

    def _value(self, s, part, local, loop, back=0):
        old, k = self.old, s.name
        value = sum(old.totals.get((k, q), 0) * TIMES[q] for q in PARTS[:PARTS.index(part)]) + local
        least = value
        if TIMES[part] > 1:
            total = old.totals.get((k, part), 0)
            value = value + (self.layer * total if part == self.part else (L - 1) * total)
        if loop:
            body = old.bodies.get((k, part, loop), 0)
            if loop == self.loop:
                value = value + self.turn * body
                least -= back * body
                if back:
                    value = value - back * body
            else:
                value = value + (old.bodies.get(loop, 1) - 1 - back) * body
        if not old.totals:
            return 1
        assert least > 0, (k, part, local, loop)
        return value

    def _count(self, phase, n, per_layer, before, per_turn):
        n = n + (before if phase in TWO else 0)
        if self.layer is not None:
            n = self.layer * per_layer + n
        return n if self.loop is None else self.turn * per_turn + n

    def split_chunk(self, phase, i):
        return self._count(phase, SPLIT_START[phase] + i, SPLIT_CHUNKS["one" if phase in ONE else "two"],
                           L * SPLIT_CHUNKS["one"], PER_TURN.get(self.loop))

    def freed(self, phase, i, before=False):
        return self._count(phase, (START[phase] + i) // RING + (1 if before else 2),
                           CHUNKS["one" if phase in ONE else "two"] // RING, L * CHUNKS["one"] // RING,
                           PER_TURN.get(self.loop, 0) // RING)

    def arrived(self, phase, i):
        n = START[phase] + i
        y = 2 if phase in TWO else 0
        loads = n // RING + 1 + (y if phase in TWO and n >= START["y"] else 0)
        return self._count(phase, 16 * loads, 16 * (CHUNKS["one" if phase in ONE else "two"] // RING + y),
                           16 * (L * CHUNKS["one"] // RING), 16 * PER_TURN.get(self.loop, 0) // RING)

    def at(self, mark=None, back=0):
        if mark is None:
            return self._value(self.own, self.part, self.count.get(self.own.name, 0), self.loop)
        if not self.old.marks:
            return 1
        s, part, local, loop = self.old.marks[mark]
        return self._value(s, part, local, loop, back)

    @contextmanager
    def turns(self, name, n):
        start = dict(self.count)
        with self.e.Fori(0, n) as turn:
            self.loop, self.turn = name, turn
            yield turn
        for k, v in list(self.count.items()):
            body = v - start.get(k, 0)
            self.plan.bodies[k, self.part, name] = body
            self.count[k] = v + (n - 1) * body
        self.plan.bodies[name] = max(n, self.plan.bodies.get(name, 0))
        self.loop = self.turn = None


ONE = {"f1in": 2 * PAIRS, "f1out": 16, "z": 12, "o": 4, "f2in": 2 * PAIRS, "f2out": 16}
TWO = {"z2": 32, "y": 4, "wo": 4, "up": 16, "dn": 16}
CHUNKS = {"one": sum(ONE.values()), "two": sum(TWO.values())}
assert CHUNKS["one"] % RING == 0 and CHUNKS["two"] % RING == 0
START = {}
for _phases in (ONE, TWO):
    _at = 0
    for _name, _n in _phases.items():
        START[_name] = _at
        _at += _n
FF_PARTS = ((0, 6), (6, 6), (12, 5), (17, 5))
DN_PARTS = ((0, 8), (8, 8), (16, 8), (24, 8))
assert sum(n for _, n in FF_PARTS) == FT

SPLIT_START = {"f1in": 0, "z": ONE["f1in"], "f2in": ONE["f1in"] + ONE["z"], "z2": 0, "up": TWO["z2"]}
SPLIT_CHUNKS = {"one": 2 * ONE["f1in"] + ONE["z"], "two": TWO["z2"] + TWO["up"]}
PER_TURN = {"f1in": 4, "f1out": 8, "f2in": 4, "f2out": 8, "up": 4, "dn": 8}

Z_UNITS = (("ca", (0, 1), 768, False), ("cg", (2, 3), 1024, False), ("dq", (4,), 0, False), ("dk", (5,), 256, False),
           ("dv", (6,), 512, True), ("fq", (7,), 1792, False), ("fk", (8,), 2048, False), ("fv", (9,), 2304, True),
           ("gu", (10,), 1280, False), ("gv", (11,), 1536, True))
FOX_F0 = 2560
Z2_UNITS = tuple((f"{'qkvgg'[i // 6]}{i if i >= 18 else i % 6}", (2 * i, 2 * i + 1) if i < 2 else (i + 2,),
                  256 * i, 12 <= i < 18) for i in range(30))


def slot_of(phase, i):
    return (START[phase] + i) % RING


def split_slot(phase, i):
    return (SPLIT_START[phase] + i) % 2


def k_tiles(phase, i):
    return 4 if phase[0] == "z" and i < 4 else 8


class Head:

    def __init__(self, name, kind, maps, out_tile, half):
        self.name, self.kind, self.maps, self.out_tile, self.half = name, kind, maps, out_tile, half


HEADS_ONE = [Head(f"d{h}", "diff", [(4 * (h // 2) + 2 * (h % 2) + c, h // 2, h // 2, "causal") for c in range(2)],
                  h // 2, h % 2) for h in range(4)]
HEADS_ONE += [Head(f"x{h}", "fox", [(h, h // 2, h // 2, "causal")], h // 2, h % 2) for h in range(4)]
HEADS_TWO = [Head(f"a{j}", "soft", [(4 * g + j, (4 * g + j) // 2, (4 * g + j) // 2, f"window{g}") for g in range(3)],
                  j // 2, j % 2) for j in range(4)]
HEADS_TWO += [Head(f"b{j}", "soft", [(12 + j, (12 + j) // 2, (12 + j) // 2, "causal")], 2 + j // 2, j % 2)
              for j in range(6)]
HEADS_TWO += [Head(f"c{j}", "stick", [(18 + j, (18 + j) // 2, (18 + j) // 2, None)], 5 + j // 2, j % 2)
              for j in range(6)]
ARENA = 20480 + 2 * 6 * SCW


def lag(heads, j):
    return 1 if len(heads[j].maps) == 3 else 2


STEPS_AFTER = 3
SLOTS = 6


def place_heads(heads):
    n = {"two banks": 0, "four banks": 0, "tp": 0, "pb": 0, "ps": 0}
    last = {}

    def take(kind, size, frees):
        i = n[kind] % size
        n[kind] += 1
        if kind in ("two banks", "four banks"):
            kind, i = "sb", (2, 3, 0, 1)[i]
        before = last.get((kind, i))
        last[kind, i] = frees
        return i, before

    for u, h in enumerate(heads):
        h.u, h.pair = u, u // 2
        if h.kind == "stick":
            h.sb = [take("two banks", 2, f"sp {h.name}")]
            h.tp = [take("tp", SLOTS, f"copied {h.name} 0"), take("tp", SLOTS, f"arg {h.name}")]
            h.pb = [take("pb", 2, f"argm {h.name}")]
            h.ps = [take("ps", SLOTS, f"out {h.name}")]
        else:
            turned = 1 if h.kind == "diff" else len(h.maps)
            kind, size = ("four banks", 4) if h.kind == "diff" else ("two banks", 2)
            h.sb = [take(kind, size, f"max {h.name} {m}") for m in range(len(h.maps))]
            h.tp = [take("tp", SLOTS, f"turned {h.name} {min(m, turned - 1)}") for m in range(len(h.maps))]
            h.pb = [take("pb", 2, f"copied {h.name} {m}") for m in range(turned)]
            h.ps = [take("ps", SLOTS, f"out {h.name}") for m in range(turned)]
    return heads


place_heads(HEADS_ONE)
place_heads(HEADS_TWO)

IN_NAMES = ["x", "c", "ada_w", "ada_b", "norm_g", "ffn1_w_in", "ffn1_w_out", "ffn2_w_in", "ffn2_w_out", "w_in",
            "w_out", "diff_qk_g", "diff_lambda", "diff_out_g", "conv_w", "conv_b", "conv_norm_g", "conv_norm_b",
            "gmlp_norm_g", "gmlp_norm_b", "gmlp_ws", "gmlp_bs", "fox_qk_g", "fox_fb", "norm_mix_2", "w_in_2",
            "w_out_a_2", "w_out_b_2", "w_out_c_2", "w_o_2", "norm_mlp_2", "w_up_2", "w_down_2", "norm_final_2"]


def build(nc, dram, out, at, old):
    plan = Plan()
    with ExitStack() as ctx:
        def sb(name, *shape, dtype=F32):
            return ctx.enter_context(nc.sbuf_tensor(name, [P, *shape], dtype))

        def sem(name):
            return ctx.enter_context(nc.semaphore(name))

        bank = ctx.enter_context(nc.psum_tensor("bank", [P, 8, 512], F32))
        ring = sb("ring", RING, 8, 256)
        w_hi, w_lo = sb("w_hi", 2, 8, 256, dtype=F32R), sb("w_lo", 2, 8, 256, dtype=F32R)
        h = sb("h", KT, S)
        hn, hn_lo = sb("hn", KT, S, dtype=F32R), sb("hn_lo", KT, S, dtype=F32R)
        normed = sb("normed", 2, S)
        square_sum = sb("square_sum", S)
        rstd = sb("rstd", S)
        n_const = dram["constants"].shape[1]
        const = sb("const", n_const)
        mod = sb("mod", MOD_TILES)
        der = sb("der", 64)
        cond = sb("cond", KT)
        norm2 = sb("norm2", 40)
        stat = sb("stat", 4, 16)
        small = sb("small", 64)
        arena = sb("arena", ARENA)

        def view(start, *dims):
            n = int(np.prod(dims))
            assert start + n <= ARENA
            v = arena[:, start:start + n]
            names = " ".join(f"d{i}" for i in range(len(dims)))
            if len(dims) == 1:
                return v
            return v.rearrange(f"p ({names}) -> p {names}", **{f"d{i}": d for i, d in enumerate(dims[1:], 1)})

        act_tmp = view(ARENA - 1024, 2, 512)
        ada_acc = view(ARENA - 2048, 2, ADA_COLS)
        wfx = view(ARENA - 2048, KT, P)
        par_at = ARENA - 2048 - L * N_PAR
        par_all = view(par_at, L, N_PAR)
        par = par_all[:, 0]
        ada = view(0, 2, 8, ADA_COLS)
        gated = view(8192, FT, S)
        x_rows = view(8192 + 2048, 2, D)
        tile1, turned1 = view(0, SLOTS, SCW), view(SLOTS * SCW, SLOTS, SCW)
        o = 2 * SLOTS * SCW
        place = {}
        for name, dims in (("qd", (8, S)), ("kd", (2, S)), ("vd", (2, S)), ("qf", (4, S)), ("kf", (2, S)),
                           ("vf", (2, S)), ("mix", (8, S)), ("fa", (4, S)), ("fb", (S,)), ("yp", (2, 288)), ("cv", (2, S)),
                           ("u", (2, S)), ("vg", (2, S)), ("ft", (3, S)), ("od", (2, S)),
                           ("cg", (2, S)), ("cd", (2, S)), ("qs", (2, 2 * S)), ("rr", (2, 2 * S))):
            place[name] = view(o, *dims)
            o += int(np.prod(dims))
        assert o <= par_at, o
        qd, kd, vd, qf, kf, vf, mix, fa, fb, yp, cv, u_, vg, ft, od, cg, cd, qs, rr = place.values()
        rows = view(8192, L, P)
        rows_cw = view(8192 + 256, L, P)
        rows_ws = view(8192 + 512, L, 4, P)
        rows_n2 = view(8192 + 1536, P)
        rows_c = view(8192 + 1664, P)
        q2 = view(0, 24, S)
        k2 = view(6144, 12, S)
        v2 = view(9216, 2, MIXW2)
        gates = view(12288, 24, S)
        o2 = view(18432, KT, S)
        merged = view(9216, KT, S)
        up2 = view(0, 32, S)
        tile2, turned2 = view(20480, SLOTS, SCW), view(20480 + SLOTS * SCW, SLOTS, SCW)
        raw, rot_tmp = view(20480, 2, 2 * S), view(20480 + 4 * S, 2, 2 * S)
        result, result_rows = view(0, KT, S), view(KT * S, 2, D)

        def tab(name, n=P, off=0):
            return const[:, at[name] + off:at[name] + off + n]

        ident, ones = tab("ident"), tab("ones")
        eps = tab("eps", 1)

        tensor_done, scalar_done = sem("tensor_done"), sem("scalar_done")
        vector_done, pool_done = sem("vector_done"), sem("pool_done")
        weights_used = sem("weights_used")
        silu_done, relu_done = sem("silu_done"), sem("relu_done")
        weights_rounded, weights_split = sem("weights_rounded"), sem("weights_split")
        weights_free = [sem(f"weights_free_{i}") for i in range(RING)]
        weights_in = [sem(f"weights_in_{i}") for i in range(RING)]
        ada_in = [sem("ada_in_0"), sem("ada_in_1")]
        first_ada_in = [sem("first_ada_in_0"), sem("first_ada_in_1")]
        ada_summed, ada_reduced = sem("ada_summed"), sem("ada_reduced")
        x_in, params_in, tables_in, stored = sem("x_in"), sem("params_in"), sem("tables_in"), sem("stored")

        passed = [sem("tensor_passed"), sem("vector_passed"), sem("sync_passed")]

        def done_by(mark):
            return {"turned": tensor_done, "arg": tensor_done, "out": tensor_done, "copied": scalar_done,
                    "max": vector_done, "sp": vector_done, "argm": vector_done}[mark.split()[0]]

        block = ctx.enter_context(nc.Block())

        assert L == 2
        ADA_PRE = ADA_FIRST
        ADA_REST = ADA_CHUNKS - ADA_FIRST
        n_params = [0]
        n_params_total = 1 + L * (4 + 1 + 5 + 1 + 1 + 1 + 4 + 2 + 1 + 1) + 3

        @block.sync
        def _(sp):
            eng = Engine(sp, weights_used, plan, old)
            sp.dma_start(x_rows,
                         dram["x"][0].rearrange("(t p) d -> p t d", p=P)).then_inc(x_in, 16)

            def ada_fill(n, j, layer, first_col):
                source = dram["ada_w"][bass.ds(layer, 1), :, bass.ds(first_col, ADA_COLS)] \
                    .rearrange("o (k p) n -> p (o k) n", p=P)
                sp.wait_ge(ada_summed, n - 1)
                sp.dma_start(ada[:, j], source).then_inc(ada_in[j], 16)

            def fill(phase, i, nk, *sources):
                s = slot_of(phase, i)
                sp.wait_ge(weights_free[s], eng.freed(phase, i, before=True))
                sp.sem_inc(passed[2], 1)
                k = 0
                for src in sources:
                    n = src.shape[1]
                    assert k + n <= nk
                    sp.dma_start(ring[:, s, k:k + n, :], src).then_inc(weights_in[s], 16)
                    k += n

            def chunk(w, layer, k0, nk, col):
                return w[bass.ds(layer, 1), k0 * P:(k0 + nk) * P, col].rearrange("o (k p) n -> p (o k) n", p=P)

            def ffn(s, w_in, w_out, layer, n0):
                with eng.turns(s + "in", PAIRS // 2) as t:
                    for i in range(4):
                        fill(s + "in", i, 8,
                             chunk(w_in, layer, 0, 8, bass.ds(t * 512 + (i // 2) * 256 + (i % 2) * D_FF, 256)))
                        if s == "f1" and i % 2:
                            ada_fill(n0 + t * 2 + i // 2, i // 2, layer,
                                     t * (2 * ADA_COLS) + (ADA_FIRST + i // 2) * ADA_COLS)
                for i in (2 * PAIRS - 2, 2 * PAIRS - 1):
                    c = 256 * (PAIRS - 1) + (i % 2) * D_FF
                    fill(s + "in", i, 8, chunk(w_in, layer, 0, 8, slice(c, c + 256)))
                with eng.turns(s + "out", 2) as t:
                    for i in range(8):
                        if i % 4 == 0 and s == "f1":
                            ada_fill(n0 + t * 2 + 10 + i // 4, i // 4, layer,
                                     t * (2 * ADA_COLS) + (ADA_FIRST + 10 + i // 4) * ADA_COLS)
                        elif i % 4 == 0:
                            ada_fill(n0 + t * 2 + ADA_REST + i // 4, i // 4, layer * -1 + (L - 1),
                                     t * (2 * ADA_COLS) + (i // 4) * ADA_COLS)
                        k0, nk = FF_PARTS[i % 4]
                        fill(s + "out", i, nk,
                             chunk(w_out, layer, k0, nk, bass.ds(t * 512 + (i // 4) * 256, 256)))

            with eng.layers("one") as layer:
                ffn("f1", dram["ffn1_w_in"], dram["ffn1_w_out"], layer, layer * ADA_CHUNKS + ADA_PRE)
                for _, chunks, col, _ in Z_UNITS:
                    for j, i in enumerate(chunks):
                        nk = 8 // len(chunks)
                        fill("z", i, nk, chunk(dram["w_in"], layer, nk * j, nk, slice(col, col + 256)))
                for i in range(4):
                    fill("o", i, 8, chunk(dram["w_out"], layer, 0, 8, slice(256 * i, 256 * i + 256)))
                ffn("f2", dram["ffn2_w_in"], dram["ffn2_w_out"], layer, layer * ADA_CHUNKS + ADA_PRE)
            with eng.layers("two") as layer:
                for _, chunks, col, _ in Z2_UNITS:
                    for j, i in enumerate(chunks):
                        nk = 8 // len(chunks)
                        fill("z2", i, nk, chunk(dram["w_in_2"], layer, nk * j, nk, slice(col, col + 256)))
                for i in range(4):
                    c = slice(256 * i, 256 * i + 256)
                    fill("y", i, 8, chunk(dram["w_out_a_2"], layer, 0, 2, c),
                         chunk(dram["w_out_b_2"], layer, 0, 3, c), chunk(dram["w_out_c_2"], layer, 0, 3, c))
                for i in range(4):
                    fill("wo", i, 8, chunk(dram["w_o_2"], layer, 0, 8, slice(256 * i, 256 * i + 256)))
                with eng.turns("up", 4) as t:
                    for i in range(4):
                        fill("up", i, 8,
                             chunk(dram["w_up_2"], layer, 0, 8, bass.ds(t * 1024 + i * 256, 256)))
                with eng.turns("dn", 2) as t:
                    for i in range(8):
                        k0, nk = DN_PARTS[i % 4]
                        fill("dn", i, nk,
                             chunk(dram["w_down_2"], layer, k0, nk, bass.ds(t * 512 + (i // 4) * 256, 256)))
            for t in range(2):
                sp.wait_ge(scalar_done, eng.at(f"result {t}"))
                sp.dma_start(out[0, t * P:(t + 1) * P, :],
                             result_rows[:, t]).then_inc(stored, 16)
            sp.wait_ge(stored, 32)

        @block.gpsimd
        def _(pool):
            eng = Engine(pool, pool_done, plan, old)
            for n in range(ADA_PRE):
                if n >= 2:
                    pool.wait_ge(ada_summed, n - 1)
                pool.dma_start(ada[:, n % 2], dram["ada_w"][0, :, n * ADA_COLS:(n + 1) * ADA_COLS]
                               .rearrange("(k p) n -> p k n", p=P)).then_inc(first_ada_in[n % 2], 16)

            def split(phase, i):
                r, q, n = slot_of(phase, i), split_slot(phase, i), k_tiles(phase, i) // 2
                for half, done in enumerate((weights_split, weights_free[r])):
                    ks = slice(half * 4, half * 4 + n)
                    pool.wait_ge(weights_rounded, eng.split_chunk(phase, i) * 2 + half + 1)
                    pool.tensor_tensor(w_lo[:, q, ks], ring[:, r, half * n:half * n + n], w_hi[:, q, ks], ALU.subtract) \
                        .then_inc(done, 1)

            def ffn_in(phase):
                with eng.turns(phase, PAIRS // 2):
                    for i in range(4):
                        split(phase, i)
                for i in (2 * PAIRS - 2, 2 * PAIRS - 1):
                    split(phase, i)

            with eng.layers("one"):
                ffn_in("f1in")
                for i in range(ONE["z"]):
                    split("z", i)
                ffn_in("f2in")
            with eng.layers("two"):
                for i in range(TWO["z2"]):
                    split("z2", i)
                with eng.turns("up", 4):
                    for i in range(4):
                        split("up", i)
            eng._close()

        @block.tensor
        def _(pe):
            eng = Engine(pe, tensor_done, plan, old)
            mm = pe.matmul
            for slot in weights_free:
                pe.sem_inc(slot, 1)
            pe.sem_inc(weights_used, eng.step(None, weights_used, 4))

            def turn(dst, src, mark=None):
                n = src.shape[0]
                i = pe.transpose(dst, src, ident[0:n, 0:n])
                if mark:
                    i.then_inc(tensor_done, eng.step(mark))

            def terms(out, w, w_lo, x, x_lo, token_major, start, stop):
                for i, (a, b) in enumerate(((w, x), (w, x_lo), (w_lo, x))):
                    if token_major:
                        a, b = b, a
                    last = mm(out, a, b, start=start and i == 0, stop=stop and i == 2)
                return last

            def product(phase, chunks, outs, token_major=False, free=(), first=None):
                for by, mark, back in free:
                    pe.wait_ge(by, eng.at(mark, back))
                for c in range(2):
                    ws, xs = (slice(0, 256), slice(c * P, (c + 1) * P)) if token_major \
                        else (slice(c * P, (c + 1) * P), slice(0, S))
                    for j, i in enumerate(chunks):
                        r, q, n = slot_of(phase, i), split_slot(phase, i), k_tiles(phase, i) // 2
                        for half in range(2):
                            if c == 0 and half == 0:
                                pe.wait_ge(weights_split, eng.split_chunk(phase, i) + 1)
                            elif c == 0:
                                pe.wait_ge(weights_free[r], eng.freed(phase, i))
                            for k in range(half * n, half * n + n):
                                kx = 2 * n * j + k
                                if first and c == 0:
                                    pe.wait_ge(vector_done, eng.at(f"split {first} {kx}"))
                                kw = half * 4 + k - half * n
                                last = terms(outs[c], w_hi[:, q, kw, ws], w_lo[:, q, kw, ws], hn[:, kx, xs],
                                             hn_lo[:, kx, xs], token_major, kx == 0, kx == KT - 1)
                            if c == 1:
                                last.then_inc(weights_used, eng.step(f"used {phase} {i}" if half else
                                                                     f"half used {phase} {i}", weights_used))

            def plain_product(phase, chunks, x, outs, done, parts=((0, KT),), free=()):
                total = sum(n for _, n in parts)
                for i, (k0, nk) in zip(chunks, parts):
                    s = slot_of(phase, i)
                    for c in range(2):
                        if i == chunks[0]:
                            for by, mark, back in free[c:c + 1]:
                                pe.wait_ge(by, eng.at(mark, back))
                        if c == 0:
                            pe.wait_ge(weights_in[s], eng.arrived(phase, i))
                        for k in range(nk):
                            last = mm(outs[c], ring[:, s, k, c * P:(c + 1) * P], x[:, k0 + k, :],
                                      start=(k0 + k == 0), stop=(k0 + k == total - 1))
                        if c == 1:
                            last.then_inc(weights_free[s], 1)
                        elif i == chunks[-1]:
                            last.then_inc(tensor_done, eng.step(done))

            def norm_sum(n):
                pe.wait_ge(vector_done, eng.at("layer params" if n == "f1" else f"h {n}"))
                mm(bank[:, 4, 0:S], ones, square_sum[:], start=True, stop=True) \
                    .then_inc(tensor_done, eng.step(f"sum {n}"))

            def ada_reduce(n, slot, col):
                pe.wait_ge(ada_summed, n + 1)
                for j in range(4):
                    last = mm(bank[:, 7, bass.ds(col + j, 1)], ada_acc[:, slot, j * P:(j + 1) * P], ones[:, 0:1],
                              start=True, stop=True)
                last.then_inc(ada_reduced, 1)

            pe.wait_ge(tables_in, 32)
            turn(bank[:, 4, 0:KT], rows_c[0:KT], "c turned")
            pe.wait_ge(x_in, 16)
            for k in range(KT):
                for t in range(2):
                    turn(bank[:, k // 2, (k % 2) * S + t * P:(k % 2) * S + (t + 1) * P], x_rows[:, t, k * P:(k + 1) * P],
                         f"x turned {k // 2}" if k % 2 and t else None)
            for n in range(ADA_PRE):
                ada_reduce(n, n % 2, 4 * n)
            pe.wait_ge(params_in, 16 * n_params_total)
            for l in range(L):
                turn(bank[:, 5, l * P:l * P + N_ROWS], rows[0:N_ROWS, l])
                turn(bank[:, 5, 256 + l * 64:256 + l * 64 + 62], rows_cw[0:62, l])
            turn(bank[:, 5, 384:424], rows_n2[0:40], "rows turned")
            for l in range(L):
                if l:
                    pe.wait_ge(vector_done, eng.at("mix weights 0"))
                for j in range(4):
                    turn(bank[:, 6, j * P:(j + 1) * P], rows_ws[:, l, j], f"ws turned {l}" if j == 3 else None)

            def ffn(s, n0):
                with eng.turns(s + "in", PAIRS // 2) as t:
                    for j in range(2):
                        for r in range(2):
                            b = bank[:, 2 * j + r].rearrange("p (c s) -> p c s", c=2)
                            product(s + "in", (2 * j + r,), (b[:, 0], b[:, 1]),
                                    first=None if j or r else s,
                                    free=(((silu_done, f"{s} silu {j}", 1), (vector_done, f"{s} gated {j}", 1))[r],))
                        if s == "f1":
                            ada_reduce(n0 + t * 2 + j, j, t * 8 + 16 + 4 * j)
                for r in range(2):
                    b = bank[:, r].rearrange("p (c s) -> p c s", c=2)
                    product(s + "in", (2 * PAIRS - 2 + r,), (b[:, 0], b[:, 1]),
                            free=(((silu_done, f"{s} silu 0", 0), (vector_done, f"{s} gated 0", 0))[r],))
                pe.wait_ge(vector_done, eng.at(f"{s} gated last"))
                pe.sem_inc(passed[0], 1)
                with eng.turns(s + "out", 2) as t:
                    for j in range(2):
                        plain_product(s + "out", tuple(range(4 * j, 4 * j + 4)), gated,
                                (bank[:, 2 * j, 0:S], bank[:, 2 * j + 1, 0:S]), f"{s} out {j}", parts=FF_PARTS,
                                free=((vector_done, f"{s} h {j} 0", 1), (vector_done, f"{s} h {j} 1", 1)))
                        if s == "f1":
                            ada_reduce(n0 + t * 2 + 10 + j, j, t * 8 + 56 + 4 * j)
                        else:
                            ada_reduce(n0 + t * 2 + ADA_REST + j, j, t * 8 + 4 * j)

            def scores(hd, q, k):
                for m, (qi, ki, _, _) in enumerate(hd.maps):
                    sbk, free = hd.sb[m]
                    if free:
                        pe.wait_ge(vector_done, eng.at(free))
                    b = bank[:, sbk]
                    if hd.kind == "stick":
                        mm(b[:, 0:256], k[:, ki, 0:P], q[:, qi, :], start=True, stop=True)
                        last = mm(b[:, 256:384], k[:, ki, P:S], q[:, qi, P:S], start=True, stop=True)
                    else:
                        fox = hd.kind == "fox"
                        for c0, c1, n in ((0, P, P), (P, SCW, S)):
                            qq = slice(0, P) if c0 == 0 else slice(P, S)
                            last = mm(b[:, c0:c1], q[:, qi, qq], k[:, ki, 0:n], start=True, stop=not fox)
                            if fox:
                                last = mm(b[:, c0:c1], fa[:, qi, qq], fb[:, 0:n], start=False, stop=True)
                    last.then_inc(tensor_done, eng.step(f"scores {hd.name} {m}"))

            def turned(hd, q, k, tile):
                if hd.kind == "stick":
                    (qi, ki, _, _), (pb, free) = hd.maps[0], hd.pb[0]
                    if free:
                        pe.wait_ge(done_by(free), eng.at(free))
                    b, sp_ = bank[:, 4 + pb], tile[:, hd.tp[1][0], :]
                    mm(b[:, 0:256], k[:, ki, 0:P], q[:, qi, :], start=True, stop=False)
                    pe.wait_ge(vector_done, eng.at(f"sp {hd.name}"))
                    mm(b[:, 0:256], tab("neg_suffix"), sp_[:, 0:256], start=False, stop=False)
                    mm(b[:, 128:256], tab("neg_ones"), sp_[:, 256:384], start=False, stop=True)
                    mm(b[:, 256:384], k[:, ki, P:S], q[:, qi, P:S], start=True, stop=False)
                    mm(b[:, 256:384], tab("neg_suffix"), sp_[:, 256:384], start=False, stop=True) \
                        .then_inc(tensor_done, eng.step(f"arg {hd.name}"))
                    return
                pe.wait_ge(vector_done, eng.at(f"scaled {hd.name}"))
                for m in range(len(hd.pb)):
                    pb, free = hd.pb[m]
                    if free:
                        pe.wait_ge(scalar_done, eng.at(free))
                    for j in range(3):
                        turn(bank[:, 4 + pb, j * P:(j + 1) * P], tile[:, hd.tp[m][0], j * P:(j + 1) * P],
                             f"turned {hd.name} {m}" if j == 2 else None)

            def outputs(hd, v, tt, evacuated):
                if evacuated and hd.half == 0:
                    pe.wait_ge(vector_done, eng.at(evacuated))
                b = bank[:, 6 + hd.pair % 2].rearrange("p (a s) -> p a s", a=2)[:, hd.half]
                n = len(hd.ps)
                for m in range(n):
                    pe.wait_ge(scalar_done, eng.at(f"copied {hd.name} {m}"))
                    vt = hd.maps[m][2]
                    p_ = tt[:, hd.ps[m][0]]
                    mm(b[:, 0:S], v[:, 0, vt * P:(vt + 1) * P], p_[:, 0:S], start=(m == 0), stop=False)
                    last = mm(b[:, P:S], v[:, 1, vt * P:(vt + 1) * P], p_[:, S:SCW], start=False, stop=(m == n - 1))
                last.then_inc(tensor_done, eng.step(f"out {hd.name}"))

            def attention(heads, q_of, tile, tt, filler):
                for i in range(len(heads) + STEPS_AFTER):
                    if i < len(heads):
                        scores(heads[i], *q_of(heads[i])[:2])
                    filler(i)
                    for j, hd in enumerate(heads):
                        if j + lag(heads, j) == i:
                            turned(hd, *q_of(hd)[:2], tile)
                    for j, hd in enumerate(heads):
                        if j + lag(heads, j) + 1 == i:
                            outputs(hd, q_of(hd)[2], tt,
                                    f"heads {heads[0].name} {hd.pair - 2}" if hd.pair >= 2 else None)

            with eng.layers("one") as layer:
                n0 = layer * ADA_CHUNKS + ADA_PRE
                norm_sum("f1")
                ffn("f1", n0)
                norm_sum("z")
                z_free = {"dv": (vector_done, "conv in", 0), "fq": (scalar_done, "conv gate", 0),
                          "fk": (vector_done, "dq scaled", 0), "fv": (vector_done, "dk scaled", 0),
                          "gu": (scalar_done, "dv copied", 0), "gv": (vector_done, "fq scaled", 0)}

                def z_unit(i):
                    name, chunks, _, tm = Z_UNITS[i]
                    b = bank[:, i % 4].rearrange("p (c s) -> p c s", c=2)
                    product("z", chunks, (b[:, 0], b[:, 1]), token_major=tm,
                            first="z" if i == 0 else None,
                            free=(z_free[name],) if name in z_free else ())

                def group_sum(name, group, b):
                    pe.wait_ge(scalar_done, eng.at(f"{name} squares"))
                    mm(bank[:, b], tab(group), qs[:, 0 if name in ("dq", "fq", "od") else 1, :],
                       start=True, stop=True).then_inc(tensor_done, eng.step(f"{name} sum"))

                for i in range(4):
                    z_unit(i)
                group_sum("dq", "group32", 5)
                z_unit(4)
                group_sum("dk", "group32", 6)
                z_unit(5)
                z_unit(6)
                pe.wait_ge(scalar_done, eng.at("dq rstd"))
                group_sum("fq", "group64", 5)
                z_unit(7)
                pe.wait_ge(scalar_done, eng.at("dk rstd"))
                group_sum("fk", "group64", 6)
                pe.wait_ge(vector_done, eng.at("forget weights"))
                for k in range(KT):
                    for i, x in enumerate((hn, hn_lo)):
                        last = mm(bank[:, 4, 0:S], wfx[:, k, :], x[:, k, :].bitcast(F32),
                                  start=(k == 0 and i == 0), stop=(k == KT - 1 and i == 1))
                last.then_inc(tensor_done, eng.step("forget sum"))
                for i in range(8, 10):
                    z_unit(i)
                pe.wait_ge(vector_done, eng.at("gate normed"))
                pe.wait_ge(scalar_done, eng.at("u"))
                for j in range(4):
                    for c in range(2):
                        last = mm(bank[:, j // 2].rearrange("p (a c s) -> p a c s", a=2, c=2)[:, j % 2, c],
                                  vg[:, c, (j // 2) * P:(j // 2 + 1) * P],
                                  par[:, O_WST + j * P:O_WST + (j + 1) * P], start=True, stop=True)
                    if j % 2:
                        last.then_inc(tensor_done, eng.step(f"mixed {j // 2}"))
                pe.wait_ge(vector_done, eng.at("forget rows"))
                pe.wait_ge(vector_done, eng.at("fk scaled"))

                def between(i):
                    if i == 0:
                        pe.wait_ge(vector_done, eng.at("mixed out"))
                    if i == 5:
                        pe.wait_ge(vector_done, eng.at("max d3 1"))
                        for j in range(2):
                            last = mm(bank[:, 0, 0:S], ones, cv[:, j, :], start=(j == 0), stop=(j == 1))
                        last.then_inc(tensor_done, eng.step("conv mean"))
                    if i == 6:
                        pe.wait_ge(scalar_done, eng.at("conv squares"))
                        for j in range(2):
                            last = mm(bank[:, 1, 0:S], ones, cg[:, j, :], start=(j == 0), stop=(j == 1))
                        last.then_inc(tensor_done, eng.step("conv var"))
                    if i == 8:
                        pe.wait_ge(vector_done, eng.at("conv centred"))
                        group_sum("od", "group64", 0)

                attention(HEADS_ONE, lambda hd: (qd, kd, vd) if hd.kind == "diff" else (qf, kf, vf),
                          tile1, turned1, between)
                pe.wait_ge(vector_done, eng.at("heads d0 3"))
                pe.wait_ge(vector_done, eng.at("od normed"))
                pe.wait_ge(scalar_done, eng.at("conv done"))
                for i in range(4):
                    plain_product("o", (i,), mix, (bank[:, 2 * (i % 2), 0:S], bank[:, 2 * (i % 2) + 1, 0:S]), f"o {i}",
                                  free=((vector_done, f"h o {2 * i - 4}", 0), (vector_done, f"h o {2 * i - 3}", 0))
                                  if i >= 2 else ())
                norm_sum("f2")
                ffn("f2", n0)

            with eng.layers("two") as layer:
                norm_sum("z2")

                def z2_unit(i):
                    name, chunks, _, tm = Z2_UNITS[i]
                    b = bank[:, i % 4] if i < 18 else bank[:, i % 2]
                    b = b.rearrange("p (c s) -> p c s", c=2)
                    free = ()
                    if 4 <= i:
                        free = ((scalar_done, f"z2 out {i - 4 if i < 18 else i - 2}", 0),)
                    product("z2", chunks, (b[:, 0], b[:, 1]), token_major=tm, free=free,
                            first="z2" if i == 0 else None)

                def rotate(i):
                    pe.wait_ge(scalar_done, eng.at(f"z2 out {i}"))
                    if i >= 2 and i not in (6, 7):
                        pe.wait_ge(vector_done, eng.at(f"rotated {i - 2}"))
                    if i in (6, 7):
                        pe.wait_ge(vector_done, eng.at(f"rotated {i - 3}"))
                    mm(bank[:, 5 + i % 2], tab("rotate"), raw[:, i % 2, :], start=True, stop=True) \
                        .then_inc(tensor_done, eng.step(f"rotary {i}"))

                for i in range(18):
                    z2_unit(i)
                    if 1 <= i <= 12 and (i - 1) not in (5, 11):
                        rotate(i - 1)
                pe.wait_ge(vector_done, eng.at("rotated 10"))
                pe.wait_ge(scalar_done, eng.at("z2 out 17"))
                for g in range(2):
                    z2_unit(18 + g)
                done = [20]

                def filler(i):
                    if done[0] < 30:
                        z2_unit(done[0])
                        done[0] += 1

                attention(HEADS_TWO, lambda hd: (q2, k2, v2), tile2, turned2, filler)
                pe.wait_ge(vector_done, eng.at("heads a0 7"))
                y_parts = (("a", 0, 2), ("b", 2, 3), ("c", 5, 3))
                for i in range(4):
                    s = slot_of("y", i)
                    pe.wait_ge(weights_in[s], eng.arrived("y", i))
                    if i == 0:
                        pe.wait_ge(scalar_done, eng.at("z2 out 29"))
                    if i >= 2:
                        pe.wait_ge(vector_done, eng.at(f"merged {i - 2}"))
                    for br, (_, k0, nk) in enumerate(y_parts):
                        b = bank[:, 3 * (i % 2) + br].rearrange("p (c s) -> p c s", c=2)
                        for c in range(2):
                            for k in range(nk):
                                last = mm(b[:, c], ring[:, s, k0 + k, c * P:(c + 1) * P], o2[:, k0 + k, :],
                                          start=(k == 0), stop=(k == nk - 1))
                        if br == 1:
                            last.then_inc(tensor_done, eng.step(f"y {i}"))
                    last.then_inc(weights_free[s], 1)
                pe.wait_ge(vector_done, eng.at("merged 3"))
                for i in range(4):
                    plain_product("wo", (i,), merged, (bank[:, 2 * (i % 2), 0:S], bank[:, 2 * (i % 2) + 1, 0:S]),
                                  f"wo {i}", free=((vector_done, f"h wo {2 * i - 4}", 0),
                                                   (vector_done, f"h wo {2 * i - 3}", 0)) if i >= 2 else ())
                norm_sum("up")
                with eng.turns("up", 4) as t:
                    for i in range(4):
                        b = bank[:, i].rearrange("p (c s) -> p c s", c=2)
                        product("up", (i,), (b[:, 0], b[:, 1]), first=None if i else "up",
                                free=((relu_done, f"up relu {i}", 1),))
                pe.wait_ge(vector_done, eng.at("up squared 3"))
                pe.sem_inc(passed[0], 1)
                with eng.turns("dn", 2) as t:
                    for j in range(2):
                        plain_product("dn", tuple(range(4 * j, 4 * j + 4)), up2,
                                (bank[:, 2 * j, 0:S], bank[:, 2 * j + 1, 0:S]), f"dn out {j}", parts=DN_PARTS,
                                free=((vector_done, f"dn h {j} 0", 1), (vector_done, f"dn h {j} 1", 1)))

            norm_sum("final")
            for t in range(2):
                for k in range(KT):
                    pe.wait_ge(vector_done, eng.at(f"normed k final {k}"))
                    b = 2 * t + k // 4
                    turn(bank[:, b, (k % 4) * P:(k % 4 + 1) * P], result[:, k, t * P:(t + 1) * P],
                         f"result turned {t} {k // 4}" if k % 4 == 3 else None)
            eng._close()

        @block.scalar
        def _(act):
            eng = Engine(act, scalar_done, plan, old)
            f = act.activation
            act.sem_inc(silu_done, eng.step(None, silu_done, 2))
            act.sem_inc(relu_done, eng.step(None, relu_done, 4))

            def load(dst, src, s=params_in):
                act.dma_start(dst, src).then_inc(s, 16)
                if s is params_in:
                    n_params[0] += 1

            load(const[:, 0:2 * P], dram["constants"][:, 0:2 * P], tables_in)
            load(rows_c[0:KT], dram["c"].rearrange("o (k p) -> (o k) p", p=P), tables_in)
            act.wait_ge(tensor_done, eng.at("c turned"))
            f(cond[:], bank[:, 4, 0:KT], ACT.Silu).then_inc(scalar_done, eng.step("cond"))
            load(const[:, 2 * P:], dram["constants"][:, 2 * P:])
            for l in range(L):
                for r, name in ((R_ADA_B, "ada_b"), (R_CONV_B, "conv_b"), (R_CONV_G, "conv_norm_g"),
                                (R_CONV_NB, "conv_norm_b")):
                    src = dram[name][l].rearrange("(k p) -> k p", p=P)
                    load(rows[r:r + src.shape[0], l], src)
                load(rows[R_NORM_G:R_NORM_G + 24, l], dram["norm_g"][l].rearrange("a (k p) -> (a k) p", p=P))
                for r, src, n in ((R_DQ, dram["diff_qk_g"][l, 0:1], 4), (R_DK, dram["diff_qk_g"][l, 1:2], 4),
                                  (R_FQ, dram["fox_qk_g"][l, 0:1], 2), (R_FK, dram["fox_qk_g"][l, 1:2], 2),
                                  (R_DO, dram["diff_out_g"][l:l + 1], 2)):
                    w = P // n
                    load(rows[r:r + 1, l].rearrange("o (a b) -> o a b", a=n),
                         src.rearrange("o (a b) -> o a b", a=1).to_broadcast([1, n, w]))
                load(par_all[:, l, O_FB:O_FB + 4], dram["fox_fb"][l:l + 1].to_broadcast([P, 4]))
                load(rows_cw[0:62, l], dram["conv_w"][l].rearrange("j (t p) -> (j t) p", p=P))
                load(rows_ws[:, l], dram["gmlp_ws"][l].rearrange("h t s -> t h s"))
                bs = par_all[:, l, O_BS:O_BS + 256].rearrange("p (i t) -> p i t", i=2)
                for j in range(4):
                    load(bs[64 * (j % 2):64 * (j % 2) + 64, j // 2],
                         dram["gmlp_bs"][l, j:j + 1].to_broadcast([64, P]))
                for k, name in ((0, "gmlp_norm_g"), (1, "gmlp_norm_b")):
                    load(par_all[:, l, O_GG + k * 256:O_GG + (k + 1) * 256],
                         dram[name][l:l + 1].to_broadcast([P, 256]))
                load(par_all[:, l, O_LAM:O_LAM + 128],
                     dram["diff_lambda"][l:l + 1].rearrange("o a b -> o (a b)").to_broadcast([P, 128]))
                load(par_all[:, l, O_WF:O_WF + 32].rearrange("p (k h) -> p k h", k=KT),
                     dram["w_in"][l, :, FOX_F0:FOX_F0 + 4].rearrange("(k p) h -> p k h", p=P))
            load(rows_n2[0:16], dram["norm_mix_2"].rearrange("l (k p) -> (l k) p", p=P))
            load(rows_n2[16:32], dram["norm_mlp_2"].rearrange("l (k p) -> (l k) p", p=P))
            load(rows_n2[32:40], dram["norm_final_2"].rearrange("(k p) -> k p", p=P))

            ahead = [0]

            def round_chunk(phase, i):
                r, q, n = slot_of(phase, i), split_slot(phase, i), k_tiles(phase, i) // 2
                act.wait_ge(weights_in[r], eng.arrived(phase, i))
                for half in range(2):
                    act.wait_ge(weights_used, eng.split_chunk(phase, i) * 2 + half + 1)
                    f(w_hi[:, q, half * 4:half * 4 + n], ring[:, r, half * n:half * n + n], ACT.Copy).then_inc(weights_rounded, 1)

            def round_to(phase, n):
                for i in range(ahead[0], n + 1):
                    round_chunk(phase, i)
                ahead[0] = max(ahead[0], n + 1)


            def functions(name):
                act.preload_act_table_set(name)

            ln_exp = "natural_log_exp_and_others"

            def norm(n, shift=None):
                functions(ln_exp)
                act.wait_ge(tensor_done, eng.at(f"sum {n}"))
                f(rstd[:], bank[:, 4, 0:S], ACT.Ln, bias=eps, scale=1.0 / D).then_inc(scalar_done, eng.step())
                act.wait_ge(scalar_done, eng.at())
                f(rstd[:], rstd[:], ACT.Exp, scale=-0.5).then_inc(scalar_done, eng.step(f"rstd {n}"))
                if n == "final":
                    return
                for k in range(KT):
                    act.wait_ge(vector_done, eng.at(f"normed k {n} {k}"))
                    if shift is None:
                        i = f(hn[:, k, :], normed[:, k % 2], ACT.Copy)
                    else:
                        i = f(hn[:, k, :], normed[:, k % 2], ACT.Identity, bias=mod[:, shift + k:shift + k + 1])
                    i.then_inc(scalar_done, eng.step(f"hi {n} {k}"))

            def ffn(s):
                functions("silu_and_others")
                with eng.turns(s + "in", PAIRS // 2):
                    for j in range(2):
                        act.wait_ge(weights_used, eng.at(f"used {s}in {2 * j}"))
                        act.wait_ge(vector_done, eng.at(f"{s} gated {j}", 1))
                        f(act_tmp[:, j], bank[:, 2 * j], ACT.Silu).then_inc(silu_done, eng.step(f"{s} silu {j}", silu_done))
                        round_chunk(s + "in", 2 * j + 2)
                        round_chunk(s + "in", 2 * j + 3)
                act.wait_ge(weights_used, eng.at(f"used {s}in {2 * PAIRS - 2}"))
                act.wait_ge(vector_done, eng.at(f"{s} gated 0"))
                f(act_tmp[:, 0], bank[:, 0], ACT.Silu).then_inc(silu_done, eng.step(f"{s} silu last", silu_done))

            def squares(name, b, j, i):
                round_to("z", i + 1)
                act.wait_ge(weights_used, eng.at(f"used z {i}"))
                f(qs[:, j], bank[:, b], ACT.Square).then_inc(scalar_done, eng.step(f"{name} squares"))

            def group_rstd(name, b, j, width, after=None):
                act.wait_ge(tensor_done, eng.at(f"{name} sum"))
                if after:
                    act.wait_ge(vector_done, eng.at(after))
                f(rr[:, j], bank[:, b], ACT.Ln, bias=eps, scale=1.0 / width).then_inc(scalar_done, eng.step())
                act.wait_ge(scalar_done, eng.at())
                f(rr[:, j], rr[:, j], ACT.Exp, scale=-0.5).then_inc(scalar_done, eng.step(f"{name} rstd"))

            def exps(hd, tile):
                st = stat[:, hd.u % 4]
                if hd.kind == "stick":
                    t = tile[:, hd.tp[0][0]]
                    act.wait_ge(tensor_done, eng.at(f"scores {hd.name} 0"))
                    if hd.tp[0][1]:
                        act.wait_ge(done_by(hd.tp[0][1]), eng.at(hd.tp[0][1]))
                    f(t, bank[:, hd.sb[0][0], 0:SCW], ACT.Abs).then_inc(scalar_done, eng.step())
                    act.wait_ge(scalar_done, eng.at())
                    f(t, t, ACT.Exp, scale=-1.0).then_inc(scalar_done, eng.step())
                    act.wait_ge(scalar_done, eng.at())
                    f(t, t, ACT.Ln, bias=ones[:, 0:1]).then_inc(scalar_done, eng.step(f"ln {hd.name}"))
                    return
                act.wait_ge(vector_done, eng.at(f"neg {hd.name}"))
                scale = 32 ** -0.5 if hd.kind == "diff" else 1.0
                n = len(hd.maps)
                for m in range(n):
                    b = 6 + (2 * m if hd.kind == "diff" else 0)
                    for j, (c0, c1) in enumerate(((0, P), (P, SCW))):
                        t = tile[:, hd.tp[m][0], c0:c1]
                        f(t, t, ACT.Exp, bias=st[:, b + j:b + j + 1], scale=scale,
                          accum_out=st[:, 10 + 2 * m + j:11 + 2 * m + j]) \
                            .then_inc(scalar_done, eng.step(f"exp {hd.name}" if m == n - 1 and j else None))

            def copies(hd, tile, tt):
                if hd.kind == "stick":
                    act.wait_ge(vector_done, eng.at(f"argm {hd.name}"))
                    if hd.ps[0][1]:
                        act.wait_ge(tensor_done, eng.at(hd.ps[0][1]))
                    f(tt[:, hd.ps[0][0]], tile[:, hd.tp[0][0]], ACT.Exp) \
                        .then_inc(scalar_done, eng.step(f"copied {hd.name} 0"))
                    return
                for m in range(len(hd.pb)):
                    act.wait_ge(tensor_done, eng.at(f"turned {hd.name} {m}"))
                    if hd.ps[m][1]:
                        act.wait_ge(tensor_done, eng.at(hd.ps[m][1]))
                    f(tt[:, hd.ps[m][0]], bank[:, 4 + hd.pb[m][0], 0:SCW], ACT.Copy) \
                        .then_inc(scalar_done, eng.step(f"copied {hd.name} {m}"))

            def attention(heads, tile, tt, before, after):
                for i in range(len(heads) + STEPS_AFTER):
                    before(i)
                    if i < len(heads):
                        exps(heads[i], tile)
                    for j, hd in enumerate(heads):
                        if j + lag(heads, j) == i:
                            copies(hd, tile, tt)
                    after(i)

            with eng.layers("one"):
                ahead[0] = 0
                round_to("f1in", 1)
                norm("f1", 0)
                ffn("f1")
                ahead[0] = 0
                round_to("z", 1)
                norm("z", 24)
                round_to("z", 4)
                functions("sigmoid_and_others")
                act.wait_ge(weights_used, eng.at("used z 3"))
                f(cg[:], bank[:, 1].rearrange("p (c s) -> p c s", c=2), ACT.Sigmoid) \
                    .then_inc(scalar_done, eng.step("conv gate"))
                functions(ln_exp)
                squares("dq", 2, 0, 4)
                squares("dk", 3, 1, 5)
                group_rstd("dq", 5, 0, 32)
                round_to("z", 7)
                act.wait_ge(weights_used, eng.at("used z 6"))
                f(vd[:], bank[:, 0].rearrange("p (c s) -> p c s", c=2), ACT.Copy) \
                    .then_inc(scalar_done, eng.step("dv copied"))
                group_rstd("dk", 6, 1, 32)
                squares("fq", 1, 0, 7)
                squares("fk", 2, 1, 8)
                group_rstd("fq", 5, 0, 64, "dq scaled")
                round_to("z", 10)
                act.wait_ge(weights_used, eng.at("used z 9"))
                f(vf[:], bank[:, 3].rearrange("p (c s) -> p c s", c=2), ACT.Copy) \
                    .then_inc(scalar_done, eng.step("fv copied"))
                group_rstd("fk", 6, 1, 64, "dk scaled")
                act.wait_ge(vector_done, eng.at("lambda sums"))
                f(small[:, 2:4], small[:, 0:2], ACT.Exp).then_inc(scalar_done, eng.step("lambda exp"))
                act.wait_ge(tensor_done, eng.at("forget sum"))
                fbc = small[:, 8:9]
                f(ft[:, 0, :], bank[:, 4, 0:S], ACT.Abs, bias=fbc).then_inc(scalar_done, eng.step())
                act.wait_ge(scalar_done, eng.at())
                f(ft[:, 0, :], ft[:, 0, :], ACT.Exp, scale=-1.0).then_inc(scalar_done, eng.step())
                act.wait_ge(scalar_done, eng.at())
                f(ft[:, 0, :], ft[:, 0, :], ACT.Ln, bias=ones[:, 0:1]).then_inc(scalar_done, eng.step("forget ln"))
                round_to("z", 11)
                act.wait_ge(weights_used, eng.at("used z 10"))
                f(u_[:], bank[:, 0].rearrange("p (c s) -> p c s", c=2), ACT.Gelu_apprx_tanh) \
                    .then_inc(scalar_done, eng.step("u"))
                round_to("z", 11)
                act.wait_ge(weights_used, eng.at("used z 11"))
                f(vg[:], bank[:, 1].rearrange("p (c s) -> p c s", c=2), ACT.Gelu_apprx_tanh) \
                    .then_inc(scalar_done, eng.step("gate gelu"))
                functions(ln_exp)
                act.wait_ge(vector_done, eng.at("gate stats"))
                f(small[:, 20:22], small[:, 16:20].rearrange("p (c b) -> p c b", c=2)[:, :, 1], ACT.Ln, bias=eps) \
                    .then_inc(scalar_done, eng.step())
                act.wait_ge(scalar_done, eng.at())
                f(small[:, 20:22], small[:, 20:22], ACT.Exp, scale=-0.5) \
                    .then_inc(scalar_done, eng.step("gate rstd"))

                def between(i):
                    if i == 5:
                        act.wait_ge(vector_done, eng.at("conv centred"))
                        f(cg[:], cd[:], ACT.Square).then_inc(scalar_done, eng.step("conv squares"))
                    if i == 6:
                        act.wait_ge(tensor_done, eng.at("conv var"))
                        f(rstd[:], bank[:, 1, 0:S], ACT.Ln, bias=eps, scale=1.0 / 256) \
                            .then_inc(scalar_done, eng.step())
                        act.wait_ge(scalar_done, eng.at())
                        f(rstd[:], rstd[:], ACT.Exp, scale=-0.5).then_inc(scalar_done, eng.step("conv rstd"))
                    if i == 7:
                        act.wait_ge(vector_done, eng.at("heads d0 1"))
                        f(qs[:, 0], od[:].rearrange("p a s -> p (a s)"), ACT.Square) \
                            .then_inc(scalar_done, eng.step("od squares"))
                    if i == 8:
                        group_rstd("od", 0, 0, 64)
                        functions("silu_and_others")
                        act.wait_ge(vector_done, eng.at("conv normed"))
                        for j in range(2):
                            f(mix[:, 2 + j, :], cd[:, j, :], ACT.Silu,
                              bias=par[:, R_CONV_NB + j:R_CONV_NB + j + 1],
                              scale=par[:, R_CONV_G + j:R_CONV_G + j + 1]) \
                                .then_inc(scalar_done, eng.step("conv done" if j else None))

                attention(HEADS_ONE, tile1, turned1, lambda i: None, between)
                ahead[0] = 0
                round_to("f2in", 1)
                norm("f2", 48)
                ffn("f2")

            with eng.layers("two"):
                ahead[0] = 0
                round_to("z2", 1)
                norm("z2")
                for i in range(18):
                    chunks = Z2_UNITS[i][1]
                    round_to("z2", chunks[-1] + 1)
                    act.wait_ge(weights_used, eng.at(f"used z2 {chunks[-1]}"))
                    b = bank[:, i % 4]
                    if i in (5, 11):
                        if i == 5:
                            for a in range(2):
                                f(q2[:, 4 * i:4 * i + 4, :].rearrange("p (t a) s -> p t a s", a=2)[:, :, a],
                                  b.rearrange("p (t s) -> p t s", t=2), ACT.Identity,
                                  scale=tab("in64_eighth", 1, a)) \
                                    .then_inc(scalar_done, eng.step(f"z2 out {i}" if a else None))
                        else:
                            f(k2[:, 10:12, :], b.rearrange("p (t s) -> p t s", t=2), ACT.Copy) \
                                .then_inc(scalar_done, eng.step(f"z2 out {i}"))
                    elif i < 12:
                        j = i % 2
                        if i >= 2:
                            act.wait_ge(vector_done, eng.at(f"rotated {i - 2 if i not in (7,) else i - 3}"))
                            if i == 6:
                                act.wait_ge(vector_done, eng.at("rotated 4"))
                        f(raw[:, j], b, ACT.Copy).then_inc(scalar_done, eng.step(f"z2 out {i}"))
                    else:
                        c = 256 * (i - 12)
                        f(v2[:, :, c:c + 256], b.rearrange("p (t s) -> p t s", t=2), ACT.Copy) \
                            .then_inc(scalar_done, eng.step(f"z2 out {i}"))

                def gate_copy(i):
                    round_to("z2", min(Z2_UNITS[i][1][-1] + 1, TWO["z2"] - 1))
                    act.wait_ge(weights_used, eng.at(f"used z2 {Z2_UNITS[i][1][-1]}"))
                    c = 2 * (i - 18)
                    f(gates[:, c:c + 2, :], bank[:, i % 2].rearrange("p (t s) -> p t s", t=2), ACT.Copy) \
                        .then_inc(scalar_done, eng.step(f"z2 out {i}"))

                for g in range(2):
                    gate_copy(18 + g)
                done = [20]

                def filler(i):
                    if i and done[0] < 30:
                        gate_copy(done[0])
                        done[0] += 1

                attention(HEADS_TWO, tile2, turned2, filler, lambda i: None)
                functions("sigmoid_and_others")
                for i in range(4):
                    for br in range(3):
                        g = gates[:, 8 * br + 2 * i:8 * br + 2 * i + 2, :]
                        f(g, g, ACT.Sigmoid).then_inc(scalar_done, eng.step(f"gate {i}" if br == 2 else None))
                ahead[0] = 0
                round_to("up", 1)
                norm("up")

                def up_turn(last):
                    for i in range(4):
                        act.wait_ge(weights_used, eng.at(f"used up {i}"))
                        if i < 2:
                            act.wait_ge(vector_done, eng.at(f"up squared {i + 2}", 1))
                        else:
                            act.wait_ge(vector_done, eng.at(f"up squared {i - 2}"))
                        f(act_tmp[:, i % 2], bank[:, i], ACT.Relu) \
                            .then_inc(relu_done, eng.step(None if last else f"up relu {i}", relu_done))
                        if not last:
                            round_chunk("up", i + 2)
                        elif i < 2:
                            round_chunk("up", 14 + i)

                with eng.turns("up", 3):
                    up_turn(False)
                up_turn(True)
            norm("final")
            for t in range(2):
                for j in range(2):
                    act.wait_ge(tensor_done, eng.at(f"result turned {t} {j}"))
                    f(result_rows[:, t, 512 * j:512 * (j + 1)],
                      bank[:, 2 * t + j], ACT.Copy).then_inc(scalar_done, eng.step(f"result {t}" if j else None))
            eng._close()

        assert n_params[0] in (0, n_params_total), n_params

        @block.vector
        def _(dve):
            eng = Engine(dve, vector_done, plan, old)
            tt, ts, stt = dve.tensor_tensor, dve.tensor_scalar, dve.scalar_tensor_tensor

            def col(t, i):
                return t[:, i:i + 1]

            def ada_sum(j, n, half, n0=None):
                if n0 is None:
                    dve.wait_ge(first_ada_in[j], half * 16 + 16)
                else:
                    dve.wait_ge(ada_in[j], half * 16 + 16)
                if n0 is not None or n >= 2:
                    dve.wait_ge(ada_reduced, n - 1)
                ts(ada_acc[:, j], ada[:, j, 0], col(cond, 0), None, ALU.mult).then_inc(vector_done, eng.step())
                for k in range(1, KT - 1):
                    dve.wait_ge(vector_done, eng.at())
                    stt(ada_acc[:, j], ada[:, j, k], col(cond, k), ada_acc[:, j], ALU.mult, ALU.add) \
                        .then_inc(vector_done, eng.step())
                dve.wait_ge(vector_done, eng.at())
                stt(ada_acc[:, j], ada[:, j, KT - 1], col(cond, KT - 1), ada_acc[:, j], ALU.mult, ALU.add) \
                    .then_inc(ada_summed, 1)

            def add_square(hk, mark):
                dve.wait_ge(vector_done, eng.at())
                tt(normed[:, 0], hk, hk, ALU.mult).then_inc(vector_done, eng.step())
                dve.wait_ge(vector_done, eng.at())
                tt(square_sum[:], square_sum[:], normed[:, 0], ALU.add).then_inc(vector_done, eng.step(mark))

            for k in range(4):
                dve.wait_ge(tensor_done, eng.at(f"x turned {k}"))
                dve.tensor_copy(h[:, 2 * k:2 * k + 2, :].rearrange("p k s -> p (k s)"), bank[:, k]) \
                    .then_inc(vector_done, eng.step("x" if k == 3 else None))
            dve.memset(square_sum[:], 0.0).then_inc(vector_done, eng.step())
            for k in range(KT):
                add_square(h[:, k, :], None)
            dve.wait_ge(scalar_done, eng.at("cond"))
            for n in range(ADA_PRE):
                ada_sum(n % 2, n, n // 2)
            dve.wait_ge(tensor_done, eng.at("rows turned"))
            for l in range(L):
                dve.tensor_copy(par_all[:, l, 0:N_ROWS], bank[:, 5, l * P:l * P + N_ROWS])
                dve.tensor_copy(par_all[:, l, O_CW:O_CW + 62], bank[:, 5, 256 + l * 64:256 + l * 64 + 62])
                dve.memset(par_all[:, l, N_ROWS:O_CW], 0.0)
                dve.memset(par_all[:, l, O_CW + 62:O_WST], 0.0)
            dve.tensor_copy(norm2[:], bank[:, 5, 384:424]).then_inc(vector_done, eng.step("columns"))
            for l in range(L):
                dve.wait_ge(tensor_done, eng.at(f"ws turned {l}"))
                tt(par_all[:, l, O_WST:O_WST + 512].rearrange("p (h t) -> p h t", h=4),
                   bank[:, 6].rearrange("p (h t) -> p h t", h=4),
                   tab("mix_seen").rearrange("p (o t) -> p o t", o=1).to_broadcast([P, 4, P]), ALU.mult) \
                    .then_inc(vector_done, eng.step(f"mix weights {l}"))
            dve.wait_ge(vector_done, eng.at())

            def scale_norm(n, gains, shift=None):
                dve.wait_ge(vector_done, eng.at())
                dve.wait_ge(scalar_done, eng.at(f"rstd {n}"))
                for k in range(KT + 1):
                    if k < KT:
                        if k >= 2 and n != "final":
                            dve.wait_ge(vector_done, eng.at())
                        stt(result[:, k] if n == "final" else normed[:, k % 2], h[:, k, :], gains(k), rstd[:],
                            ALU.mult, ALU.mult) \
                            .then_inc(vector_done, eng.step(f"normed k {n} {k}"))
                    if k and n != "final":
                        dve.wait_ge(scalar_done, eng.at(f"hi {n} {k - 1}"))
                        if shift is None:
                            i = tt(hn_lo[:, k - 1, :], normed[:, (k - 1) % 2], hn[:, k - 1, :], ALU.subtract)
                        else:
                            i = stt(hn_lo[:, k - 1, :], normed[:, (k - 1) % 2], col(mod, shift + k - 1),
                                    hn[:, k - 1, :], ALU.add, ALU.subtract)
                        i.then_inc(vector_done, eng.step(f"split {n} {k - 1}"))
                dve.memset(square_sum[:], 0.0).then_inc(vector_done, eng.step())

            def gated_scale(dst, scale_at, gain_at):
                return stt(der[:, dst:dst + 8], mod[:, scale_at:scale_at + 8], 1.0,
                           par[:, gain_at:gain_at + 8], ALU.add, ALU.mult)

            def ffn(s, gate_at, n0, half0):
                with eng.turns(s + "in", PAIRS // 2) as t:
                    for j in range(2):
                        if s == "f1":
                            ada_sum(j, n0 + t * 2 + j, half0 + t, n0)
                        dve.wait_ge(silu_done, eng.at(f"{s} silu {j}"))
                        dve.wait_ge(weights_used, eng.at(f"used {s}in {2 * j + 1}"))
                        tt(gated[:, bass.ds(t * 4 + 2 * j, 2), :].rearrange("p c s -> p (c s)"),
                           act_tmp[:, j], bank[:, 2 * j + 1], ALU.mult) \
                            .then_inc(vector_done, eng.step(f"{s} gated {j}"))
                dve.wait_ge(silu_done, eng.at(f"{s} silu last"))
                dve.wait_ge(weights_used, eng.at(f"used {s}in {2 * PAIRS - 1}"))
                tt(gated[:, FT - 2:FT, :].rearrange("p c s -> p (c s)"), act_tmp[:, 0], bank[:, 1], ALU.mult) \
                    .then_inc(vector_done, eng.step(f"{s} gated last"))
                if s == "f1":
                    dve.wait_ge(ada_reduced, n0 + 10)
                    tt(mod[:, 16:56], bank[:, 7, 16:56], par[:, 16:56], ALU.add).then_inc(vector_done, eng.step())
                    dve.wait_ge(vector_done, eng.at())
                ts(der[:, 24:32], mod[:, gate_at:gate_at + 8], 0.5, None, ALU.mult) \
                    .then_inc(vector_done, eng.step())
                dve.wait_ge(vector_done, eng.at())
                dve.sem_inc(passed[1], 1)
                with eng.turns(s + "out", 2) as t:
                    for j in range(2):
                        if s == "f1":
                            ada_sum(j, n0 + t * 2 + 10 + j, half0 + t + PAIRS // 2, n0)
                        else:
                            ada_sum(j, n0 + t * 2 + ADA_REST + j, half0 + t + ADA_REST // 2, n0)
                        for c in range(2):
                            if c == 0:
                                dve.wait_ge(tensor_done, eng.at(f"{s} out {j}"))
                            else:
                                dve.wait_ge(weights_free[slot_of(s + "out", 4 * j + 3)], eng.freed(s + "out", 4 * j + 3))
                            k = t * 4 + 2 * j + c
                            hk = h[:, bass.ds(k, 1), :].rearrange("p o s -> p (o s)")
                            stt(hk, bank[:, 2 * j + c, 0:S], der[:, bass.ds(k + 24, 1)], hk,
                                ALU.mult, ALU.add).then_inc(vector_done, eng.step(f"{s} h {j} {c}"))
                            add_square(hk, f"{s} squares {j} {c}")

            def maxima(hd, tile):
                st = stat[:, hd.u % 4]
                if hd.kind == "stick":
                    t, sp_ = tile[:, hd.tp[0][0]], tile[:, hd.tp[1][0]]
                    if hd.tp[1][1]:
                        dve.wait_ge(tensor_done, eng.at(hd.tp[1][1]))
                    dve.wait_ge(scalar_done, eng.at(f"ln {hd.name}"))
                    stt(sp_, bank[:, hd.sb[0][0], 0:SCW], 0.0, t, ALU.max, ALU.add) \
                        .then_inc(vector_done, eng.step())
                    dve.wait_ge(vector_done, eng.at())
                    tt(sp_, sp_, tab("before", SCW), ALU.mult).then_inc(vector_done, eng.step(f"sp {hd.name}"))
                    return
                for m, (_, _, _, mask) in enumerate(hd.maps):
                    dve.wait_ge(tensor_done, eng.at(f"scores {hd.name} {m}"))
                    dve.sem_inc(passed[1], 1)
                    for j, (c0, c1) in enumerate(((0, P), (P, SCW))):
                        dve.tensor_tensor_reduce(
                            out=tile[:, hd.tp[m][0], c0:c1], in0=bank[:, hd.sb[m][0], c0:c1],
                            in1=tab(mask, c1 - c0, c0), scale=1.0, scalar=-3e38, op0=ALU.add, op1=ALU.max,
                            accum_out=st[:, 2 * m + j:2 * m + j + 1]) \
                            .then_inc(vector_done, eng.step(f"max {hd.name} {m}" if j else None))
                dve.wait_ge(vector_done, eng.at())
                if hd.kind == "diff":
                    i = ts(st[:, 6:10], st[:, 0:4], -(32 ** -0.5), None, ALU.mult)
                elif len(hd.maps) == 1:
                    i = ts(st[:, 6:8], st[:, 0:2], -1.0, None, ALU.mult)
                else:
                    i = dve.tensor_reduce(st[:, 6:8], st[:, 0:6].rearrange("p (m j) -> p j m", j=2), AX.X, ALU.max,
                                          negate=True)
                i.then_inc(vector_done, eng.step(f"neg {hd.name}"))

            def scaling(hd, tile):
                st = stat[:, hd.u % 4]
                if hd.kind == "stick":
                    dve.wait_ge(tensor_done, eng.at(f"arg {hd.name}"))
                    tt(tile[:, hd.tp[0][0]], bank[:, 4 + hd.pb[0][0], 0:SCW], tab("before_neg", SCW), ALU.add) \
                        .then_inc(vector_done, eng.step(f"argm {hd.name}"))
                    return
                dve.wait_ge(scalar_done, eng.at(f"exp {hd.name}"))
                n = len(hd.maps)
                if n == 3:
                    dve.tensor_reduce(st[:, 8:10], st[:, 10:16].rearrange("p (m j) -> p j m", j=2),
                                      AX.X, ALU.add).then_inc(vector_done, eng.step())
                    dve.wait_ge(vector_done, eng.at())
                r0, r1 = (8, 10) if n == 3 else (10, 14) if n == 2 else (10, 12)
                dve.reciprocal(st[:, r0:r1], st[:, r0:r1]).then_inc(vector_done, eng.step())
                dve.wait_ge(vector_done, eng.at())
                if hd.kind == "diff":
                    ts(st[:, 12:14], st[:, 12:14], small[:, 4:5], None, ALU.mult).then_inc(vector_done, eng.step())
                    dve.wait_ge(vector_done, eng.at())
                    for j, (c0, c1) in enumerate(((0, P), (P, SCW))):
                        a, b = (tile[:, hd.tp[m][0], c0:c1] for m in range(2))
                        ts(a, a, st[:, 10 + j:11 + j], None, ALU.mult).then_inc(vector_done, eng.step())
                        dve.wait_ge(vector_done, eng.at())
                        stt(a, b, st[:, 12 + j:13 + j], a, ALU.mult, ALU.add) \
                            .then_inc(vector_done, eng.step(f"scaled {hd.name}" if j else None))
                    return
                for m in range(n):
                    for j, (c0, c1) in enumerate(((0, P), (P, SCW))):
                        a = tile[:, hd.tp[m][0], c0:c1]
                        ts(a, a, st[:, r0 + j:r0 + j + 1], None, ALU.mult) \
                            .then_inc(vector_done, eng.step(f"scaled {hd.name}" if m == n - 1 and j else None))

            def pair_out(heads, i, dst):
                hd = heads[i]
                if hd.half == 0:
                    return
                dve.wait_ge(tensor_done, eng.at(f"out {hd.name}"))
                b = bank[:, 6 + hd.pair % 2].rearrange("p (a s) -> p a s", a=2)
                for a in range(2):
                    dve.tensor_copy(dst(hd)[64 * a:64 * a + 64], b[64 * a:64 * a + 64, a]) \
                        .then_inc(vector_done, eng.step(f"heads {heads[0].name} {hd.pair}" if a else None))
            tap = [0]

            def conv_taps(n):
                for j in range(tap[0], min(tap[0] + n, CONV_K)):
                    if j:
                        dve.wait_ge(vector_done, eng.at())
                    for i in range(2):
                        w = col(par, O_CW + 2 * j + i)
                        src = yp[:, i, j:j + S]
                        if j == 0:
                            ins = ts(cv[:, i, :], src, w, col(par, R_CONV_B + i), ALU.mult, ALU.add)
                        else:
                            ins = stt(cv[:, i, :], src, w, cv[:, i, :], ALU.mult, ALU.add)
                        ins.then_inc(vector_done, eng.step("conv out" if j == CONV_K - 1 and i else None))
                tap[0] += n

            def attention(heads, tile, dst, filler):
                for i in range(len(heads) + STEPS_AFTER):
                    if i < len(heads):
                        maxima(heads[i], tile)
                    for j, hd in enumerate(heads):
                        if j + (lag(heads, j) if hd.kind == "stick" else 1) == i:
                            scaling(hd, tile)
                    for j in range(len(heads)):
                        if j + lag(heads, j) + 1 == i:
                            pair_out(heads, j, dst)
                    filler(i)

            with eng.layers("one") as layer:
                n0 = layer * ADA_CHUNKS + ADA_PRE
                half0 = layer * (ADA_CHUNKS // 2)
                dve.wait_ge(vector_done, eng.at())
                dve.tensor_copy(small[:, 6:8], const[:, bass.ds(layer * 2 + at["lam_init"], 2)]) \
                    .then_inc(vector_done, eng.step("layer params"))
                dve.wait_ge(ada_reduced, n0)
                tt(mod[:, 0:16], bank[:, 7, 0:16], par[:, 0:16], ALU.add).then_inc(vector_done, eng.step())
                dve.wait_ge(vector_done, eng.at())
                gated_scale(0, 8, R_NORM_G).then_inc(vector_done, eng.step())
                scale_norm("f1", lambda k: col(der, k), 0)
                ffn("f1", 16, n0, half0)
                plan.marks["h z"] = plan.marks["f1 squares 1 1"]
                dve.wait_ge(ada_reduced, n0 + ADA_REST)
                dve.wait_ge(vector_done, eng.at())
                tt(mod[:, 56:72], bank[:, 7, 56:72], par[:, 56:72], ALU.add).then_inc(vector_done, eng.step())
                dve.wait_ge(vector_done, eng.at())
                gated_scale(8, 32, R_NORM_G + 8).then_inc(vector_done, eng.step())
                gated_scale(16, 56, R_NORM_G + 16).then_inc(vector_done, eng.step())
                ts(der[:, 32:36], tab("in32", 4), col(par, R_DQ), None, ALU.mult).then_inc(vector_done, eng.step())
                ts(der[:, 36:38], tab("in64_eighth", 2), col(par, R_FQ), None, ALU.mult) \
                    .then_inc(vector_done, eng.step())
                ts(der[:, 38:39], col(par, R_DO), small[:, 7:8], None, ALU.mult).then_inc(vector_done, eng.step())
                tt(small[:, 40:44], tab("in32", 4), par[:, O_FB:O_FB + 4], ALU.mult) \
                    .then_inc(vector_done, eng.step())
                dve.wait_ge(vector_done, eng.at())
                dve.tensor_reduce(small[:, 8:9], small[:, 40:44], AX.X, ALU.add).then_inc(vector_done, eng.step())
                lam = par[:, O_LAM:O_LAM + 128].rearrange("p (a b c) -> p a b c", a=2, b=2)
                tt(ft[:, 2, 0:64].rearrange("p (a c) -> p a c", a=2), lam[:, :, 0], lam[:, :, 1], ALU.mult) \
                    .then_inc(vector_done, eng.step())
                dve.wait_ge(vector_done, eng.at())
                dve.tensor_reduce(small[:, 0:2], ft[:, 2, 0:64].rearrange("p (a c) -> p a c", a=2), AX.X, ALU.add) \
                    .then_inc(vector_done, eng.step("lambda sums"))
                scale_norm("z", lambda k: col(der, 8 + k), 24)
                dve.tensor_copy(
                    wfx.rearrange("p k (h r) -> p (k h) r", h=4),
                    par[:, O_WF:O_WF + 32].rearrange("p (k o) -> p k o", o=1).to_broadcast([P, 32, 32])) \
                    .then_inc(vector_done, eng.step("forget weights"))
                dve.memset(yp[:, :, 0:CONV_K - 1], 0.0).then_inc(vector_done, eng.step())

                def scale_q(name, b, j, dst, gain, maps):
                    dve.wait_ge(scalar_done, eng.at(f"{name} rstd"))
                    for i in range(2):
                        for m in range(maps):
                            stt(dst[:, maps * i + m, :], bank[:, b, i * S:(i + 1) * S], gain(m),
                                rr[:, j, i * S:(i + 1) * S], ALU.mult, ALU.mult) \
                                .then_inc(vector_done, eng.step(f"{name} scaled" if i and m == maps - 1 else None))

                dve.wait_ge(scalar_done, eng.at("conv gate"))
                dve.wait_ge(weights_used, eng.at("used z 1"))
                tt(yp[:, :, CONV_K - 1:CONV_K - 1 + S], bank[:, 0].rearrange("p (c s) -> p c s", c=2), cg[:],
                   ALU.mult).then_inc(vector_done, eng.step("conv in"))
                dve.wait_ge(vector_done, eng.at())
                tap[0] = 0
                conv_taps(10)
                scale_q("dq", 2, 0, qd, lambda m: col(der, 32 + m), 4)
                conv_taps(3)
                scale_q("dk", 3, 1, kd, lambda m: col(par, R_DK), 1)
                conv_taps(7)
                scale_q("fq", 1, 0, qf, lambda m: col(der, 36 + m), 2)
                conv_taps(3)
                scale_q("fk", 2, 1, kf, lambda m: col(par, R_FK), 1)
                conv_taps(8)
                dve.wait_ge(scalar_done, eng.at("lambda exp"))
                tt(small[:, 4:5], small[:, 3:4], small[:, 2:3], ALU.subtract).then_inc(vector_done, eng.step())
                dve.wait_ge(vector_done, eng.at())
                tt(small[:, 4:5], small[:, 4:5], small[:, 6:7], ALU.subtract).then_inc(vector_done, eng.step())
                dve.wait_ge(vector_done, eng.at())
                dve.wait_ge(scalar_done, eng.at("forget ln"))
                ts(ft[:, 1, :], bank[:, 4, 0:S], col(small, 8), 0.0, ALU.add, ALU.min) \
                    .then_inc(vector_done, eng.step())
                dve.wait_ge(vector_done, eng.at())
                tt(ft[:, 1, :], ft[:, 1, :], ft[:, 0, :], ALU.subtract).then_inc(vector_done, eng.step())
                dve.wait_ge(vector_done, eng.at())
                dve.tensor_tensor_scan(ft[:, 2, :], ones[:, 0:1].to_broadcast([P, S]), ft[:, 1, :], 0.0,
                                         ALU.mult, ALU.add).then_inc(vector_done, eng.step())
                dve.wait_ge(vector_done, eng.at())
                for m in range(4):
                    ts(fa[:, m, :], ft[:, 2, :], tab("cum_row", 1, m), tab("one_row", 1, m), ALU.mult, ALU.add) \
                        .then_inc(vector_done, eng.step())
                ts(fb[:], ft[:, 2, :], tab("neg_cum_rows", 1), tab("one_rows", 1), ALU.mult, ALU.add) \
                    .then_inc(vector_done, eng.step("forget rows"))
                dve.wait_ge(scalar_done, eng.at("gate gelu"))
                for c in range(2):
                    dve.bn_stats(small[:, 24 + 6 * c:30 + 6 * c], vg[:, c, :]).then_inc(vector_done, eng.step())
                dve.wait_ge(vector_done, eng.at())
                dve.sem_inc(passed[1], 1)
                for c in range(2):
                    dve.bn_aggr(small[:, 16 + 2 * c:18 + 2 * c], small[:, 24 + 6 * c:30 + 6 * c]) \
                        .then_inc(vector_done, eng.step("gate stats" if c else None))
                dve.wait_ge(scalar_done, eng.at("gate rstd"))
                for c in range(2):
                    ts(vg[:, c, :], vg[:, c, :], small[:, 16 + 2 * c:17 + 2 * c], small[:, 20 + c:21 + c],
                       ALU.subtract, ALU.mult).then_inc(vector_done, eng.step())
                dve.wait_ge(vector_done, eng.at())
                gain = par[:, O_GG:O_GG + 512].rearrange("p (k s) -> p k s", k=2)
                for k, op in ((0, ALU.mult), (1, ALU.add)):
                    i = tt(vg[:], vg[:], gain[:, k:k + 1].to_broadcast([P, 2, 256]), op)
                    i.then_inc(vector_done, eng.step("gate normed" if k else None))
                    if not k:
                        dve.wait_ge(vector_done, eng.at())
                for j in range(4):
                    dve.wait_ge(tensor_done, eng.at(f"mixed {j // 2}"))
                    r = slice(64 * (j % 2), 64 * (j % 2) + 64)
                    dst = mix[r, 4 + j // 2, :].rearrange("p (c t) -> p c t", c=2)
                    b = bank[:, j // 2].rearrange("p (a c s) -> p a c s", a=2, c=2)[r, j % 2]
                    bias = par[r, O_BS + (j // 2) * P:O_BS + (j // 2 + 1) * P].rearrange("p (o t) -> p o t", o=1)
                    tt(dst, b, bias.to_broadcast([64, 2, P]), ALU.add).then_inc(vector_done, eng.step())
                    dve.wait_ge(vector_done, eng.at())
                    tt(dst, dst, u_[r, j // 2, :].rearrange("p (c t) -> p c t", c=2), ALU.mult) \
                        .then_inc(vector_done, eng.step("mixed out" if j == 3 else None))

                def between(i):
                    if i == 5:
                        dve.wait_ge(tensor_done, eng.at("conv mean"))
                        for j in range(2):
                            stt(cd[:, j, :], bank[:, 0, 0:S], -1.0 / 256, cv[:, j, :], ALU.mult, ALU.add) \
                                .then_inc(vector_done, eng.step("conv centred" if j else None))
                    if i == 7:
                        dve.wait_ge(scalar_done, eng.at("conv rstd"))
                        for j in range(2):
                            tt(cd[:, j, :], cd[:, j, :], rstd[:], ALU.mult) \
                                .then_inc(vector_done, eng.step("conv normed" if j else None))
                    if i == 9:
                        dve.wait_ge(scalar_done, eng.at("od rstd"))
                        for j in range(2):
                            stt(mix[:, j, :], od[:, j, :], col(der, 38), rr[:, 0, j * S:(j + 1) * S],
                                ALU.mult, ALU.mult).then_inc(vector_done, eng.step("od normed" if j else None))

                attention(HEADS_ONE, tile1,
                          lambda hd: od[:, hd.out_tile, :] if hd.kind == "diff" else mix[:, 6 + hd.out_tile, :],
                          between)
                for i in range(4):
                    for c in range(2):
                        k = 2 * i + c
                        if c == 0:
                            dve.wait_ge(tensor_done, eng.at(f"o {i}"))
                        else:
                            dve.wait_ge(weights_free[slot_of("o", i)], eng.freed("o", i))
                        stt(h[:, k, :], bank[:, 2 * (i % 2) + c, 0:S], col(mod, 40 + k), h[:, k, :],
                            ALU.mult, ALU.add).then_inc(vector_done, eng.step(f"h o {k}"))
                        add_square(h[:, k, :], "h f2" if k == KT - 1 else None)
                dve.wait_ge(vector_done, eng.at())
                scale_norm("f2", lambda k: col(der, 16 + k), 48)
                dve.tensor_copy(par, par_all[:, L - 1]).then_inc(vector_done, eng.step())
                ffn("f2", 64, n0, half0)

            with eng.layers("two") as layer:
                dve.wait_ge(vector_done, eng.at())
                dve.tensor_copy(der[:, 0:8], norm2[:, bass.ds(layer * 8, 8)])
                dve.tensor_copy(der[:, 8:16], norm2[:, bass.ds(layer * 8 + 16, 8)]) \
                    .then_inc(vector_done, eng.step("h z2"))
                dve.wait_ge(vector_done, eng.at())
                scale_norm("z2", lambda k: col(der, k))
                cosb = tab("cos", S).rearrange("p (o s) -> p o s", o=1).to_broadcast([P, 2, S])
                sinb = tab("sin", S).rearrange("p (o s) -> p o s", o=1).to_broadcast([P, 2, S])
                for i in [x for x in range(12) if x not in (5, 11)]:
                    dve.wait_ge(tensor_done, eng.at(f"rotary {i}"))
                    a = rot_tmp[:, 0].rearrange("p (c s) -> p c s", c=2)
                    b = rot_tmp[:, 1].rearrange("p (c s) -> p c s", c=2)
                    src = raw[:, i % 2].rearrange("p (c s) -> p c s", c=2)
                    rot = bank[:, 5 + i % 2].rearrange("p (c s) -> p c s", c=2)
                    half = i % 6 == 4
                    n = 1 if half else 2
                    tt(a[:, 0:n], rot[:, 0:n], sinb[:, 0:n], ALU.mult).then_inc(vector_done, eng.step())
                    tt(b[:, 0:n], src[:, 0:n], cosb[:, 0:n], ALU.mult).then_inc(vector_done, eng.step())
                    dve.wait_ge(vector_done, eng.at())
                    if i < 6:
                        tt(a[:, 0:n], a[:, 0:n], b[:, 0:n], ALU.add).then_inc(vector_done, eng.step())
                        if half:
                            dve.tensor_copy(a[:, 1], src[:, 1]).then_inc(vector_done, eng.step())
                        dve.wait_ge(vector_done, eng.at())
                        dst = q2[:, 4 * i:4 * i + 4, :].rearrange("p (t a) s -> p t a s", a=2)
                        for m in range(2):
                            ts(dst[:, :, m], a, tab("in64_eighth", 1, m), None, ALU.mult) \
                                .then_inc(vector_done, eng.step(f"rotated {i}" if m else None))
                    else:
                        k0 = 2 * (i - 6)
                        if half:
                            dve.tensor_copy(k2[:, k0 + 1, :], src[:, 1]).then_inc(vector_done, eng.step())
                        tt(k2[:, k0:k0 + n, :], a[:, 0:n], b[:, 0:n], ALU.add) \
                            .then_inc(vector_done, eng.step(f"rotated {i}"))
                    dve.wait_ge(vector_done, eng.at())
                attention(HEADS_TWO, tile2, lambda hd: o2[:, hd.out_tile, :], lambda i: None)
                for i in range(4):
                    dve.wait_ge(tensor_done, eng.at(f"y {i}"))
                    dve.wait_ge(scalar_done, eng.at(f"gate {i}"))
                    dst = merged[:, 2 * i:2 * i + 2, :]
                    t = act_tmp[:, 0].rearrange("p (c s) -> p c s", c=2)
                    for br in range(3):
                        if br == 2:
                            dve.wait_ge(weights_free[slot_of("y", i)], eng.freed("y", i))
                        b = bank[:, 3 * (i % 2) + br].rearrange("p (c s) -> p c s", c=2)
                        g = gates[:, 8 * br + 2 * i:8 * br + 2 * i + 2, :]
                        tt(t if br else dst, b, g, ALU.mult).then_inc(vector_done, eng.step())
                        dve.wait_ge(vector_done, eng.at())
                        if br:
                            tt(dst, dst, t, ALU.add) \
                                .then_inc(vector_done, eng.step(f"merged {i}" if br == 2 else None))
                            dve.wait_ge(vector_done, eng.at())
                for i in range(4):
                    for c in range(2):
                        k = 2 * i + c
                        if c == 0:
                            dve.wait_ge(tensor_done, eng.at(f"wo {i}"))
                        else:
                            dve.wait_ge(weights_free[slot_of("wo", i)], eng.freed("wo", i))
                        tt(h[:, k, :], bank[:, 2 * (i % 2) + c, 0:S], h[:, k, :], ALU.add) \
                            .then_inc(vector_done, eng.step(f"h wo {k}"))
                        add_square(h[:, k, :], "h up" if k == KT - 1 else None)
                dve.wait_ge(vector_done, eng.at())
                scale_norm("up", lambda k: col(der, 8 + k))
                with eng.turns("up", 4) as t:
                    for i in range(4):
                        dve.wait_ge(relu_done, eng.at(f"up relu {i}"))
                        tt(up2[:, bass.ds(t * 8 + 2 * i, 2), :].rearrange("p c s -> p (c s)"),
                           act_tmp[:, i % 2], act_tmp[:, i % 2], ALU.mult) \
                            .then_inc(vector_done, eng.step(f"up squared {i}"))
                with eng.turns("dn", 2) as t:
                    for j in range(2):
                        for c in range(2):
                            if c == 0:
                                dve.wait_ge(tensor_done, eng.at(f"dn out {j}"))
                            else:
                                dve.wait_ge(weights_free[slot_of("dn", 4 * j + 3)], eng.freed("dn", 4 * j + 3))
                            hk = h[:, bass.ds(t * 4 + 2 * j + c, 1), :].rearrange("p o s -> p (o s)")
                            tt(hk, bank[:, 2 * j + c, 0:S], hk, ALU.add) \
                                .then_inc(vector_done, eng.step(f"dn h {j} {c}"))
                            add_square(hk, f"dn squares {j} {c}")
            plan.marks["h final"] = plan.marks["dn squares 1 1"]
            dve.wait_ge(vector_done, eng.at())
            scale_norm("final", lambda k: col(norm2, 32 + k))
            eng._close()
    return plan


def kernel(**inputs):
    import concourse.bacc as bacc
    from concourse.bass_utils import run_bass_kernel_spmd

    table, at = constant_tables()
    arrays = {name: np.ascontiguousarray(inputs[name]) for name in IN_NAMES}
    arrays["constants"] = table

    def program(old):
        nc = bacc.Bacc("TRN2", target_bir_lowering=False, num_devices=1)
        dram = {n: nc.dram_tensor(f"in_{n}", a.shape, mybir.dt.from_np(a.dtype), kind="ExternalInput").ap()
                for n, a in arrays.items()}
        out = nc.dram_tensor("out_0", (1, S, D), F32, kind="ExternalOutput").ap()
        return nc, build(nc, dram, out, at, old)

    _, counted = program(Plan())
    nc, _ = program(counted)
    r = run_bass_kernel_spmd(nc, [{f"in_{n}": a for n, a in arrays.items()}], core_ids=[0])
    return r.results[0]["out_0"]
```
